# Optimizing a Trainium2 kernel written in Bass

```python
import math
import jax, jax.numpy as jnp
from jax import lax
import numpy as np
import math, functools

D_MODEL = 1024
BATCH = 1
SEQ = 256
DEPTH = 2

CTX_LEN = 256
GRID_W = 64
POOL_WIDTH = 512
POOL_WINDOWS = (2, 4, 8, 16)
POOL_GROUPS = len(POOL_WINDOWS)
POOL_GC = POOL_WIDTH // POOL_GROUPS
N_HEADS = 4
HEAD_DIM = 64
V_DIM = 2 * HEAD_DIM
QK_WIDTH = N_HEADS * 2 * HEAD_DIM
ATTN_WIDTH = N_HEADS * V_DIM
MIX_WIDTH = POOL_WIDTH + ATTN_WIDTH
IN_WIDTH = POOL_WIDTH + 2 * QK_WIDTH + ATTN_WIDTH
ROT_AXIS = HEAD_DIM // 2
ROPE_BASE = 10000.0
D_FF = 4 * D_MODEL
Q_BLOCK = 128
N_ADA = 6
EPS = 1e-6


def rms_norm(x, g):
    xf = x.astype(jnp.float32)
    y = xf * lax.rsqrt(jnp.mean(xf * xf, axis=-1, keepdims=True) + EPS)
    return (y * g.astype(jnp.float32)).astype(x.dtype)

def modulate(h, shift, scale):
    return h * (1 + scale) + shift

def ada_params(cvec, w_ada, b_ada):
    return jnp.split(jax.nn.silu(cvec) @ w_ada + b_ada, N_ADA, axis=-1)

def axial_rope(n, dtype):
    rows = n // GRID_W
    row = jnp.repeat(jnp.arange(rows), GRID_W).astype(jnp.float32)
    col = jnp.tile(jnp.arange(GRID_W), rows).astype(jnp.float32)
    inv = ROPE_BASE ** (-jnp.arange(0, ROT_AXIS, 2, dtype=jnp.float32) / ROT_AXIS)
    ang = jnp.concatenate([row[:, None] * inv, col[:, None] * inv], axis=-1)
    return jnp.cos(ang).astype(dtype), jnp.sin(ang).astype(dtype)

def apply_rope(x, cos, sin):
    x1, x2 = x[..., :HEAD_DIM // 2], x[..., HEAD_DIM // 2:]
    return jnp.concatenate([x1 * cos - x2 * sin, x1 * sin + x2 * cos], axis=-1)

def centred_mean(x, w):
    b, n, ch = x.shape
    xf = x.astype(jnp.float32)
    cs = jnp.concatenate([jnp.zeros((b, 1, ch), jnp.float32), jnp.cumsum(xf, axis=1)], axis=1)
    t = jnp.arange(n)
    lo = jnp.clip(t - w // 2, 0, n)
    hi = jnp.clip(t + w - w // 2, 0, n)
    s = cs[:, hi] - cs[:, lo]
    cnt = (hi - lo).astype(jnp.float32)
    return (s / cnt[None, :, None]).astype(x.dtype)

def pool_mixer(u, w_pool, s_pool):
    b, n, _ = u.shape
    groups = jnp.split(u, POOL_GROUPS, axis=-1)
    y = jnp.stack([centred_mean(g, w) - g for g, w in zip(groups, POOL_WINDOWS)], axis=2)
    y = jnp.einsum('bngc,gcd->bngd', y, w_pool).reshape(b, n, POOL_WIDTH)
    return y * s_pool

def split_heads(z):
    b, n, _ = z.shape
    u, q, k, v = jnp.split(z, [POOL_WIDTH, POOL_WIDTH + QK_WIDTH, POOL_WIDTH + 2 * QK_WIDTH], axis=-1)
    q = q.reshape(b, n, 2 * N_HEADS, HEAD_DIM).transpose(0, 2, 1, 3)
    k = k.reshape(b, n, 2 * N_HEADS, HEAD_DIM).transpose(0, 2, 1, 3)
    v = v.reshape(b, n, N_HEADS, V_DIM).transpose(0, 2, 1, 3)
    return u, q, k, v

def diff_attn(q, k, v, lam):
    b, _, nq, _ = q.shape
    nk = k.shape[2]
    s = jnp.einsum('bhqd,bhkd->bhqk', q, k).astype(jnp.float32) * (HEAD_DIM ** -0.5)
    a = jax.nn.softmax(s, axis=-1).reshape(b, N_HEADS, 2, nq, nk)
    w = a[:, :, 0] - lam * a[:, :, 1]
    return jnp.einsum('bhqk,bhkd->bhqd', w.astype(v.dtype), v)

def diff_attn_blocks(q, k, v, lam):
    b, hh, n, d = q.shape
    nb = n // Q_BLOCK
    qb = q.reshape(b, hh, nb, Q_BLOCK, d).transpose(2, 0, 1, 3, 4)
    o = lax.map(lambda qblk: diff_attn(qblk, k, v, lam), qb)
    return o.transpose(1, 2, 0, 3, 4).reshape(b, N_HEADS, n, V_DIM)

def head_out(o, g_sub, lam_init):
    o = rms_norm(o, g_sub) * (1.0 - lam_init)
    b, h, n, d = o.shape
    return o.transpose(0, 2, 1, 3).reshape(b, n, h * d)

def sq_relu_mlp(h, w1, w2):
    return jnp.square(jax.nn.relu(h @ w1)) @ w2

def first_inputs(seed: int = 0) -> dict:
    key = jax.random.key(seed)
    ks = jax.random.split(key, 24)
    f = jnp.float32
    nrm = lambda k, shape, s: jax.random.normal(k, shape, f) * s
    L = DEPTH
    return {
        "x": nrm(ks[0], (BATCH, SEQ, D_MODEL), 1.0),
        "c": nrm(ks[1], (BATCH, D_MODEL), 1.0),
        "ctx": nrm(ks[2], (BATCH, CTX_LEN, D_MODEL), 1.0),
        "c_ctx": nrm(ks[3], (D_MODEL,), 1.0),
        "w_ada": nrm(ks[4], (L, D_MODEL, N_ADA * D_MODEL), 0.02),
        "b_ada": nrm(ks[5], (L, N_ADA * D_MODEL), 0.01),
        "g_mix": 1.0 + nrm(ks[6], (L, D_MODEL), 0.02),
        "g_mlp": 1.0 + nrm(ks[7], (L, D_MODEL), 0.02),
        "w_in": nrm(ks[8], (L, D_MODEL, IN_WIDTH), D_MODEL ** -0.5),
        "w_pool": nrm(ks[9], (L, POOL_GROUPS, POOL_GC, POOL_GC), POOL_GC ** -0.5),
        "s_pool": 1.0 + nrm(ks[10], (L, POOL_WIDTH), 0.1),
        "lam_q1": nrm(ks[11], (L, HEAD_DIM), 0.1),
        "lam_k1": nrm(ks[12], (L, HEAD_DIM), 0.1),
        "lam_q2": nrm(ks[13], (L, HEAD_DIM), 0.1),
        "lam_k2": nrm(ks[14], (L, HEAD_DIM), 0.1),
        "g_subln": 1.0 + nrm(ks[15], (L, V_DIM), 0.02),
        "w_out": nrm(ks[16], (L, MIX_WIDTH, D_MODEL), MIX_WIDTH ** -0.5),
        "w_mlp1": nrm(ks[17], (L, D_MODEL, D_FF), D_MODEL ** -0.5),
        "w_mlp2": nrm(ks[18], (L, D_FF, D_MODEL), D_FF ** -0.5),
        "g_final": 1.0 + nrm(ks[19], (D_MODEL,), 0.02),
    }

def first_block(x, c, ctx, c_ctx, w_ada, b_ada, g_mix, g_mlp, w_in, w_pool, s_pool,
              lam_q1, lam_k1, lam_q2, lam_k2, g_subln, w_out, w_mlp1, w_mlp2, g_final):
    n = x.shape[1]
    cos, sin = axial_rope(n, x.dtype)
    c_lat = c[:, None, :]
    c_cx = c_ctx[None, None, :]
    for l in range(DEPTH):
        last = l == DEPTH - 1
        sa, ca, ga, sm, cm, gm = ada_params(c_lat, w_ada[l], b_ada[l])
        sa_c, ca_c, ga_c, sm_c, cm_c, gm_c = ada_params(c_cx, w_ada[l], b_ada[l])
        lam_init = 0.8 - 0.6 * math.exp(-0.3 * l)
        lam = (jnp.exp(jnp.sum(lam_q1[l].astype(jnp.float32) * lam_k1[l].astype(jnp.float32)))
               - jnp.exp(jnp.sum(lam_q2[l].astype(jnp.float32) * lam_k2[l].astype(jnp.float32)))
               + lam_init)

        h = modulate(rms_norm(x, g_mix[l]), sa, ca)
        hc = modulate(rms_norm(ctx, g_mix[l]), sa_c, ca_c)
        u, q, k, v = split_heads(h @ w_in[l])
        uc, qc, kc, vc = split_heads(hc @ w_in[l])
        q = apply_rope(q, cos, sin)
        k = apply_rope(k, cos, sin)
        k_all = jnp.concatenate([kc, k], axis=2)
        v_all = jnp.concatenate([vc, v], axis=2)
        o_att = diff_attn_blocks(q, k_all, v_all, lam)
        mix = jnp.concatenate([pool_mixer(u, w_pool[l], s_pool[l]),
                               head_out(o_att, g_subln[l], lam_init)], axis=-1)
        x = x + ga * (mix @ w_out[l])

        x = x + gm * sq_relu_mlp(modulate(rms_norm(x, g_mlp[l]), sm, cm), w_mlp1[l], w_mlp2[l])

        if not last:
            o_c = diff_attn(qc, kc, vc, lam)
            mix_c = jnp.concatenate([pool_mixer(uc, w_pool[l], s_pool[l]),
                                     head_out(o_c, g_subln[l], lam_init)], axis=-1)
            ctx = ctx + ga_c * (mix_c @ w_out[l])
            ctx = ctx + gm_c * sq_relu_mlp(modulate(rms_norm(ctx, g_mlp[l]), sm_c, cm_c),
                                           w_mlp1[l], w_mlp2[l])
    return rms_norm(x, g_final)


N_EVEN = (DEPTH + 1) // 2
N_ODD = DEPTH // 2

A_HEADS = 8
A_HEAD_DIM = 64
A_WIDTH = A_HEADS * A_HEAD_DIM
MOBA_BLOCK = 256
MOBA_TOPK = 3
Q_CHUNK = 64
ROPE_THETA = 10000.0

B_HEADS = 8
B_HEAD_K = 32
B_HEAD_V = 64
B_KEY_WIDTH = B_HEADS * B_HEAD_K
B_VAL_WIDTH = B_HEADS * B_HEAD_V
GLA_GATE_RANK = 16
GLA_GATE_NORM = 16.0
GLA_CHUNK = 64

MIX_WIDTH_2 = A_WIDTH + B_VAL_WIDTH
EVEN_PROJ = 3 * A_WIDTH + 2 * B_KEY_WIDTH + B_VAL_WIDTH + GLA_GATE_RANK + B_VAL_WIDTH
EVEN_SPLITS = (
    A_WIDTH,
    2 * A_WIDTH,
    3 * A_WIDTH,
    3 * A_WIDTH + B_KEY_WIDTH,
    3 * A_WIDTH + 2 * B_KEY_WIDTH,
    3 * A_WIDTH + 2 * B_KEY_WIDTH + B_VAL_WIDTH,
    3 * A_WIDTH + 2 * B_KEY_WIDTH + B_VAL_WIDTH + GLA_GATE_RANK,
)

D_RNN = D_MODEL
RG_BLOCKS = 4
RG_BLOCK_W = D_RNN // RG_BLOCKS
RG_CONV = 4
LRU_C = 8.0

D_FF_2 = 3 * D_MODEL
FFN_CONV = 3

NORM_EPS = 1e-6
NEG_INF = -1e30


def rms_norm_2(x, g):
    xf = x.astype(jnp.float32)
    y = xf * lax.rsqrt(jnp.mean(xf * xf, axis=-1, keepdims=True) + NORM_EPS)
    return (y * g.astype(jnp.float32)).astype(x.dtype)

def causal_dwconv(x, w, b):
    width = w.shape[0]
    seq = x.shape[1]
    xp = jnp.pad(x, ((0, 0), (width - 1, 0), (0, 0)))
    y = b
    for i in range(width):
        y = y + xp[:, i:i + seq] * w[i]
    return y

def rotary(x, pos):
    hd = x.shape[-1]
    half = hd // 2
    inv = ROPE_THETA ** (-jnp.arange(half, dtype=jnp.float32) / half)
    ang = pos.astype(jnp.float32)[:, None] * inv[None, :]
    cos, sin = jnp.cos(ang), jnp.sin(ang)
    xf = x.astype(jnp.float32)
    x1, x2 = xf[..., :half], xf[..., half:]
    return jnp.concatenate([x1 * cos - x2 * sin, x2 * cos + x1 * sin], axis=-1).astype(x.dtype)

def moba_attention(q, k, v):
    bsz, nh, seq, hd = q.shape
    nb = -(-seq // MOBA_BLOCK)
    s_pad = nb * MOBA_BLOCK
    pad = ((0, 0), (0, 0), (0, s_pad - seq), (0, 0))
    kp = jnp.pad(k, pad)
    vp = jnp.pad(v, pad)
    kb = kp.reshape(bsz, nh, nb, MOBA_BLOCK, hd)
    vb = vp.reshape(bsz, nh, nb, MOBA_BLOCK, hd)
    kmean = jnp.mean(kb.astype(jnp.float32), axis=3)
    n_sel = min(MOBA_TOPK, nb)
    scale = hd ** -0.5
    bi = jnp.arange(bsz)[:, None, None, None]
    hi = jnp.arange(nh)[None, :, None, None]
    blk_ids = jnp.arange(nb)
    n_chunks = seq // Q_CHUNK

    def one_chunk(c):
        start = c * Q_CHUNK
        qc = lax.dynamic_slice_in_dim(q, start, Q_CHUNK, axis=2).astype(jnp.float32)
        qpos = start + jnp.arange(Q_CHUNK)
        blk = start // MOBA_BLOCK
        gate = jnp.einsum('bhqd,bhnd->bhqn', qc, kmean)
        gate = jnp.where(blk_ids < blk, gate, -jnp.inf)
        _, idx = lax.top_k(gate, n_sel)
        valid = idx < blk
        kg = kb[bi, hi, idx].astype(jnp.float32)
        vg = vb[bi, hi, idx].astype(jnp.float32)
        s_sel = jnp.einsum('bhqd,bhqnkd->bhqnk', qc, kg) * scale
        s_sel = jnp.where(valid[..., None], s_sel, NEG_INF)
        own_start = blk * MOBA_BLOCK
        k_own = lax.dynamic_slice_in_dim(kp, own_start, MOBA_BLOCK, axis=2).astype(jnp.float32)
        v_own = lax.dynamic_slice_in_dim(vp, own_start, MOBA_BLOCK, axis=2).astype(jnp.float32)
        kpos = own_start + jnp.arange(MOBA_BLOCK)
        s_own = jnp.einsum('bhqd,bhkd->bhqk', qc, k_own) * scale
        s_own = jnp.where(kpos[None, :] <= qpos[:, None], s_own, NEG_INF)
        s = jnp.concatenate([s_sel.reshape(bsz, nh, Q_CHUNK, n_sel * MOBA_BLOCK), s_own], axis=-1)
        p = jax.nn.softmax(s, axis=-1)
        p_sel = p[..., :n_sel * MOBA_BLOCK].reshape(bsz, nh, Q_CHUNK, n_sel, MOBA_BLOCK)
        p_own = p[..., n_sel * MOBA_BLOCK:]
        o = (jnp.einsum('bhqnk,bhqnkd->bhqd', p_sel, vg)
             + jnp.einsum('bhqk,bhkd->bhqd', p_own, v_own))
        return o.astype(q.dtype)

    out = lax.map(one_chunk, jnp.arange(n_chunks))
    return out.transpose(1, 2, 0, 3, 4).reshape(bsz, nh, seq, hd)

def gla_attention(q, k, v, log_a):
    bsz, nh, seq, dk = q.shape
    dv = v.shape[-1]
    nc = seq // GLA_CHUNK

    def to_chunks(t):
        return t.astype(jnp.float32).reshape(bsz, nh, nc, GLA_CHUNK, t.shape[-1]).transpose(2, 0, 1, 3, 4)

    qc, kc, vc, gc = to_chunks(q), to_chunks(k), to_chunks(v), to_chunks(log_a)
    causal = jnp.tril(jnp.ones((GLA_CHUNK, GLA_CHUNK), dtype=bool))

    def step(state, inp):
        qi, ki, vi, gi = inp
        b = jnp.cumsum(gi, axis=2)
        diff = b[:, :, :, None, :] - b[:, :, None, :, :]
        decay = jnp.exp(jnp.where(causal[:, :, None], diff, -jnp.inf))
        attn = jnp.einsum('bhtd,bhsd,bhtsd->bhts', qi, ki, decay)
        o = (jnp.einsum('bhts,bhsv->bhtv', attn, vi)
             + jnp.einsum('bhtd,bhdv->bhtv', qi * jnp.exp(b), state))
        b_last = b[:, :, -1:, :]
        state = (jnp.exp(b_last[:, :, 0, :, None]) * state
                 + jnp.einsum('bhsd,bhsv->bhdv', ki * jnp.exp(b_last - b), vi))
        return state, o

    state0 = jnp.zeros((bsz, nh, dk, dv), jnp.float32)
    _, o = lax.scan(step, state0, (qc, kc, vc, gc))
    return o.transpose(1, 2, 0, 3, 4).reshape(bsz, nh, seq, dv).astype(v.dtype)

def even_mixer(x, w_in, w_gk2, b_gk2, gla_norm_g, w_out, pos):
    bsz, seq, _ = x.shape
    proj = x @ w_in
    aq, ak, av, bq, bk, bv, bgk, bog = jnp.split(proj, EVEN_SPLITS, axis=-1)

    def heads(t, n):
        return t.reshape(bsz, seq, n, -1).transpose(0, 2, 1, 3)

    o_a = moba_attention(rotary(heads(aq, A_HEADS), pos), rotary(heads(ak, A_HEADS), pos),
                         heads(av, A_HEADS))
    o_a = o_a.transpose(0, 2, 1, 3).reshape(bsz, seq, A_WIDTH)
    log_a = jax.nn.log_sigmoid((bgk @ w_gk2 + b_gk2).astype(jnp.float32)) / GLA_GATE_NORM
    o_b = gla_attention(heads(bq, B_HEADS) * (B_HEAD_K ** -0.5), heads(bk, B_HEADS),
                        heads(bv, B_HEADS), heads(log_a, B_HEADS))
    o_b = rms_norm_2(o_b, gla_norm_g[:, None, :])
    o_b = o_b.transpose(0, 2, 1, 3).reshape(bsz, seq, B_VAL_WIDTH) * jax.nn.silu(bog)
    return jnp.concatenate([o_a, o_b], axis=-1) @ w_out

def lru_combine(left, right):
    a1, b1 = left
    a2, b2 = right
    return a1 * a2, a2 * b1 + b2

def odd_mixer(x, w_in, conv_w, conv_b, w_a, b_a, w_x, b_x, lam, w_out):
    bsz, seq, _ = x.shape
    gate_branch, xr = jnp.split(x @ w_in, 2, axis=-1)
    xr = causal_dwconv(xr, conv_w, conv_b)
    xb = xr.reshape(bsz, seq, RG_BLOCKS, RG_BLOCK_W)
    r = jax.nn.sigmoid(jnp.einsum('bsnc,ncd->bsnd', xb, w_a).reshape(bsz, seq, D_RNN) + b_a)
    i = jax.nn.sigmoid(jnp.einsum('bsnc,ncd->bsnd', xb, w_x).reshape(bsz, seq, D_RNN) + b_x)
    log_a = (-LRU_C * r.astype(jnp.float32)) * jax.nn.softplus(-lam.astype(jnp.float32))
    a = jnp.exp(log_a)
    u = jnp.sqrt(-jnp.expm1(2.0 * log_a)) * (i * xr).astype(jnp.float32)
    _, h = lax.associative_scan(lru_combine, (a, u), axis=1)
    y = h.astype(x.dtype) * jax.nn.gelu(gate_branch)
    return y @ w_out

def conv_ffn(x, w_up, conv_w, conv_b, w_down):
    h = causal_dwconv(x @ w_up, conv_w, conv_b)
    u, g = jnp.split(h, 2, axis=-1)
    return (u * jax.nn.gelu(g)) @ w_down

def second_inputs(seed: int = 0) -> dict:
    key = jax.random.key(seed)
    ks = jax.random.split(key, 24)

    def nrm(k, shape, scale):
        return jax.random.normal(k, shape, jnp.float32) * scale

    u = jax.random.uniform(ks[14], (N_ODD, D_RNN), jnp.float32, 0.9, 0.999)
    sig = u ** (1.0 / LRU_C)
    lam = jnp.log(sig) - jnp.log1p(-sig)
    return {
        "x": nrm(ks[0], (BATCH, SEQ, D_MODEL), 1.0),
        "mix_norm_g": 1.0 + nrm(ks[1], (DEPTH, D_MODEL), 0.02),
        "ffn_norm_g": 1.0 + nrm(ks[2], (DEPTH, D_MODEL), 0.02),
        "final_norm_g": 1.0 + nrm(ks[3], (D_MODEL,), 0.02),
        "ev_w_in": nrm(ks[4], (N_EVEN, D_MODEL, EVEN_PROJ), D_MODEL ** -0.5),
        "ev_w_gk2": nrm(ks[5], (N_EVEN, GLA_GATE_RANK, B_KEY_WIDTH), GLA_GATE_RANK ** -0.5),
        "ev_b_gk2": nrm(ks[6], (N_EVEN, B_KEY_WIDTH), 0.1),
        "ev_gla_norm_g": 1.0 + nrm(ks[7], (N_EVEN, B_HEADS, B_HEAD_V), 0.02),
        "ev_w_out": nrm(ks[8], (N_EVEN, MIX_WIDTH_2, D_MODEL), MIX_WIDTH_2 ** -0.5),
        "od_w_in": nrm(ks[9], (N_ODD, D_MODEL, 2 * D_RNN), D_MODEL ** -0.5),
        "od_conv_w": nrm(ks[10], (N_ODD, RG_CONV, D_RNN), RG_CONV ** -0.5),
        "od_conv_b": nrm(ks[11], (N_ODD, D_RNN), 0.01),
        "od_w_a": nrm(ks[12], (N_ODD, RG_BLOCKS, RG_BLOCK_W, RG_BLOCK_W), RG_BLOCK_W ** -0.5),
        "od_b_a": nrm(ks[13], (N_ODD, D_RNN), 0.01),
        "od_w_x": nrm(ks[15], (N_ODD, RG_BLOCKS, RG_BLOCK_W, RG_BLOCK_W), RG_BLOCK_W ** -0.5),
        "od_b_x": nrm(ks[16], (N_ODD, D_RNN), 0.01),
        "od_lambda": lam,
        "od_w_out": nrm(ks[17], (N_ODD, D_RNN, D_MODEL), D_RNN ** -0.5),
        "ffn_w_up": nrm(ks[18], (DEPTH, D_MODEL, 2 * D_FF_2), D_MODEL ** -0.5),
        "ffn_conv_w": nrm(ks[19], (DEPTH, FFN_CONV, 2 * D_FF_2), FFN_CONV ** -0.5),
        "ffn_conv_b": nrm(ks[20], (DEPTH, 2 * D_FF_2), 0.01),
        "ffn_w_down": nrm(ks[21], (DEPTH, D_FF_2, D_MODEL), D_FF_2 ** -0.5),
    }

def second_block(x, mix_norm_g, ffn_norm_g, final_norm_g,
              ev_w_in, ev_w_gk2, ev_b_gk2, ev_gla_norm_g, ev_w_out,
              od_w_in, od_conv_w, od_conv_b, od_w_a, od_b_a, od_w_x, od_b_x, od_lambda, od_w_out,
              ffn_w_up, ffn_conv_w, ffn_conv_b, ffn_w_down):
    seq = x.shape[1]
    pos = jnp.arange(seq, dtype=jnp.int32)
    h = x
    for l in range(DEPTH):
        hn = rms_norm_2(h, mix_norm_g[l])
        j = l // 2
        if l % 2 == 0:
            mix = even_mixer(hn, ev_w_in[j], ev_w_gk2[j], ev_b_gk2[j], ev_gla_norm_g[j], ev_w_out[j], pos)
        else:
            mix = odd_mixer(hn, od_w_in[j], od_conv_w[j], od_conv_b[j], od_w_a[j], od_b_a[j],
                            od_w_x[j], od_b_x[j], od_lambda[j], od_w_out[j])
        h = h + mix
        h = h + conv_ffn(rms_norm_2(h, ffn_norm_g[l]), ffn_w_up[l], ffn_conv_w[l], ffn_conv_b[l], ffn_w_down[l])
    return rms_norm_2(h, final_norm_g)


_first_inputs = second_inputs


def second_inputs(seed=0):
    import zlib

    import numpy as np

    out = dict(_first_inputs(seed))
    spreads = {}
    factors = {'final_norm_g': 2.997,
     'ev_gla_norm_g': 5.694,
     'od_conv_b': 2.727,
     'od_b_a': 8.0,
     'od_b_x': 8.0,
     'ffn_conv_b': 5.009}
    for name, (base, spread) in spreads.items():
        noise = np.random.default_rng([zlib.crc32(name.encode()), seed]).standard_normal(out[name].shape)
        drawn = base * np.exp(spread * noise) if base else spread * noise
        out[name] = __import__('jax').numpy.asarray(drawn.astype(out[name].dtype))
    for name, factor in factors.items():
        out[name] = (out[name] * factor).astype(out[name].dtype)
    return out


def setup_inputs(seed=0):
    out = dict(first_inputs(seed))
    for name, value in second_inputs(seed + 1).items():
        if name != "x":
            out[name + "_2"] = value
    return out


def reference(
    x, c, ctx, c_ctx, w_ada, b_ada, g_mix, g_mlp, w_in, w_pool, s_pool, lam_q1, lam_k1, lam_q2,
    lam_k2, g_subln, w_out, w_mlp1, w_mlp2, g_final, mix_norm_g_2, ffn_norm_g_2, final_norm_g_2,
    ev_w_in_2, ev_w_gk2_2, ev_b_gk2_2, ev_gla_norm_g_2, ev_w_out_2, od_w_in_2, od_conv_w_2,
    od_conv_b_2, od_w_a_2, od_b_a_2, od_w_x_2, od_b_x_2, od_lambda_2, od_w_out_2, ffn_w_up_2,
    ffn_conv_w_2, ffn_conv_b_2, ffn_w_down_2,
):
    x = first_block(
        x, c, ctx, c_ctx, w_ada, b_ada, g_mix, g_mlp, w_in, w_pool, s_pool, lam_q1, lam_k1,
        lam_q2, lam_k2, g_subln, w_out, w_mlp1, w_mlp2, g_final,
    )
    return second_block(
        x, mix_norm_g_2, ffn_norm_g_2, final_norm_g_2, ev_w_in_2, ev_w_gk2_2, ev_b_gk2_2,
        ev_gla_norm_g_2, ev_w_out_2, od_w_in_2, od_conv_w_2, od_conv_b_2, od_w_a_2, od_b_a_2,
        od_w_x_2, od_b_x_2, od_lambda_2, od_w_out_2, ffn_w_up_2, ffn_conv_w_2, ffn_conv_b_2,
        ffn_w_down_2,
    )


_drawn_inputs = setup_inputs


def setup_inputs(seed=0):
    import zlib

    import numpy as np

    out = dict(_drawn_inputs(seed))
    spreads = {}
    factors = {'g_mix': 3.302,
     'lam_q2': 2.757,
     'lam_k2': 3.224,
     'g_subln': 4.524,
     'ffn_norm_g_2': 5.909,
     'final_norm_g_2': 22.885,
     'ev_gla_norm_g_2': 3.064,
     'od_b_a_2': 200.0,
     'od_b_x_2': 200.0,
     'od_w_in_2': 26.432,
     'od_conv_w_2': 27.096,
     'od_conv_b_2': 64.0,
     'od_w_a_2': 64.0,
     'od_w_x_2': 64.0,
     'od_lambda_2': 64.0,
     'od_w_out_2': 26.504,
     'ffn_conv_b_2': 3.389}
    for name, (base, spread) in spreads.items():
        noise = np.random.default_rng([zlib.crc32(name.encode()), seed]).standard_normal(out[name].shape)
        drawn = base * np.exp(spread * noise) if base else spread * noise
        out[name] = __import__('jax').numpy.asarray(drawn.astype(out[name].dtype))
    for name, factor in factors.items():
        out[name] = (out[name] * factor).astype(out[name].dtype)
    return out
```

```python
import concourse.bass as bass
from concourse import mybir
from contextlib import ExitStack
import math
import numpy as np

F32 = mybir.dt.float32
F32R = mybir.dt.float32r
I32 = mybir.dt.int32
ALU = mybir.AluOpType
ACT = mybir.ActivationFunctionType
AX_X = mybir.AxisListType.X

P = 128
D = 1024
KT = D // P
SEQ = 256
ALLT = 2 * SEQ
EPS = 1e-6
CH = 256
LAM_INIT = [0.8 - 0.6 * math.exp(-0.3 * l) for l in range(2)]

N_WIN = [0, 44]
N_WOUT = [8, 52]
N_MLP = [12, 56]
N_EV, N_EVOUT = 88, 100
N_FFN = [104, 154]
N_OD, N_RG, N_ODOUT = 140, 148, 150
N_CHUNKS = 190

VEC = {}
V_COLS = 0
for _name, _n in (
    [("c", 16)]
    + [(f"{k}{l}", n) for l in range(2) for k, n in
       (("g_mix", 8), ("g_mlp", 8), ("s_pool", 4), ("g_sub", 1), ("b_ada", 48), ("lam", 4))]
    + [("g_final", 8), ("mix_g0", 8), ("mix_g1", 8), ("ffn_g0", 8), ("ffn_g1", 8), ("final_g", 8),
       ("b_gk", 2), ("g_gla", 4), ("od_w", 32), ("od_b", 8), ("b_a", 8), ("b_x", 8), ("lam_od", 8),
       ("ffn0", 192), ("ffn1", 192)]
):
    VEC[_name] = V_COLS
    V_COLS += _n

CST = {"cos": 0, "sin": 256, "cos2": 512, "sin2": 768, "ident": 1024, "ones": 1152, "causal": 1280}
C_COLS = 1408


class Steps:

    def __init__(self, eng, sem):
        self.eng, self.sem, self.n, self.loop = eng, sem, 0, None

    def step(self, ins):
        ins.then_inc(self.sem, 1)
        self.n += 1
        return ins

    def join(self):
        self.eng.wait_ge(self.sem, self.n if self.loop is None else self.loop[0] * self.loop[1] + self.n)

    def enter(self, i, per):
        self.loop, self.start = (i, per), self.n

    def leave(self, iters):
        per = self.n - self.start
        assert per == self.loop[1], (per, self.loop[1])
        self.n += per * (iters - 1)
        self.loop = None


def build_program(nc, w_stream, ada_stream, x_in, vec_in, cst_in, pool_mats, gla_masks, w_pool, w_gk, w_gk2,
                  out):
    ctx = ExitStack()
    with ctx:
        base = (nc.sbuf_base + 31) // 32 * 32
        top = [base]

        def place(name, shape, dt=F32, at=None):
            size = 4
            for d in shape[1:]:
                size *= d
            if at is None:
                at = top[0]
                top[0] += size
            return nc.alloc_sbuf_tensor_at(name, shape, dt, offset=at)

        x = place("x", [P, KT, ALLT])
        h_hi = place("h_hi", [P, KT, ALLT], F32R)
        h_lo = place("h_lo", [P, KT, ALLT], F32R)
        g_base = top[0]
        g_hi = place("g_hi", [P, KT, ALLT], F32R)
        g_lo = place("g_lo", [P, KT, ALLT], F32R)
        w_raw = place("w_raw", [P, 4, KT * CH])
        w_hi = place("w_hi", [P, 2, KT, CH], F32R)
        w_lo = place("w_lo", [P, 2, KT, CH], F32R)
        r_base = top[0]
        top[0] += 32768
        a_base = top[0]
        ada_w = place("ada_w", [P, 4, KT, P])
        vec = place("vec", [P, V_COLS])
        cst = place("cst", [P, C_COLS])
        wp = place("wp", [P, 2, 4, P])
        c_act = place("c_act", [P, KT, 2])
        ada = place("ada", [P, 2, 48, 2])
        mod = place("mod", [P, 2, 2, KT, 2])
        small = place("small", [P, 96])
        assert top[0] <= nc.sbuf_usable_end, top[0]

        KB = 1024
        qT = place("qT", [P, 4, ALLT], at=r_base)
        kT = place("kT", [P, 4, ALLT], at=r_base + 8 * KB)
        v_tok = place("v_tok", [P, 4, 512], at=r_base + 16 * KB)
        u_tok = place("u_tok", [P, 4, 512], at=r_base + 24 * KB)
        sq = place("sq", [P, KT, ALLT], at=r_base)
        diag = place("diag", [P, 4, P], at=r_base + 16 * KB)
        h_raw = place("h_raw", [P, 2, ALLT], at=r_base + 18 * KB)
        relu = place("relu", [P, 2, 2, ALLT], at=r_base + 16 * KB)
        relu2 = place("relu2", [P, 2, ALLT], at=r_base + 24 * KB)
        aq = place("aq", [P, 4, SEQ], at=r_base)
        ak = place("ak", [P, 4, SEQ], at=r_base + 4 * KB)
        av = place("av", [P, 2, 512], at=r_base + 8 * KB)
        bq = place("bq", [P, 2, SEQ], at=r_base + 12 * KB)
        bk = place("bk", [P, 2, SEQ], at=r_base + 14 * KB)
        bv = place("bv", [P, 2, 512], at=r_base + 16 * KB)
        bog = place("bog", [P, 4, SEQ], at=r_base + 20 * KB)
        bcum = place("bcum", [P, 2, SEQ], at=r_base + 24 * KB)
        wgk = place("wgk", [P, KT, 16], at=r_base + 26 * KB)
        wgk2 = place("wgk2", [16, SEQ], at=r_base + 26 * KB + 512)
        gkT = place("gkT", [16, SEQ], at=r_base + 26 * KB + 1536)
        rot_tmp = place("rot_tmp", [P, 2, SEQ], at=r_base + 30 * KB)
        conv_y = place("conv_y", [P, 2, 2, SEQ], at=r_base)
        gelu_g = place("gelu_g", [P, 2, SEQ], at=r_base + 4 * KB)
        ffn_p = place("ffn_p", [P, 2, SEQ], at=r_base + 6 * KB)
        conv_w = place("conv_w", [P, 64], at=r_base + 8 * KB)
        gate = place("gate", [P, KT, SEQ], at=r_base)
        xr = place("xr", [P, KT, SEQ], at=r_base + 8 * KB)
        rg_r = place("rg_r", [P, KT, SEQ], at=r_base + 16 * KB)
        rg_i = place("rg_i", [P, KT, SEQ], at=r_base + 24 * KB)
        prob = place("prob", [P, 2, 2, 512], at=g_base)
        wgt = place("wgt", [P, 2, 512], at=g_base + 8 * KB)
        wgtT = place("wgtT", [P, 2, 512], at=g_base + 12 * KB)
        o_sq = place("o_sq", [P, 512], at=g_base + 16 * KB)
        o_n = place("o_n", [P, 512], at=g_base + 18 * KB)
        rope_tmp = place("rope_tmp", [P, 2, SEQ], at=g_base + 20 * KB)
        pool_y = place("pool_y", [P, 2, SEQ], at=g_base + 22 * KB)
        pmat = place("pmat", [P, 2, 4, SEQ], at=g_base + 24 * KB)
        y_out = place("y_out", [P, KT, SEQ], at=g_base)
        a_p = place("a_p", [P, 8, SEQ], at=g_base)
        a_pT = place("a_pT", [P, 2, 8, P], at=g_base + 8 * KB)
        a_o = place("a_o", [P, 512], at=g_base + 16 * KB)
        a_raw = place("a_raw", [P, 4, P], at=g_base + 18 * KB)
        attn = place("attn", [P, 4, 2, 2, P], at=g_base)
        attnX = place("attnX", [P, 4, 2, P], at=g_base + 8 * KB)
        dec = place("dec", [P, 2, 2, SEQ], at=g_base + 16 * KB)
        gq = place("gq", [P, 2, 2, SEQ], at=g_base + 24 * KB)
        gk = place("gk", [P, 2, 2, SEQ], at=g_base + 28 * KB)
        b_o = place("b_o", [P, 512], at=g_base + 20 * KB)
        b_sq = place("b_sq", [P, 512], at=g_base + 22 * KB)
        b_raw = place("b_raw", [P, 4, P], at=g_base + 12 * KB)
        gl_e = place("gl_e", [P, 2, SEQ], at=g_base + 12 * KB)
        gl_z = place("gl_z", [P, 2, SEQ], at=g_base + 14 * KB)
        gmask = place("gmask", [P, 8, P], I32, at=a_base)
        xr_hi = place("xr_hi", [P, KT, SEQ], F32R, at=g_base)
        xr_lo = place("xr_lo", [P, KT, SEQ], F32R, at=g_base + 8 * KB)
        rg_a = place("rg_a", [P, KT, SEQ], at=g_base + 16 * KB)
        rg_t = place("rg_t", [P, KT, SEQ], at=g_base + 24 * KB)

        ps = ctx.enter_context(nc.psum_tensor("ps", [P, 8, 512], F32))

        def sem(name):
            return ctx.enter_context(nc.semaphore(name))

        raw_in = [sem(f"raw_in{i}") for i in range(4)]
        hi_ready, lo_ready, gemm_done, psum_free = sem("hi_ready"), sem("lo_ready"), sem("gemm_done"), sem("psum_free")
        ada_in = [sem(f"ada_in{i}") for i in range(4)]
        ada_done, ada_read = sem("ada_done"), sem("ada_read")
        vec_in_s, cst_in_s, x_in_s = sem("vec_in"), sem("cst_in"), sem("x_in")
        pool_in, glam_in, gk_in = sem("pool_in"), sem("glam_in"), sem("gk_in")
        silu_done = sem("silu_done")
        lam_prod, lam_sum, lam_exp, lam_done = sem("lam_prod"), sem("lam_sum"), sem("lam_exp"), sem("lam_done")
        h_ready, g_ready = sem("h_ready"), sem("g_ready")
        sq_ready, ss_done, std_ready, diag_ready, rbc_ready = (
            sem("sq_ready"), sem("ss_done"), sem("std_ready"), sem("diag_ready"), sem("rbc_ready"))
        norm_raw, norm_hi, x_final = sem("norm_raw"), sem("norm_hi"), sem("x_final")
        relu_ready, ghi_ready = sem("relu_ready"), sem("ghi_ready")
        py_done, py_copied, po_done, po_hi, po_lo = (
            sem("py_done"), sem("py_copied"), sem("po_done"), sem("po_hi"), sem("po_lo"))
        scores, nmax, exps, wgt_ready, wgtT_done, wgtT_copied, pv_done = (
            sem("scores"), sem("nmax"), sem("exps"), sem("wgt_ready"), sem("wgtT_done"), sem("wgtT_copied"),
            sem("pv_done"))
        osq_ready, oss_ready, ostd_ready, on_ready, oT_done, ohi_ready, olo_ready = (
            sem("osq_ready"), sem("oss_ready"), sem("ostd_ready"), sem("on_ready"), sem("oT_done"),
            sem("ohi_ready"), sem("olo_ready"))
        m_scores, m_max, m_exp, m_T, m_Tc, m_pv, m_o, m_oT, m_raw, m_hi, m_lo = (
            sem("m_scores"), sem("m_max"), sem("m_exp"), sem("m_T"), sem("m_Tc"), sem("m_pv"), sem("m_o"),
            sem("m_oT"), sem("m_raw"), sem("m_hi"), sem("m_lo"))
        gk_done, gk_copied, z_done, z_ready, e_ready, l_ready, b_ready = (
            sem("gk_done"), sem("gk_copied"), sem("z_done"), sem("z_ready"), sem("e_ready"), sem("l_ready"),
            sem("b_ready"))
        l_diff, l_dec, l_qk, l_scores, l_merged, bog_act = (
            sem("l_diff"), sem("l_dec"), sem("l_qk"), sem("l_scores"), sem("l_merged"), sem("bog_act"))
        b_pv, b_sqr, b_ssr, b_stdr, b_on, b_oT, b_rawr, b_hi, b_lo = (
            sem("b_pv"), sem("b_sqr"), sem("b_ssr"), sem("b_stdr"), sem("b_on"), sem("b_oT"), sem("b_rawr"),
            sem("b_hi"), sem("b_lo"))
        conv_w_ready, conv0, gelu_ready, prod_ready, prod_hi = (
            sem("conv_w_ready"), sem("conv0"), sem("gelu_ready"), sem("prod_ready"),
            sem("prod_hi"))
        xc0, xc_hi, gate_act = (
            sem("xc0"), sem("xc_hi"), sem("gate_act"))
        lam_e, lam_c, sig_r, sig_i, rg_exp, rg_s, rg_sqrt, rg_y, rg_yhi, rg_ylo = (
            sem("lam_e"), sem("lam_c"), sem("sig_r"), sem("sig_i"), sem("rg_exp"), sem("rg_s"), sem("rg_sqrt"),
            sem("rg_y"), sem("rg_yhi"), sem("rg_ylo"))
        out_ready, stored = sem("out_ready"), sem("stored")
        eps_set = sem("eps_set")
        act_step, dve_step = sem("act_step"), sem("dve_step")

        def V(name, i=0, n=1):
            return vec[:, VEC[name] + i:VEC[name] + i + n]

        def C(name, n=256):
            return cst[:, CST[name]:CST[name] + n]

        ones, ident, causal = C("ones", P), C("ident", P), C("causal", P)

        def bc(ap, n):
            return ap.rearrange("p (o m) -> p o m", o=1).broadcast_to([ap.shape[0], n, ap.shape[1]])

        def bcl(ap, n):
            return ap.rearrange("p (m o) -> p m o", o=1).broadcast_to([ap.shape[0], ap.shape[1], n])

        S_EPS, S_STD, S_RS, S_MAX, S_Z, S_R, S_NLAM, S_GS = 0, 1, 5, 9, 25, 33, 41, 43
        S_LP, S_LE, S_LAMP, S_OSS, S_OSTD, S_ORS = 45, 49, 53, 61, 69, 77

        def sm(c, n=1):
            return small[:, c:c + n]

        S2 = place("small2", [P, 64])
        assert top[0] <= nc.sbuf_usable_end, top[0]

        NORMS = [("mod", 0, 0, ALLT), ("mod", 0, 1, ALLT), ("mod", 1, 0, ALLT), ("mod", 1, 1, SEQ),
                 ("x", "g_final", None, SEQ), ("gain", "mix_g0", None, SEQ), ("gain", "ffn_g0", None, SEQ),
                 ("gain", "mix_g1", None, SEQ), ("gain", "ffn_g1", None, SEQ), ("out", "final_g", None, SEQ)]
        H_NORM = [0, 1, 2, 3, None, 4, 5, 6, 7, None]
        H0 = {"win0": 0, "mlp0": 8, "win1": 16, "mlp1": 24, "ev": 32, "ffn0": 40, "od": 48, "ffn1": 56}
        G0 = {"mlp0": 0, "mlp1": 32, "ffn0": 64, "od": 88, "ffn1": 96}
        X_AT = [0, 12, 44, 56, 88, 88, 104, 140, 154, 190]

        block = ctx.enter_context(nc.Block())

        @block.sync
        def _(sp):
            def load_chunk(n, r, wait=None):
                if wait is not None:
                    sp.wait_ge(lo_ready, wait)
                sp.dma_start(w_raw[:, r, :], w_stream[n] if isinstance(n, int) else
                             w_stream[bass.ds(n, 1)].rearrange("a p n -> p (a n)")).then_inc(raw_in[r], 16)

            def load_ada(a, r, wait=None):
                if wait is not None:
                    sp.wait_ge(ada_done, wait)
                sp.dma_start(ada_w[:, r, :, :].rearrange("p k n -> p (k n)"), ada_stream[a] if isinstance(a, int) else
                             ada_stream[bass.ds(a, 1)].rearrange("a p n -> p (a n)")).then_inc(ada_in[r], 16)

            sp.dma_start(vec[:, :], vec_in).then_inc(vec_in_s, 16)
            sp.dma_start(x[:, :, :], x_in).then_inc(x_in_s, 16)
            for a in range(16):
                load_ada(a, a % 4, a - 3 if a >= 4 else None)
                if a >= 8 and a % 2:
                    load_chunk((a - 8) // 2, (a - 8) // 2)
            n, a = 0, 16
            for n in range(12):
                if n >= 4:
                    load_chunk(n, n % 4, n - 3)
                for _ in range(3 if n < 8 else 2):
                    load_ada(a, a % 4, a - 3)
                    a += 1
            with sp.Fori(0, 4) as it:
                r = 0
                for c in range(8):
                    n = N_MLP[0] + c
                    load_chunk(it * 8 + n, n % 4, it * 8 + (n - 3))
                    for _ in range(1 + c % 2):
                        load_ada(it * 12 + (48 + r), r % 4, it * 12 + (48 + r - 3))
                        r += 1
            with sp.Fori(0, (N_CHUNKS - N_WIN[1]) // 4) as it:
                for c in range(4):
                    n = N_WIN[1] + c
                    load_chunk(it * 4 + n, n % 4, it * 4 + (n - 3))
            for n in range(N_CHUNKS // 4 * 4, N_CHUNKS):
                load_chunk(n, n % 4, n - 3)
            sp.wait_ge(out_ready, KT)
            sp.dma_start(out, y_out[:, :, :]).then_inc(stored, 16)
            sp.wait_ge(stored, 16)

        @block.gpsimd
        def _(pool):
            pool.memset(sm(S_EPS), EPS).then_inc(eps_set, 1)
            pool.dma_start(cst[:, :], cst_in).then_inc(cst_in_s, 16)
            pool.dma_start(wp[:, :, :, :], w_pool).then_inc(pool_in, 16)
            pool.dma_start(pmat[:, :, :, :], pool_mats).then_inc(pool_in, 16)
            pool.wait_ge(psum_free, N_WIN[1])
            pool.dma_start(pmat[:, :, :, :], pool_mats).then_inc(pool_in, 16)
            pool.wait_ge(ada_done, 96)
            pool.dma_start(gmask[:, :, :], gla_masks).then_inc(glam_in, 16)
            pool.wait_ge(psum_free, N_EV)
            pool.dma_start(wgk[:, :, :], w_gk).then_inc(gk_in, 16)
            pool.dma_start(wgk2[:, :], w_gk2).then_inc(gk_in, 16)

        @block.tensor
        def _(pe):
            mm = nc.tensor.matmul

            def same(n):
                return n

            def start_chunk(n, at):
                pe.wait_ge(lo_ready, at(n + 1))
                if n >= 2:
                    pe.wait_ge(psum_free, at(n - 1))

            def gemm_f(n, hi, lo, cols, ready, at=same):
                start_chunk(n, at)
                s = n % 2
                for k in range(KT):
                    if ready is not None:
                        pe.wait_ge(ready[0], at_of(ready, at)(k + 1))
                    for m in range(2):
                        o = ps[:, 2 * s + m, 0:cols.stop - cols.start]
                        wh, wl = w_hi[:, s, k, m * P:(m + 1) * P], w_lo[:, s, k, m * P:(m + 1) * P]
                        mm(o, wh, hi[:, k, cols], start=(k == 0), stop=False)
                        mm(o, wh, lo[:, k, cols], start=False, stop=False)
                        last = mm(o, wl, hi[:, k, cols], start=False, stop=(k == KT - 1))
                last.then_inc(gemm_done, 1)

            def at_of(ready, at):
                if len(ready) == 2:
                    return lambda k: ready[1] + k
                return lambda k: ready[3] * ready[2] + (ready[1] + k)

            def gemm_t(n, tiles, ready=None):
                start_chunk(n, same)
                if ready is not None:
                    pe.wait_ge(ready[0], ready[1] + KT)
                s = n % 2
                for i in range(tiles):
                    o = ps[:, 2 * s + i // 2, (i % 2) * CH:(i % 2 + 1) * CH]
                    t = slice(i * P, (i + 1) * P)
                    for k in range(KT):
                        mm(o, h_hi[:, k, t], w_hi[:, s, k, :], start=(k == 0), stop=False)
                        mm(o, h_lo[:, k, t], w_hi[:, s, k, :], start=False, stop=False)
                        last = mm(o, h_hi[:, k, t], w_lo[:, s, k, :], start=False, stop=(k == KT - 1))
                last.then_inc(gemm_done, 1)

            def ada_tile(r, bank, col, wait):
                pe.wait_ge(ada_in[r], wait)
                o = ps[:, bank, col:col + 2]
                for k in range(KT):
                    last = mm(o, ada_w[:, r, k, :], c_act[:, k, :], start=(k == 0), stop=(k == KT - 1))
                last.then_inc(ada_done, 1)

            def ada_tiles(first, count, bank):
                for a in range(first, first + count):
                    ada_tile(a % 4, bank, 2 * (a % 48), 16 * (a // 4 + 1))

            def norm(k):
                nt = NORMS[k][3] // P
                for t in range(KT):
                    pe.wait_ge(sq_ready, KT * k + t + 1)
                    for j in range(nt):
                        last = mm(ps[:, 4, j:j + 1], sq[:, t, j * P:(j + 1) * P], ones[:, 0:1],
                                  start=(t == 0 and j == 0), stop=(t == KT - 1), skip_group_check=True)
                last.then_inc(ss_done, 1)
                pe.wait_ge(diag_ready, k + 1)
                mm(ps[:, 5, 0:nt * P], ones, diag[:, 0:nt, :], start=True, stop=True).then_inc(rbc_ready, 1)

            def pooling(streams, m0):
                def mix_out(m, g):
                    pe.wait_ge(py_copied, m + 1)
                    if m - m0 >= 2:
                        pe.wait_ge(po_lo, m - 1)
                    mm(ps[:, 2 + m % 2, 0:SEQ], wp[:, m0 // 8, g, :], pool_y[:, m % 2, :], start=True, stop=True)\
                        .then_inc(po_done, 1)
                todo = [(g, s) for g in range(4) for s in range(streams)]
                for i, (g, s) in enumerate(todo):
                    m = m0 + i
                    if i >= 2:
                        pe.wait_ge(py_copied, m - 1)
                    for t in range(2):
                        last = mm(ps[:, m % 2, 0:SEQ], u_tok[:, 2 * s + t, g * P:(g + 1) * P], pmat[:, t, g, :],
                                  start=(t == 0), stop=(t == 1))
                    last.then_inc(py_done, 1)
                    if i:
                        mix_out(m - 1, todo[i - 1][0])
                mix_out(m0 + len(todo) - 1, todo[-1][0])

            def attention(units, u0, q0):
                def score(i):
                    qt, hd, k0 = units[i]
                    u = u0 + i
                    if i >= 3:
                        pe.wait_ge(exps, u - 2)
                    for a in range(2):
                        r = slice(64 * a, 64 * a + 64)
                        last = mm(ps[:, 2 + 2 * (u % 3) + a, 0:ALLT - k0], qT[r, hd, qt * P:(qt + 1) * P],
                                  kT[r, hd, k0:ALLT], start=True, stop=True)
                    last.then_inc(scores, 1)

                def transposes(i):
                    u, kb = u0 + i, (ALLT - units[i][2]) // P
                    pe.wait_ge(wgt_ready, u + 1)
                    if i:
                        pe.wait_ge(wgtT_copied, u)
                    if i >= 4 and i % 4 == 1:
                        pe.wait_ge(olo_ready, q0 + i // 4)
                    for b in range(kb):
                        last = nc.tensor.transpose(ps[:, 0, b * P:(b + 1) * P], wgt[:, u % 2, b * P:(b + 1) * P], ident)
                    last.then_inc(wgtT_done, 1)

                def values(i):
                    qt, hd, k0 = units[i]
                    u, kb = u0 + i, (ALLT - k0) // P
                    pe.wait_ge(wgtT_copied, u + 1)
                    if hd == 0 and i >= 4:
                        pe.wait_ge(on_ready, q0 + i // 4)
                    for b in range(kb):
                        last = mm(ps[:, 1, hd * P:(hd + 1) * P], wgtT[:, u % 2, b * P:(b + 1) * P],
                                  v_tok[:, k0 // P + b, hd * P:(hd + 1) * P], start=(b == 0), stop=(b == kb - 1))
                    last.then_inc(pv_done, 1)

                def outputs(q):
                    pe.wait_ge(on_ready, q + 1)
                    pe.wait_ge(wgtT_copied, u0 + min(4 * (q - q0 + 1) + 1, len(units)))
                    for hd in range(4):
                        last = nc.tensor.transpose(ps[:, 0, hd * P:(hd + 1) * P], o_n[:, hd * P:(hd + 1) * P], ident)
                    last.then_inc(oT_done, 1)

                for i in range(3):
                    score(i)
                for i in range(len(units)):
                    transposes(i)
                    if i + 3 < len(units):
                        score(i + 3)
                    values(i)
                    if i >= 4 and i % 4 == 0:
                        outputs(q0 + i // 4 - 1)
                outputs(q0 + len(units) // 4 - 1)

            pe.wait_ge(cst_in_s, 16)
            pe.wait_ge(lam_prod, 1)
            mm(ps[:, 6, 0:4], ones, small[:, S_LAMP:S_LAMP + 4], start=True, stop=True).then_inc(lam_sum, 1)
            pe.wait_ge(silu_done, 1)
            norm(0)
            ada_tiles(0, 16, 7)

            n_ada = 16
            for l in range(2):
                n0 = N_WIN[l]
                hr = (h_ready, H0[f"win{l}"])
                for c in range(8):
                    n = n0 + c
                    if c < 4:
                        width = ALLT if l == 0 or c >= 2 else SEQ
                        gemm_f(n, h_hi, h_lo, slice(0, width), hr if c == 0 else None)
                    else:
                        gemm_t(n, 4 if l == 0 or c < 6 else 2)
                    if l == 0:
                        ada_tiles(n_ada, 3, 6)
                        n_ada += 3
                pe.wait_ge(psum_free, n0 + 8)
                if l == 0:
                    pe.wait_ge(ada_read, 2)
                pe.wait_ge(pool_in, 32 + 16 * l)
                pooling(2 - l, 8 * l)
                pe.wait_ge(po_lo, 8 + 4 * l)
                if l == 0:
                    attention([(qt, hd, 0 if qt < 2 else SEQ) for qt in range(4) for hd in range(4)], 0, 0)
                else:
                    attention([(qt, hd, 0) for qt in range(2) for hd in range(4)], 16, 4)
                pe.wait_ge(olo_ready, 4 + 2 * l)
                for c in range(4):
                    gemm_f(N_WOUT[l] + c, h_hi, h_lo, slice(0, ALLT if l == 0 else SEQ), None)
                    if l == 0:
                        ada_tiles(n_ada, 2, 7)
                        n_ada += 2
                norm(2 * l + 1)
                width = slice(0, ALLT if l == 0 else SEQ)
                with pe.Fori(0, 4) as it:
                    def at(n):
                        return it * 8 + n
                    for c in range(8):
                        n = N_MLP[l] + c
                        if c < 4:
                            gemm_f(n, h_hi, h_lo, width, (h_ready, H0[f"mlp{l}"]) if c == 0 else None, at)
                        else:
                            gemm_f(n, g_hi, g_lo, width, (g_ready, G0[f"mlp{l}"], 8, it) if c == 4 else None, at)
                        if l == 0:
                            for r in range((3 * c + 1) // 2, (3 * c + 4) // 2):
                                pe.wait_ge(ada_in[r % 4], it * 48 + 16 * (12 + r // 4 + 1))
                                o = ps[:, 6, bass.ds(it * 24 + 2 * r, 2)]
                                for k in range(KT):
                                    last = mm(o, ada_w[:, r % 4, k, :], c_act[:, k, :], start=(k == 0), stop=(k == KT - 1))
                                last.then_inc(ada_done, 1)
                norm(2 * l + 2)
            norm(5)

            for c in range(12):
                n = N_EV + c
                if c in (4, 5, 8, 9):
                    gemm_t(n, 2)
                else:
                    gemm_f(n, h_hi, h_lo, slice(0, SEQ), (h_ready, H0["ev"]) if c == 0 else None)
            pe.wait_ge(gk_in, 32)
            for k in range(KT):
                for part in (h_hi, h_lo):
                    last = mm(ps[0:16, 4, 0:SEQ], wgk[:, k, :], part[:, k, 0:SEQ].bitcast(F32),
                              start=(k == 0 and part is h_hi), stop=(k == KT - 1 and part is h_lo))
            last.then_inc(gk_done, 1)
            pe.wait_ge(gk_copied, 1)
            for g in range(2):
                last = mm(ps[:, 5, g * SEQ:(g + 1) * SEQ], wgk2[:, g * P:(g + 1) * P], gkT[:, :], start=True, stop=True)
            last.then_inc(z_done, 1)
            pe.wait_ge(z_ready, 1)
            pe.wait_ge(psum_free, N_EV + 12)

            for qt in range(2):
                if qt:
                    pe.wait_ge(m_Tc, 1)
                for hd in range(8):
                    r = slice(64 * (hd % 2), 64 * (hd % 2) + 64)
                    c = (hd // 2 % 2) * SEQ
                    last = mm(ps[:, 4 + 2 * (hd // 4) + hd % 2, c:c + (qt + 1) * P], aq[r, hd // 2, qt * P:(qt + 1) * P],
                              ak[r, hd // 2, 0:(qt + 1) * P], start=True, stop=True)
                last.then_inc(m_scores, 1)
                pe.wait_ge(m_exp, qt + 1)
                for kb in range(qt + 1):
                    for hd in range(8):
                        last = nc.tensor.transpose(ps[:, 4 + 2 * kb + hd // 4, hd % 4 * P:(hd % 4 + 1) * P],
                                                   a_p[:, hd, kb * P:(kb + 1) * P], ident)
                last.then_inc(m_T, 1)
                pe.wait_ge(m_Tc, qt + 1)
                for hd in range(8):
                    for kb in range(qt + 1):
                        last = mm(ps[:, qt, hd * 64:(hd + 1) * 64], a_pT[:, kb, hd, :], av[:, kb, hd * 64:(hd + 1) * 64],
                                  start=(kb == 0), stop=(kb == qt))
                last.then_inc(m_pv, 1)
                pe.wait_ge(m_o, qt + 1)
                for i in range(4):
                    last = nc.tensor.transpose(ps[:, 2 + qt, i * P:(i + 1) * P], a_o[:, i * P:(i + 1) * P], ident)
                last.then_inc(m_oT, 1)

            pe.wait_ge(m_lo, 2)
            for lv in range(9):
                kk, qq = (bk, bq) if lv == 0 else (gk[:, lv % 2, :, :], gq[:, lv % 2, :, :])
                if lv:
                    pe.wait_ge(l_qk, lv)
                b0 = 4 * (lv % 2)
                if lv >= 2:
                    pe.wait_ge(l_merged, lv - 1)
                for hd in range(8):
                    r = slice(32 * (hd % 4), 32 * (hd % 4) + 32)
                    g = hd // 4
                    for t in range(2 if lv < 8 else 1):
                        c = (g * 2 + t) * P if lv < 8 else g * P
                        tq = t if lv < 8 else 1
                        last = mm(ps[:, b0 + hd % 4, c:c + P], kk[r, g, t * P:(t + 1) * P],
                                  qq[r, g, tq * P:(tq + 1) * P], start=True, stop=True, tile_position=(32 * (hd % 4), 0))
                last.then_inc(l_scores, 1)
            pe.wait_ge(l_merged, 9)
            for t in range(2):
                for hd in range(8):
                    o = ps[:, 4 + t, hd * 64:(hd + 1) * 64]
                    if t:
                        mm(o, attnX[:, hd % 4, hd // 4, :], bv[:, 0, hd * 64:(hd + 1) * 64], start=True, stop=False)
                    last = mm(o, attn[:, hd % 4, hd // 4, t, :], bv[:, t, hd * 64:(hd + 1) * 64], start=(t == 0), stop=True)
                last.then_inc(b_pv, 1)
            for t in range(2):
                pe.wait_ge(b_on, t + 1)
                for i in range(4):
                    last = nc.tensor.transpose(ps[:, 6 + t, i * P:(i + 1) * P], b_o[:, i * P:(i + 1) * P], ident)
                last.then_inc(b_oT, 1)

            pe.wait_ge(b_lo, 2)
            for c in range(4):
                gemm_f(N_EVOUT + c, h_hi, h_lo, slice(0, SEQ), None)
            norm(6)

            def ffn(l):
                with pe.Fori(0, 3) as it:
                    def at(n):
                        return it * 12 + n
                    for c in range(12):
                        n = N_FFN[l] + c
                        if c < 8:
                            gemm_f(n, h_hi, h_lo, slice(0, SEQ), (h_ready, H0[f"ffn{l}"]) if c == 0 else None, at)
                        else:
                            gemm_f(n, g_hi, g_lo, slice(0, SEQ), (g_ready, G0[f"ffn{l}"], 8, it) if c == 8 else None, at)

            ffn(0)
            norm(7)
            for c in range(8):
                gemm_f(N_OD + c, h_hi, h_lo, slice(0, SEQ), (h_ready, H0["od"]) if c == 0 else None)
            for w in range(2):
                n = N_RG + w
                pe.wait_ge(lo_ready, n + 1)
                if w == 0:
                    pe.wait_ge(g_ready, G0["od"] + KT)
                else:
                    pe.wait_ge(psum_free, N_RG)
                s = n % 2
                for b in range(4):
                    for m in range(2):
                        o = ps[:, 4 * (1 - w) + b, m * SEQ:(m + 1) * SEQ]
                        for kk in range(2):
                            k = 2 * b + kk
                            wh, wl = w_hi[:, s, k, m * P:(m + 1) * P], w_lo[:, s, k, m * P:(m + 1) * P]
                            mm(o, wh, xr_hi[:, k, :], start=(kk == 0), stop=False)
                            mm(o, wh, xr_lo[:, k, :], start=False, stop=False)
                            last = mm(o, wl, xr_hi[:, k, :], start=False, stop=(kk == 1))
                last.then_inc(gemm_done, 1)
            pe.wait_ge(rg_ylo, 2)
            for c in range(4):
                gemm_f(N_ODOUT + c, h_hi, h_lo, slice(0, SEQ), None)
            norm(8)
            ffn(1)
            norm(9)

        @block.scalar
        def _(act):
            A = nc.scalar.activation
            own = Steps(act, act_step)

            def same(n):
                return n

            def split_hi(n, at=same, it=None, per=0):
                if n >= N_CHUNKS:
                    return
                w = 16 * (n // 4 + 1)
                act.wait_ge(raw_in[n % 4], w if it is None else it * (per * 4) + w)
                if n >= 2:
                    act.wait_ge(gemm_done, at(n - 1))
                A(w_hi[:, n % 2, :, :].rearrange("p k n -> p (k n)"), w_raw[:, n % 4, :], ACT.Copy).then_inc(hi_ready, 1)

            def norm(k):
                mode, _, _, w = NORMS[k]
                act.wait_ge(x_in_s, 16)
                if k:
                    act.wait_ge(psum_free, X_AT[k])
                if k == 5:
                    act.wait_ge(x_final, KT)
                for t in range(KT):
                    A(sq[:, t, 0:w], x[:, t, 0:w], ACT.Square).then_inc(sq_ready, 1)
                act.wait_ge(ss_done, k + 1)
                A(small[:, S_STD:S_STD + w // P], ps[:, 4, 0:w // P], ACT.Sqrt, bias=sm(S_EPS), scale=1.0 / D)\
                    .then_inc(std_ready, 1)
                if H_NORM[k] is not None:
                    for t in range(KT):
                        n = KT * H_NORM[k] + t
                        act.wait_ge(norm_raw, n + 1)
                        A(h_hi[:, t, 0:w], h_raw[:, t % 2, 0:w], ACT.Copy).then_inc(norm_hi, 1)

            def pooling(streams, m0, l):
                todo = [(g, s) for g in range(4) for s in range(streams)]

                def scaled(m, g, s):
                    act.wait_ge(po_done, m + 1)
                    A(h_hi[:, g, s * SEQ:(s + 1) * SEQ], ps[:, 2 + m % 2, 0:SEQ], ACT.Copy, scale=V(f"s_pool{l}", g))\
                        .then_inc(po_hi, 1)
                for i, (g, s) in enumerate(todo):
                    m = m0 + i
                    act.wait_ge(py_done, m + 1)
                    A(pool_y[:, m % 2, :], ps[:, m % 2, 0:SEQ], ACT.Copy).then_inc(py_copied, 1)
                    if i:
                        scaled(m - 1, *todo[i - 1])
                scaled(m0 + len(todo) - 1, *todo[-1])

            def attention(units, u0, q0, l):
                def exponentials(i):
                    u, w = u0 + i, ALLT - units[i][2]
                    act.wait_ge(nmax, u + 1)
                    if i >= 2:
                        act.wait_ge(wgt_ready, u - 1)
                    for a in range(2):
                        last = A(prob[:, u % 2, a, 0:w], ps[:, 2 + 2 * (u % 3) + a, 0:w], ACT.Exp,
                                 bias=sm(S_MAX + 2 * (u % 4) + a), scale=0.125, accum_out=sm(S_Z + 2 * (u % 2) + a))
                    last.then_inc(exps, 1)

                def copyT(i):
                    u, w = u0 + i, ALLT - units[i][2]
                    act.wait_ge(wgtT_done, u + 1)
                    A(wgtT[:, u % 2, 0:w], ps[:, 0, 0:w], ACT.Copy).then_inc(wgtT_copied, 1)

                def head_norm(q):
                    act.wait_ge(pv_done, u0 + 4 * (q - q0 + 1))
                    A(o_sq[:, :], ps[:, 1, :], ACT.Square).then_inc(osq_ready, 1)
                    act.wait_ge(oss_ready, q + 1)
                    A(small[:, S_OSTD:S_OSTD + 4], small[:, S_OSS:S_OSS + 4], ACT.Sqrt, bias=sm(S_EPS), scale=1.0 / P)\
                        .then_inc(ostd_ready, 1)

                def out_hi(q):
                    act.wait_ge(oT_done, q + 1)
                    qt = units[4 * (q - q0)][0]
                    A(h_hi[:, 4:8, qt * P:(qt + 1) * P], ps[:, 0, :].rearrange("p (h t) -> p h t", h=4), ACT.Copy,
                      scale=small[:, S_GS + l:S_GS + l + 1]).then_inc(ohi_ready, 1)

                exponentials(0)
                for i in range(len(units)):
                    if i + 1 < len(units):
                        exponentials(i + 1)
                    copyT(i)
                    if i >= 3 and i % 4 == 3:
                        head_norm(q0 + i // 4)
                    if i >= 4 and i % 4 == 0:
                        out_hi(q0 + i // 4 - 1)
                out_hi(q0 + len(units) // 4 - 1)

            act.wait_ge(vec_in_s, 16)
            act.wait_ge(eps_set, 1)
            A(c_act[:, :, :].rearrange("p k s -> p (k s)"), V("c", 0, 16), ACT.Silu).then_inc(silu_done, 1)
            act.wait_ge(lam_sum, 1)
            A(sm(S_LE, 4), ps[:, 6, 0:4], ACT.Exp).then_inc(lam_exp, 1)
            norm(0)
            split_hi(0)
            split_hi(1)
            for l in range(2):
                for c in range(8):
                    split_hi(N_WIN[l] + c + 2)
                pooling(2 - l, 8 * l, l)
                if l == 0:
                    attention([(qt, hd, 0 if qt < 2 else SEQ) for qt in range(4) for hd in range(4)], 0, 0, l)
                else:
                    attention([(qt, hd, 0) for qt in range(2) for hd in range(4)], 16, 4, l)
                for c in range(4):
                    split_hi(N_WOUT[l] + c + 2)
                norm(2 * l + 1)
                w = ALLT if l == 0 else SEQ
                r0 = 16 * l
                with act.Fori(0, 4) as it:
                    def at(n):
                        return it * 8 + n
                    for c in range(8):
                        n = N_MLP[l] + c
                        if c < 4:
                            act.wait_ge(gemm_done, at(n + 1))
                            A(relu[:, c % 2, :, 0:w], ps[:, 2 * (n % 2):2 * (n % 2) + 2, 0:w], ACT.Relu)\
                                .then_inc(relu_ready, 1)
                            act.wait_ge(relu_ready, it * 4 + (r0 + c + 1))
                            A(g_hi[:, 2 * c:2 * c + 2, 0:w], relu[:, c % 2, :, 0:w], ACT.Square).then_inc(ghi_ready, 1)
                        split_hi(n + 2, at, it, 8)
                norm(2 * l + 2)
            norm(5)

            for c in range(12):
                if c >= 10:
                    act.wait_ge(psum_free, N_EV + c + 1)
                    b = bog[:, 2 * (c - 10):2 * (c - 10) + 2, :]
                    A(b, b, ACT.Silu).then_inc(bog_act, 1)
                split_hi(N_EV + c + 2)
            act.wait_ge(gk_done, 1)
            A(gkT[:, :], ps[0:16, 4, 0:SEQ], ACT.Copy).then_inc(gk_copied, 1)
            act.wait_ge(z_ready, 1)
            A(gl_e[:, :, :], gl_z[:, :, :], ACT.Abs).then_inc(e_ready, 1)
            act.wait_ge(e_ready, 1)
            A(gl_e[:, :, :], gl_e[:, :, :], ACT.Exp, scale=-1.0).then_inc(e_ready, 1)
            act.wait_ge(e_ready, 2)
            A(gl_e[:, :, :], gl_e[:, :, :], ACT.Ln, bias=1.0).then_inc(l_ready, 1)

            for qt in range(2):
                act.wait_ge(m_max, qt + 1)
                for hd in range(8):
                    s_i = (2 * (hd // 4) + hd % 2) * 2 + hd // 2 % 2
                    c = (hd // 2 % 2) * SEQ
                    last = A(a_p[:, hd, 0:(qt + 1) * P], ps[:, 4 + 2 * (hd // 4) + hd % 2, c:c + (qt + 1) * P], ACT.Exp,
                             bias=sm(S_MAX + s_i), scale=0.125, accum_out=sm(S_Z + hd))
                last.then_inc(m_exp, 1)
                act.wait_ge(m_T, qt + 1)
                A(a_pT[:, 0:qt + 1, :, :].rearrange("p k h t -> p (k h t)"),
                  ps[:, 4:4 + 2 * (qt + 1), :].rearrange("p b c -> p (b c)"), ACT.Copy).then_inc(m_Tc, 1)
                act.wait_ge(m_oT, qt + 1)
                A(h_hi[:, 0:4, qt * P:(qt + 1) * P], ps[:, 2 + qt, :].rearrange("p (h t) -> p h t", h=4), ACT.Copy)\
                    .then_inc(m_hi, 1)

            for lv in range(1, 9):
                act.wait_ge(l_diff, lv)
                d = dec[:, lv % 2, :, :]
                own.step(A(d, d, ACT.Abs))
                own.join()
                A(d, d, ACT.Exp, scale=-1.0 / 32).then_inc(l_dec, 1)
            for t in range(2):
                act.wait_ge(b_pv, t + 1)
                if t:
                    act.wait_ge(b_ssr, 1)
                A(b_sq[:, :], ps[:, 4 + t, :], ACT.Square).then_inc(b_sqr, 1)
                act.wait_ge(b_ssr, t + 1)
                A(small[:, S_OSTD:S_OSTD + 8], small[:, S_OSS:S_OSS + 8], ACT.Sqrt, bias=sm(S_EPS), scale=1.0 / 64)\
                    .then_inc(b_stdr, 1)
            for t in range(2):
                act.wait_ge(b_rawr, t + 1)
                A(h_hi[:, 4:8, t * P:(t + 1) * P], b_raw[:, :, :], ACT.Copy).then_inc(b_hi, 1)
            for c in range(4):
                split_hi(N_EVOUT + c + 2)
            norm(6)

            def ffn(l):
                def body(it, third):
                    def at(n):
                        return n + 12 * third if it is None else it * 12 + n

                    def pairs(j):
                        return 12 * l + 4 * third + j if it is None else it * 4 + (12 * l + j)

                    act.wait_ge(conv_w_ready, 3 * l + third + 1 if it is None else it + (3 * l + 1))
                    for c in range(12):
                        n = N_FFN[l] + c
                        if c < 8:
                            p = c % 2
                            act.wait_ge(gemm_done, at(n + 1))
                            for m in range(2):
                                o = 32 * p + 2 * (c // 2) + m
                                last = A(conv_y[:, p, m, :], ps[:, 2 * (n % 2) + m, 0:SEQ], ACT.Identity,
                                         scale=conv_w[:, o + 16:o + 17], bias=conv_w[:, o + 24:o + 25])
                            last.then_inc(conv0, 1)
                        m = n + 2
                        if it is None:
                            split_hi(m + 12 * third)
                        else:
                            split_hi(m, at, it, 12)
                        if c < 8 and c % 2:
                            act.wait_ge(psum_free, at(n + 1))
                            A(gelu_g[:, :, :], conv_y[:, 1, :, :], ACT.Gelu_apprx_tanh).then_inc(gelu_ready, 1)
                            act.wait_ge(prod_ready, pairs(c // 2 + 1))
                            A(g_hi[:, c - 1:c + 1, 0:SEQ], ffn_p[:, :, :], ACT.Copy).then_inc(prod_hi, 1)
                with act.Fori(0, 2) as it:
                    body(it, 0)
                body(None, 2)

            ffn(0)
            norm(7)
            A(S2[:, 0:8], V("lam_od", 0, 8), ACT.Abs).then_inc(lam_e, 1)
            act.wait_ge(lam_e, 1)
            A(S2[:, 0:8], S2[:, 0:8], ACT.Exp, scale=-1.0).then_inc(lam_e, 1)
            for c in range(8):
                n = N_OD + c
                b = 2 * (n % 2)
                if c < 4:
                    act.wait_ge(gemm_done, n + 1)
                    for m in range(2):
                        t = 2 * c + m
                        last = A(xr[:, t, :], ps[:, b + m, 0:SEQ], ACT.Identity, scale=V("od_w", 24 + t), bias=V("od_b", t))
                    last.then_inc(xc0, 1)
                split_hi(n + 2)
                if c < 4:
                    act.wait_ge(psum_free, n + 1)
                    A(xr_hi[:, 2 * c:2 * c + 2, :], xr[:, 2 * c:2 * c + 2, :], ACT.Copy).then_inc(xc_hi, 1)
                else:
                    act.wait_ge(psum_free, n + 1)
                    g = gate[:, 2 * (c - 4):2 * (c - 4) + 2, :]
                    A(g, g, ACT.Gelu_apprx_tanh).then_inc(gate_act, 1)
            for w, (dst, name, done) in enumerate(((rg_r, "b_a", sig_r), (rg_i, "b_x", sig_i))):
                act.wait_ge(gemm_done, N_RG + w + 1)
                for t in range(KT):
                    last = A(dst[:, t, :], ps[:, 4 * (1 - w) + t // 2, (t % 2) * SEQ:(t % 2 + 1) * SEQ], ACT.Sigmoid,
                             bias=V(name, t))
                last.then_inc(done, 1)
                split_hi(N_RG + w + 2)
            act.wait_ge(lam_c, 1)
            act.wait_ge(sig_r, 1)
            for half in range(2):
                for t in range(4 * half, 4 * half + 4):
                    A(rg_a[:, t, :], rg_r[:, t, :], ACT.Exp, scale=S2[:, 16 + t:17 + t])
                    last = A(rg_t[:, t, :], rg_r[:, t, :], ACT.Tanh, scale=S2[:, 8 + t:9 + t])
                last.then_inc(rg_exp, 1)
            for half in range(2):
                act.wait_ge(rg_s, half + 1)
                a = rg_t[:, 4 * half:4 * half + 4, :]
                A(a, a, ACT.Sqrt).then_inc(rg_sqrt, 1)
            for half in range(2):
                act.wait_ge(rg_y, half + 1)
                A(h_hi[:, 4 * half:4 * half + 4, 0:SEQ], rg_r[:, 4 * half:4 * half + 4, :], ACT.Copy).then_inc(rg_yhi, 1)
            for c in range(4):
                split_hi(N_ODOUT + c + 2)
            norm(8)
            ffn(1)
            norm(9)

        @block.vector
        def _(dve):
            TT, TS, STT, CP = nc.vector.tensor_tensor, nc.vector.tensor_scalar, nc.vector.scalar_tensor_tensor, nc.vector.tensor_copy
            own = Steps(dve, dve_step)

            def same(n):
                return n

            def split_lo(n, at=same):
                if n >= N_CHUNKS:
                    return
                dve.wait_ge(hi_ready, at(n + 1))
                TT(w_lo[:, n % 2, :, :].rearrange("p k n -> p (k n)"), w_raw[:, n % 4, :],
                   w_hi[:, n % 2, :, :].rearrange("p k n -> p (k n)").bitcast(F32), ALU.subtract).then_inc(lo_ready, 1)

            def norm(k, before=None):
                mode, p1, p2, w = NORMS[k]
                nt = w // P
                dve.wait_ge(x_in_s, 16)
                dve.wait_ge(std_ready, k + 1)
                own.step(nc.vector.reciprocal(small[:, S_RS:S_RS + nt], small[:, S_STD:S_STD + nt]))
                own.join()
                TT(diag[:, 0:nt, :], bc(ident, nt), bcl(small[:, S_RS:S_RS + nt], P), ALU.mult).then_inc(diag_ready, 1)
                if before is not None:
                    before()
                dve.wait_ge(rbc_ready, k + 1)
                if mode in ("x", "out"):
                    dst, done = (x, x_final) if mode == "x" else (y_out, out_ready)
                    for t in range(KT):
                        STT(dst[:, t, 0:w], x[:, t, 0:w], V(p1, t), ps[:, 5, 0:w], ALU.mult, ALU.mult).then_inc(done, 1)
                    return
                h0 = KT * H_NORM[k]

                def lo(t):
                    dve.wait_ge(norm_hi, h0 + t + 1)
                    TT(h_lo[:, t, 0:w], h_raw[:, t % 2, 0:w], h_hi[:, t, 0:w].bitcast(F32), ALU.subtract)\
                        .then_inc(h_ready, 1)

                for t in range(KT):
                    if t >= 2:
                        dve.wait_ge(h_ready, h0 + t - 1)
                    if mode == "gain":
                        STT(h_raw[:, t % 2, 0:w], x[:, t, 0:w], V(p1, t), ps[:, 5, 0:w], ALU.mult, ALU.mult)\
                            .then_inc(norm_raw, 1)
                    else:
                        for s in range(w // SEQ):
                            c = slice(s * SEQ, (s + 1) * SEQ)
                            own.step(STT(h_raw[:, t % 2, c], x[:, t, c], mod[:, p1, p2, t, s:s + 1], ps[:, 5, c],
                                         ALU.mult, ALU.mult))
                        own.join()
                        for s in range(w // SEQ):
                            c = slice(s * SEQ, (s + 1) * SEQ)
                            last = TS(h_raw[:, t % 2, c], h_raw[:, t % 2, c], ada[:, p1, 24 * p2 + t, s:s + 1], None, ALU.add)
                        last.then_inc(norm_raw, 1)
                    if t:
                        lo(t - 1)
                lo(KT - 1)

            def ada_out(l, first, count, bank, done=None):
                a = ada[:, l, first:first + count, :]
                ins = TT(a, ps[:, bank, 2 * first:2 * (first + count)].rearrange("p (m s) -> p m s", s=2),
                         bcl(V(f"b_ada{l}", first, count), 2), ALU.add)
                if done is not None:
                    ins.then_inc(done, 1)
                    return
                own.step(ins)
                own.join()

            def ada_mod(l, which):
                own.step(TS(mod[:, l, which, :, :], ada[:, l, 8 + 24 * which:16 + 24 * which, :], 1.0, None, ALU.add))
                own.join()
                return TT(mod[:, l, which, :, :], mod[:, l, which, :, :], bcl(V(("g_mix", "g_mlp")[which] + str(l), 0, 8), 2),
                          ALU.mult)

            def rope(dst, c, b, cos, sin, tmp, width):
                src = ps[:, b:b + 2, 0:SEQ]
                own.join()
                TT(dst[:, 2 * c:2 * c + 2, 0:SEQ], src, bc(cos, 2), ALU.mult)
                for q in range(4):
                    f, t = slice(32 * q, 32 * q + 32), slice(32 * (q ^ 1), 32 * (q ^ 1) + 32)
                    last = TT(tmp[t, :, :], ps[f, b:b + 2, 0:SEQ], bc(sin[f, :], 2), ALU.mult)
                if width > SEQ:
                    last = CP(dst[:, 2 * c:2 * c + 2, SEQ:width], ps[:, b:b + 2, SEQ:width])
                return last

            def rope_add(dst, c, tmp, n):
                dve.wait_ge(psum_free, n + 1)
                d = dst[:, 2 * c:2 * c + 2, 0:SEQ]
                own.step(TT(d, d, tmp[:, :, :], ALU.add))

            def pooling(streams, m0, l):
                todo = [(g, s) for g in range(4) for s in range(streams)]
                for i, (g, s) in enumerate(todo):
                    m = m0 + i
                    dve.wait_ge(po_hi, m + 1)
                    c = slice(s * SEQ, (s + 1) * SEQ)
                    STT(h_lo[:, g, c], ps[:, 2 + m % 2, 0:SEQ], V(f"s_pool{l}", g), h_hi[:, g, c].bitcast(F32),
                        ALU.mult, ALU.subtract).then_inc(po_lo, 1)

            def attention(units, u0, q0, l):
                def maxima(i):
                    u, k0 = u0 + i, units[i][2]
                    dve.wait_ge(scores, u + 1)
                    b, c = 2 + 2 * (u % 3), S_MAX + 2 * (u % 4)
                    own.step(nc.vector.tensor_reduce(small[:, c:c + 2], ps[:, b:b + 2, 0:ALLT - k0], AX_X, ALU.max))
                    own.join()
                    TS(small[:, c:c + 2], small[:, c:c + 2], -0.125, None, ALU.mult).then_inc(nmax, 1)

                def weights(i):
                    u, w = u0 + i, ALLT - units[i][2]
                    dve.wait_ge(exps, u + 1)
                    if u:
                        dve.wait_ge(wgt_ready, u)
                    own.step(nc.vector.reciprocal(small[:, S_R:S_R + 2], small[:, S_Z + 2 * (u % 2):S_Z + 2 * (u % 2) + 2]))
                    own.join()
                    own.step(TT(sm(S_R + 1), sm(S_R + 1), sm(S_NLAM + l), ALU.mult))
                    if i >= 2:
                        dve.wait_ge(wgtT_done, u - 1)
                    own.step(TS(wgt[:, u % 2, 0:w], prob[:, u % 2, 0, 0:w], sm(S_R), None, ALU.mult))
                    own.join()
                    STT(wgt[:, u % 2, 0:w], prob[:, u % 2, 1, 0:w], sm(S_R + 1), wgt[:, u % 2, 0:w], ALU.mult, ALU.add)\
                        .then_inc(wgt_ready, 1)

                def head_norm(q):
                    dve.wait_ge(osq_ready, q + 1)
                    nc.vector.tensor_reduce(small[:, S_OSS:S_OSS + 4], o_sq[:, :].rearrange("p (h d) -> p h d", h=4), AX_X,
                                            ALU.add).then_inc(oss_ready, 1)
                    dve.wait_ge(ostd_ready, q + 1)
                    own.step(nc.vector.reciprocal(small[:, S_ORS:S_ORS + 4], small[:, S_OSTD:S_OSTD + 4]))
                    own.join()
                    if q > q0:
                        dve.wait_ge(oT_done, q)
                    TT(o_n[:, :].rearrange("p (h d) -> p h d", h=4), ps[:, 1, :].rearrange("p (h d) -> p h d", h=4),
                       bcl(small[:, S_ORS:S_ORS + 4], P), ALU.mult).then_inc(on_ready, 1)

                def out_lo(q):
                    dve.wait_ge(ohi_ready, q + 1)
                    qt = units[4 * (q - q0)][0]
                    t = slice(qt * P, (qt + 1) * P)
                    STT(h_lo[:, 4:8, t], ps[:, 0, :].rearrange("p (h t) -> p h t", h=4), sm(S_GS + l),
                        h_hi[:, 4:8, t].bitcast(F32), ALU.mult, ALU.subtract).then_inc(olo_ready, 1)

                maxima(0)
                maxima(1)
                for i in range(len(units)):
                    weights(i)
                    if i + 2 < len(units):
                        maxima(i + 2)
                    if i >= 4 and i % 4 == 0:
                        head_norm(q0 + i // 4 - 1)
                        out_lo(q0 + i // 4 - 1)
                head_norm(q0 + len(units) // 4 - 1)
                out_lo(q0 + len(units) // 4 - 1)

            def gated(n, tile0, l, part, at=same):
                dve.wait_ge(gemm_done, at(n + 1))
                for m in range(2):
                    for s in range(2 - l):
                        c = slice(s * SEQ, (s + 1) * SEQ)
                        t = tile0 + m
                        last = STT(x[:, t, c], ps[:, 2 * (n % 2) + m, c], ada[:, l, part + t, s:s + 1], x[:, t, c],
                                   ALU.mult, ALU.add)
                last.then_inc(psum_free, 1)

            def added(n, tile0, at=same):
                dve.wait_ge(gemm_done, at(n + 1))
                t = slice(tile0, tile0 + 2)
                TT(x[:, t, 0:SEQ], ps[:, 2 * (n % 2):2 * (n % 2) + 2, 0:SEQ], x[:, t, 0:SEQ], ALU.add).then_inc(psum_free, 1)

            dve.wait_ge(vec_in_s, 16)
            dve.wait_ge(cst_in_s, 16)
            for l in range(2):
                last = TT(small[:, S_LAMP + 2 * l:S_LAMP + 2 * l + 2], V(f"lam{l}", 0, 2), V(f"lam{l}", 2, 2), ALU.mult)
            last.then_inc(lam_prod, 1)
            dve.wait_ge(lam_exp, 1)
            for l in range(2):
                own.step(TT(sm(S_NLAM + l), sm(S_LE + 2 * l + 1), sm(S_LE + 2 * l), ALU.subtract))
                own.step(TS(sm(S_GS + l), V(f"g_sub{l}"), 1.0 - LAM_INIT[l], None, ALU.mult))
                own.join()
                own.step(TS(sm(S_NLAM + l), sm(S_NLAM + l), -LAM_INIT[l], None, ALU.add))

            def first_parameters():
                dve.wait_ge(ada_done, 16)
                ada_out(0, 0, 16, 7)
                ada_mod(0, 0).then_inc(ada_read, 1)
                dve.wait_ge(ada_read, 1)

            norm(0, first_parameters)
            split_lo(0)
            split_lo(1)

            for l in range(2):
                cos, sin = C("cos"), C("sin")
                for c in range(8):
                    n = N_WIN[l] + c
                    b = 2 * (n % 2)
                    dve.wait_ge(gemm_done, n + 1)
                    if c < 4:
                        dst = (qT, kT)[c // 2]
                        rope(dst, c % 2, b, cos, sin, rope_tmp, ALLT if l == 0 or c >= 2 else SEQ).then_inc(psum_free, 1)
                        rope_add(dst, c % 2, rope_tmp, n)
                    else:
                        dst = (v_tok, u_tok)[c // 2 - 2]
                        nt = 4 if l == 0 or c < 6 else 2
                        CP(dst[:, 0:nt, (c % 2) * CH:(c % 2 + 1) * CH],
                           ps[:, b:b + nt // 2, :].rearrange("p b (t n) -> p (b t) n", t=2)).then_inc(psum_free, 1)
                    split_lo(n + 2)
                if l == 0:
                    dve.wait_ge(ada_done, 40)
                    ada_out(0, 16, 24, 6, ada_read)
                pooling(2 - l, 8 * l, l)
                if l == 0:
                    attention([(qt, hd, 0 if qt < 2 else SEQ) for qt in range(4) for hd in range(4)], 0, 0, l)
                else:
                    attention([(qt, hd, 0) for qt in range(2) for hd in range(4)], 16, 4, l)
                for c in range(4):
                    gated(N_WOUT[l] + c, 2 * c, l, 16)
                    split_lo(N_WOUT[l] + c + 2)
                if l == 0:
                    dve.wait_ge(ada_done, 48)
                    ada_out(0, 40, 8, 7)
                    own.step(ada_mod(0, 1))
                else:
                    own.step(ada_mod(1, 1))
                own.join()
                norm(2 * l + 1)
                w = ALLT if l == 0 else SEQ
                r0 = 16 * l
                with dve.Fori(0, 4) as it:
                    def at(n):
                        return it * 8 + n
                    for c in range(8):
                        n = N_MLP[l] + c
                        if c < 4:
                            up = it * 4 + (r0 + c + 1)
                            dve.wait_ge(relu_ready, up)
                            if c:
                                dve.wait_ge(g_ready, it * 8 + (G0[f"mlp{l}"] + 2 * c))
                            TT(relu2[:, :, 0:w], relu[:, c % 2, :, 0:w], relu[:, c % 2, :, 0:w], ALU.mult)\
                                .then_inc(psum_free, 1)
                            dve.wait_ge(psum_free, at(n + 1))
                            dve.wait_ge(ghi_ready, up)
                            TT(g_lo[:, 2 * c:2 * c + 2, 0:w], relu2[:, :, 0:w], g_hi[:, 2 * c:2 * c + 2, 0:w].bitcast(F32),
                               ALU.subtract).then_inc(g_ready, 2)
                        else:
                            gated(n, 2 * (c - 4), l, 40, at)
                        split_lo(n + 2, at)
                if l == 0:
                    dve.wait_ge(ada_done, 96)
                    ada_out(1, 0, 48, 6)
                    own.step(ada_mod(1, 0))
                    own.join()
                norm(2 * l + 2)
            norm(5)

            cos, sin = C("cos2"), C("sin2")
            for c in range(12):
                n = N_EV + c
                b = 2 * (n % 2)
                dve.wait_ge(gemm_done, n + 1)
                two = ps[:, b:b + 2, 0:SEQ]
                if c < 4:
                    dst = (aq, ak)[c // 2]
                    rope(dst, c % 2, b, cos, sin, rot_tmp, SEQ).then_inc(psum_free, 1)
                    rope_add(dst, c % 2, rot_tmp, n)
                elif c in (4, 5, 8, 9):
                    dst = av if c < 6 else bv
                    CP(dst[:, :, (c % 2) * CH:(c % 2 + 1) * CH], ps[:, b, :].rearrange("p (t n) -> p t n", t=2))\
                        .then_inc(psum_free, 1)
                elif c == 6:
                    TS(bq[:, :, :], two, 32 ** -0.5, None, ALU.mult).then_inc(psum_free, 1)
                elif c == 7:
                    CP(bk[:, :, :], two).then_inc(psum_free, 1)
                else:
                    CP(bog[:, 2 * (c - 10):2 * (c - 10) + 2, :], two).then_inc(psum_free, 1)
                split_lo(n + 2)

            dve.wait_ge(z_done, 1)
            for g in range(2):
                last = TS(gl_z[:, g, :], ps[:, 5, g * SEQ:(g + 1) * SEQ], V("b_gk", g), None, ALU.add)
            last.then_inc(z_ready, 1)
            dve.wait_ge(l_ready, 1)
            own.step(STT(gl_z[:, :, :], gl_z[:, :, :], 0.0, gl_e[:, :, :], ALU.min, ALU.subtract))
            own.join()
            for g in range(2):
                own.step(nc.vector.tensor_tensor_scan(bcum[:, g, :], gl_z[:, g, :], gl_z[:, g, :], 0.0, ALU.add, ALU.add))
            dve.wait_ge(bog_act, 2)
            for t in range(4):
                own.step(TS(bog[:, t, :], bog[:, t, :], V("g_gla", t), None, ALU.mult))
            own.join()

            for qt in range(2):
                dve.wait_ge(m_scores, qt + 1)
                s4 = ps[:, 4:8, :].rearrange("p b (c x) -> p b c x", c=2)
                dg = s4[:, :, :, qt * P:(qt + 1) * P]
                for b in range(4):
                    d = ps[:, 4 + b, :].rearrange("p (c x) -> p c x", c=2)[:, :, qt * P:(qt + 1) * P]
                    own.step(TT(d, d, bc(causal, 2), ALU.add))
                own.join()
                own.step(nc.vector.tensor_reduce(small[:, S_MAX:S_MAX + 8].rearrange("p (b c) -> p b c", c=2),
                                                 s4[:, :, :, 0:(qt + 1) * P], AX_X, ALU.max))
                own.join()
                TS(small[:, S_MAX:S_MAX + 8], small[:, S_MAX:S_MAX + 8], -0.125, None, ALU.mult).then_inc(m_max, 1)
                dve.wait_ge(m_exp, qt + 1)
                own.step(nc.vector.reciprocal(small[:, S_R:S_R + 8], small[:, S_Z:S_Z + 8]))
                dve.wait_ge(m_pv, qt + 1)
                own.join()
                TT(a_o[:, :].rearrange("p (h d) -> p h d", h=8), ps[:, qt, :].rearrange("p (h d) -> p h d", h=8),
                   bcl(small[:, S_R:S_R + 8], 64), ALU.mult).then_inc(m_o, 1)
                dve.wait_ge(m_hi, qt + 1)
                t = slice(qt * P, (qt + 1) * P)
                TT(h_lo[:, 0:4, t], ps[:, 2 + qt, :].rearrange("p (h t) -> p h t", h=4), h_hi[:, 0:4, t].bitcast(F32),
                   ALU.subtract).then_inc(m_lo, 1)

            dve.wait_ge(glam_in, 16)
            own.step(nc.vector.memset(attn[:, :, :, :, :].rearrange("p a b c t -> p (a b c t)"), 0.0))

            def difference(lv):
                half = 1 << (lv - 1)
                for g in range(2):
                    bb = bcum[:, g, :].rearrange("p (b x) -> p b x", x=2 * half)
                    mid = bb[:, :, half - 1:half].broadcast_to([P, SEQ // (2 * half), 2 * half])
                    last = TT(dec[:, lv % 2, g, :].rearrange("p (b x) -> p b x", x=2 * half), bb, mid, ALU.subtract)
                last.then_inc(l_diff, 1)

            def merge(lv):
                dve.wait_ge(l_scores, lv + 1)
                b0 = 4 * (lv % 2)
                if lv == 8:
                    CP(attnX[:, :, :, :].rearrange("p a g t -> p a (g t)"), ps[:, b0:b0 + 4, 0:2 * P]).then_inc(l_merged, 1)
                    return
                if lv:
                    dve.wait_ge(l_merged, lv)
                nc.vector.copy_predicated(attn[:, :, :, :, :].rearrange("p a b c t -> p (a b c) t"), bc(gmask[:, lv, :], 16),
                                          ps[:, b0:b0 + 4, :].rearrange("p a (b t) -> p (a b) t", t=P)).then_inc(l_merged, 1)

            difference(1)
            own.join()
            for lv in range(1, 9):
                if lv < 8:
                    if lv > 1:
                        dve.wait_ge(l_qk, lv - 1)
                    difference(lv + 1)
                dve.wait_ge(l_dec, lv)
                if lv >= 3:
                    dve.wait_ge(l_scores, lv - 1)
                TT(gq[:, lv % 2, :, :], bq[:, :, :], dec[:, lv % 2, :, :], ALU.mult)
                TT(gk[:, lv % 2, :, :], bk[:, :, :], dec[:, lv % 2, :, :], ALU.mult).then_inc(l_qk, 1)
                merge(lv - 1)
            merge(8)
            for t in range(2):
                dve.wait_ge(b_sqr, t + 1)
                nc.vector.tensor_reduce(small[:, S_OSS:S_OSS + 8], b_sq[:, :].rearrange("p (h d) -> p h d", h=8), AX_X,
                                        ALU.add).then_inc(b_ssr, 1)
                dve.wait_ge(b_stdr, t + 1)
                own.step(nc.vector.reciprocal(small[:, S_ORS:S_ORS + 8], small[:, S_OSTD:S_OSTD + 8]))
                own.join()
                if t:
                    dve.wait_ge(b_oT, t)
                TT(b_o[:, :].rearrange("p (h d) -> p h d", h=8), ps[:, 4 + t, :].rearrange("p (h d) -> p h d", h=8),
                   bcl(small[:, S_ORS:S_ORS + 8], 64), ALU.mult).then_inc(b_on, 1)
            for t in range(2):
                dve.wait_ge(b_oT, t + 1)
                if t:
                    dve.wait_ge(b_lo, t)
                c = slice(t * P, (t + 1) * P)
                TT(b_raw[:, :, :], ps[:, 6 + t, :].rearrange("p (h t) -> p h t", h=4), bog[:, :, c], ALU.mult)\
                    .then_inc(b_rawr, 1)
                dve.wait_ge(b_hi, t + 1)
                TT(h_lo[:, 4:8, c], b_raw[:, :, :], h_hi[:, 4:8, c].bitcast(F32), ALU.subtract).then_inc(b_lo, 1)
            for c in range(4):
                added(N_EVOUT + c, 2 * c)
                split_lo(N_EVOUT + c + 2)
            norm(6)

            def ffn(l):
                def body(it, third):
                    def at(n):
                        return n + 12 * third if it is None else it * 12 + n

                    def pairs(j):
                        return 12 * l + 4 * third + j if it is None else it * 4 + (12 * l + j)

                    def convs(j):
                        return 24 * l + 8 * third + j if it is None else it * 8 + (24 * l + j)

                    v0 = VEC[f"ffn{l}"]
                    cw = vec[:, v0 + 64 * third:v0 + 64 * third + 64] if it is None else vec[:, bass.ds(it * 64 + v0, 64)]
                    CP(conv_w[:, :], cw).then_inc(conv_w_ready, 1)
                    for c in range(12):
                        n = N_FFN[l] + c
                        if c < 8:
                            p = c % 2
                            dve.wait_ge(conv0, convs(c + 1))
                            for back in (1, 2):
                                for m in range(2):
                                    o = 32 * p + 8 * (2 - back) + 2 * (c // 2) + m
                                    y = conv_y[:, p, m, back:SEQ]
                                    last = STT(y, ps[:, 2 * (n % 2) + m, 0:SEQ - back], conv_w[:, o:o + 1], y, ALU.mult, ALU.add)
                                    if back == 1:
                                        own.step(last)
                                if back == 1:
                                    own.join()
                            last.then_inc(psum_free, 1)
                        else:
                            added(n, 2 * (c - 8), at)
                        split_lo(n + 2 if it is not None else n + 2 + 12 * third, at if it is not None else same)
                        if c < 8 and c % 2:
                            dve.wait_ge(gelu_ready, pairs(c // 2 + 1))
                            TT(ffn_p[:, :, :], conv_y[:, 0, :, :], gelu_g[:, :, :], ALU.mult).then_inc(prod_ready, 1)
                            dve.wait_ge(prod_hi, pairs(c // 2 + 1))
                            TT(g_lo[:, c - 1:c + 1, 0:SEQ], ffn_p[:, :, :], g_hi[:, c - 1:c + 1, 0:SEQ].bitcast(F32),
                               ALU.subtract).then_inc(g_ready, 2)
                with dve.Fori(0, 2) as it:
                    own.enter(it, 16)
                    body(it, 0)
                own.leave(2)
                body(None, 2)

            ffn(0)
            norm(7)

            dve.wait_ge(lam_e, 2)
            e_, s_, q_, p_ = S2[:, 0:8], S2[:, 24:32], S2[:, 32:40], S2[:, 40:48]

            def then(ins):
                own.step(ins)
                own.join()

            then(TS(s_, e_, 2.0, None, ALU.add))
            then(nc.vector.reciprocal(s_, s_))
            then(TT(s_, s_, e_, ALU.mult))
            then(TT(q_, s_, s_, ALU.mult))
            then(TS(p_, q_, 1.0 / 17, 1.0 / 15, ALU.mult, ALU.add))
            for k in (13, 11, 9, 7, 5, 3, 1):
                then(TT(p_, p_, q_, ALU.mult))
                then(TS(p_, p_, 1.0 / k, None, ALU.add))
            then(STT(p_, p_, 2.0, s_, ALU.mult, ALU.mult))
            then(TS(q_, V("lam_od", 0, 8), -1.0, 0.0, ALU.mult, ALU.max))
            then(TT(p_, p_, q_, ALU.add))
            then(TS(S2[:, 8:16], p_, 8.0, None, ALU.mult))
            TS(S2[:, 16:24], p_, -8.0, None, ALU.mult).then_inc(lam_c, 1)

            for c in range(8):
                n = N_OD + c
                b = 2 * (n % 2)
                if c < 4:
                    dve.wait_ge(xc0, c + 1)
                    for back in (1, 2, 3):
                        for m in range(2):
                            t = 2 * c + m
                            y = xr[:, t, back:SEQ]
                            last = STT(y, ps[:, b + m, 0:SEQ - back], V("od_w", 8 * (3 - back) + t), y, ALU.mult, ALU.add)
                            if back < 3:
                                own.step(last)
                        if back < 3:
                            own.join()
                    last.then_inc(psum_free, 1)
                else:
                    dve.wait_ge(gemm_done, n + 1)
                    CP(gate[:, 2 * (c - 4):2 * (c - 4) + 2, :], ps[:, b:b + 2, 0:SEQ]).then_inc(psum_free, 1)
                split_lo(n + 2)
                if c < 4:
                    dve.wait_ge(xc_hi, c + 1)
                    t = slice(2 * c, 2 * c + 2)
                    TT(xr_lo[:, t, :], xr[:, t, :], xr_hi[:, t, :].bitcast(F32), ALU.subtract).then_inc(g_ready, 2)
            for w in range(2):
                split_lo(N_RG + w + 2)
            dve.wait_ge(sig_i, 1)
            TT(rg_i[:, :, :], rg_i[:, :, :], xr[:, :, :], ALU.mult).then_inc(psum_free, 2)
            for half in range(2):
                t = slice(4 * half, 4 * half + 4)
                dve.wait_ge(rg_exp, half + 1)
                own.step(TT(rg_r[:, t, :], rg_a[:, t, :], rg_a[:, t, :], ALU.mult))
                own.join()
                STT(rg_t[:, t, :], rg_r[:, t, :], 1.0, rg_t[:, t, :], ALU.add, ALU.mult).then_inc(rg_s, 1)
            dve.wait_ge(gate_act, 4)
            for half in range(2):
                t = slice(4 * half, 4 * half + 4)
                dve.wait_ge(rg_sqrt, half + 1)
                own.step(TT(rg_i[:, t, :], rg_i[:, t, :], rg_t[:, t, :], ALU.mult))
                own.join()
                for k in range(4 * half, 4 * half + 4):
                    own.step(nc.vector.tensor_tensor_scan(rg_t[:, k, :], rg_a[:, k, :], rg_i[:, k, :], 0.0, ALU.mult, ALU.add))
                own.join()
                TT(rg_r[:, t, :], rg_t[:, t, :], gate[:, t, :], ALU.mult).then_inc(rg_y, 1)
            for half in range(2):
                t = slice(4 * half, 4 * half + 4)
                dve.wait_ge(rg_yhi, half + 1)
                TT(h_lo[:, t, 0:SEQ], rg_r[:, t, :], h_hi[:, t, 0:SEQ].bitcast(F32), ALU.subtract).then_inc(rg_ylo, 1)
            for c in range(4):
                added(N_ODOUT + c, 2 * c)
                split_lo(N_ODOUT + c + 2)
            norm(8)
            ffn(1)
            norm(9)


def chunks(w):
    k, c = w.shape
    w = w.reshape(k // D, KT, P, c // CH, CH)
    return w.transpose(3, 0, 2, 1, 4).reshape(-1, P, KT * CH)


def tiles(v):
    return v.reshape(-1, P).T


def constants():
    c = np.zeros((P, C_COLS), np.float32)
    t = np.arange(SEQ)
    inv = (10000.0 ** (-np.arange(0, 32, 2, dtype=np.float32) / np.float32(32))).astype(np.float32)
    ang = np.concatenate([(t // 64).astype(np.float32)[:, None] * inv, (t % 64).astype(np.float32)[:, None] * inv], -1)
    inv2 = (10000.0 ** (-np.arange(32, dtype=np.float32) / np.float32(32))).astype(np.float32)
    ang2 = t.astype(np.float32)[:, None] * inv2
    p = np.arange(P)
    sign = np.where(p // 32 % 2 == 0, 1, -1)[:, None]
    for name, a in (("", ang), ("2", ang2)):
        a = a.astype(np.float64).T[p % 32]
        c[:, CST["cos" + name]:CST["cos" + name] + SEQ] = np.cos(a)
        c[:, CST["sin" + name]:CST["sin" + name] + SEQ] = np.sin(a) * sign
    c[:, CST["ident"]:CST["ident"] + P] = np.eye(P)
    c[:, CST["ones"]:CST["ones"] + P] = 1
    c[:, CST["causal"]:CST["causal"] + P] = np.where(p[None, :] <= p[:, None], 0, -1e30)
    pm = np.zeros((4, SEQ, SEQ))
    for g, w in enumerate((2, 4, 8, 16)):
        for i in range(SEQ):
            lo, hi = max(i - w // 2, 0), min(i + w - w // 2, SEQ)
            pm[g, lo:hi, i] = 1.0 / (hi - lo)
            pm[g, i, i] -= 1.0
    pm = pm.reshape(4, 2, P, SEQ).transpose(2, 1, 0, 3).astype(np.float32)
    gm = np.zeros((P, 8, P), np.int32)
    gm[:, 0] = np.eye(P)
    s_, t_ = p[:, None], p[None, :]
    for lv in range(1, 8):
        h = 1 << (lv - 1)
        gm[:, lv] = (s_ // (2 * h) == t_ // (2 * h)) & (s_ // h % 2 == 0) & (t_ // h % 2 == 1)
    return c, np.ascontiguousarray(pm), gm


def layout(i):
    a = {k: np.asarray(v) for k, v in i.items()}
    two = {k[:-2]: v for k, v in a.items() if k.endswith("_2")}
    parts = []
    for l in range(2):
        w = a["w_in"][l]
        parts.append(chunks(np.concatenate([w[:, 512:], w[:, :512]], 1)))
        parts.append(chunks(a["w_out"][l]))
        up = chunks(a["w_mlp1"][l])
        down = chunks(a["w_mlp2"][l]).reshape(4, 4, P, KT * CH)
        for q in range(4):
            parts += [up[4 * q:4 * q + 4], down[:, q]]

    def ffn(l):
        up = chunks(two["ffn_w_up"][l])
        down = chunks(two["ffn_w_down"][l]).reshape(4, 3, P, KT * CH)
        for q in range(3):
            for j in range(4):
                parts.append(up[[4 * q + j, 12 + 4 * q + j]])
            parts.append(down[:, q])

    w = two["ev_w_in"][0]
    parts.append(chunks(np.concatenate([w[:, :2560], w[:, 2576:]], 1)))
    parts.append(chunks(two["ev_w_out"][0]))
    ffn(0)
    w = two["od_w_in"][0]
    parts.append(chunks(np.concatenate([w[:, D:], w[:, :D]], 1)))
    for k in ("od_w_a", "od_w_x"):
        parts.append(chunks(two[k][0].reshape(D, CH)))
    parts.append(chunks(two["od_w_out"][0]))
    ffn(1)
    stream = np.concatenate(parts, 0)
    assert stream.shape == (N_CHUNKS, P, KT * CH), stream.shape
    ada = a["w_ada"].reshape(2, KT, P, 48, P).transpose(0, 3, 2, 1, 4).reshape(96, P, KT * P)

    def both(u, v):
        return np.stack([tiles(u), tiles(v)], 2).reshape(P, 16)

    def short(v):
        return np.concatenate([v, np.zeros(P - v.shape[0], v.dtype)])[:, None]

    cols = [both(a["c"][0], a["c_ctx"])]
    for l in range(2):
        cols += [tiles(a["g_mix"][l]), tiles(a["g_mlp"][l]), tiles(a["s_pool"][l]), tiles(a["g_subln"][l]),
                 tiles(a["b_ada"][l])] + [short(a[k][l]) for k in ("lam_q1", "lam_q2", "lam_k1", "lam_k2")]
    cols += [tiles(a["g_final"]), tiles(two["mix_norm_g"][0]), tiles(two["mix_norm_g"][1]),
             tiles(two["ffn_norm_g"][0]), tiles(two["ffn_norm_g"][1]), tiles(two["final_norm_g"]),
             tiles(two["ev_b_gk2"][0]), tiles(two["ev_gla_norm_g"][0].reshape(-1)), tiles(two["od_conv_w"][0].reshape(-1)),
             tiles(two["od_conv_b"][0]), tiles(two["od_b_a"][0]), tiles(two["od_b_x"][0]), tiles(two["od_lambda"][0])]
    for l in range(2):
        cw = np.concatenate([two["ffn_conv_w"][l], two["ffn_conv_b"][l][None]], 0)
        cw = cw.reshape(4, 2, 3, 8, P).transpose(4, 2, 1, 0, 3)
        cols.append(cw.reshape(P, 192))
    vec = np.concatenate(cols, 1)
    assert vec.shape == (P, V_COLS), vec.shape
    xs = np.concatenate([a["x"][0], a["ctx"][0]], 0)
    cst, pm, gm = constants()
    return {
        "w_stream": stream, "ada_stream": ada, "x_in": xs.reshape(ALLT, KT, P).transpose(2, 1, 0),
        "vec_in": vec, "cst_in": cst, "pool_mats": pm, "gla_masks": gm,
        "w_pool": a["w_pool"].transpose(2, 0, 1, 3),
        "w_gk": two["ev_w_in"][0][:, 2560:2576].reshape(KT, P, 16).transpose(1, 0, 2),
        "w_gk2": two["ev_w_gk2"][0],
    }


def kernel(**inputs):
    import concourse.bacc as bacc
    from concourse.bass_utils import run_bass_kernel_spmd

    nc = bacc.Bacc("TRN2", target_bir_lowering=False, num_devices=1)
    arrays, args = {}, []
    for name, a in layout(inputs).items():
        a = np.ascontiguousarray(a)
        arrays[f"in_{name}"] = a
        args.append(nc.dram_tensor(f"in_{name}", a.shape, mybir.dt.from_np(a.dtype), kind="ExternalInput").ap())
    out = nc.dram_tensor("out", (P, KT, SEQ), F32, kind="ExternalOutput").ap()
    build_program(nc, *args, out)
    r = run_bass_kernel_spmd(nc, [arrays], core_ids=[0])
    y = r.results[0]["out"]
    return np.ascontiguousarray(np.asarray(y).transpose(2, 1, 0).reshape(1, SEQ, D))
```

```python
import concourse.bass as bass
from concourse import mybir
from contextlib import ExitStack
import math
import numpy as np

F32 = mybir.dt.float32
F32R = mybir.dt.float32r
I32 = mybir.dt.int32
ALU = mybir.AluOpType
ACT = mybir.ActivationFunctionType
AX_X = mybir.AxisListType.X

P = 128
D = 1024
KT = D // P
SEQ = 256
ALLT = 2 * SEQ
EPS = 1e-6
CH = 256
LAM_INIT = [0.8 - 0.6 * math.exp(-0.3 * l) for l in range(2)]

N_WIN = [8, 84]
N_WOUT = [24, 100]
N_MLP = [36, 104]
N_EV, N_EVOUT = 136, 148
N_FFN = [152, 202]
N_OD, N_RG, N_ODOUT = 188, 196, 198
N_CHUNKS = 238

VEC = {}
V_COLS = 0
for _name, _n in (
    [("c", 16)]
    + [(f"{k}{l}", n) for l in range(2) for k, n in
       (("g_mix", 8), ("g_mlp", 8), ("s_pool", 4), ("g_sub", 1), ("b_ada", 48), ("lam", 4))]
    + [("g_final", 8), ("mix_g0", 8), ("mix_g1", 8), ("ffn_g0", 8), ("ffn_g1", 8), ("final_g", 8),
       ("b_gk", 2), ("g_gla", 4), ("od_w", 32), ("od_b", 8), ("b_a", 8), ("b_x", 8), ("lam_od", 8),
       ("ffn0", 192), ("ffn1", 192)]
):
    VEC[_name] = V_COLS
    V_COLS += _n

CST = {"cos": 0, "sin": 256, "cos2": 512, "sin2": 768, "ident": 1024, "ones": 1152, "causal": 1280, "sel": 1408}
C_COLS = 1416


class Steps:

    def __init__(self, eng, sem):
        self.eng, self.sem, self.n, self.loop = eng, sem, 0, None

    def step(self, ins):
        ins.then_inc(self.sem, 1)
        self.n += 1
        return ins

    def join(self):
        self.eng.wait_ge(self.sem, self.n if self.loop is None else self.loop[0] * self.loop[1] + self.n)

    def enter(self, i, per):
        self.loop, self.start = (i, per), self.n

    def leave(self, iters):
        per = self.n - self.start
        assert per == self.loop[1], (per, self.loop[1])
        self.n += per * (iters - 1)
        self.loop = None


def build_program(nc, w_stream, x_in, vec_in, cst_in, pool_mats, gla_masks, w_pool, w_gk, w_gk2,
                  out):
    ctx = ExitStack()
    with ctx:
        base = (nc.sbuf_base + 31) // 32 * 32
        top = [base]

        def place(name, shape, dt=F32, at=None):
            size = 4
            for d in shape[1:]:
                size *= d
            if at is None:
                at = top[0]
                top[0] += size
            return nc.alloc_sbuf_tensor_at(name, shape, dt, offset=at)

        x = place("x", [P, KT, ALLT])
        h_hi = place("h_hi", [P, KT, ALLT], F32R)
        h_lo = place("h_lo", [P, KT, ALLT], F32R)
        g_base = top[0]
        g_hi = place("g_hi", [P, KT, ALLT], F32R)
        g_lo = place("g_lo", [P, KT, ALLT], F32R)
        w_raw = place("w_raw", [P, 4, KT * CH])
        w_hi = place("w_hi", [P, 2, KT, CH], F32R)
        w_lo = place("w_lo", [P, 2, KT, CH], F32R)
        r_base = top[0]
        top[0] += 32768
        acc2 = place("acc2", [P, 2, ALLT])
        a_base = top[0]
        sq = place("sq", [P, 2, 2, ALLT])
        diag = place("diag", [P, 4, P])
        rows = place("rows", [P, 2, CH])
        vec = place("vec", [P, V_COLS])
        cst = place("cst", [P, C_COLS])
        wp = place("wp", [P, 2, 4, P])
        c_act = place("c_act", [P, KT, 2])
        c_st = place("c_st", [P, KT, 4], F32R)
        ada = place("ada", [P, 2, 48, 2])
        mod = place("mod", [P, 2, 2, KT, 2])
        small = place("small", [P, 96])
        assert top[0] <= nc.sbuf_usable_end, top[0]

        KB = 1024
        qT = place("qT", [P, 4, ALLT], at=r_base)
        kT = place("kT", [P, 4, ALLT], at=r_base + 8 * KB)
        v_tok = place("v_tok", [P, 4, 512], at=r_base + 16 * KB)
        u_tok = place("u_tok", [P, 4, 512], at=r_base + 24 * KB)
        h_raw = place("h_raw", [P, 2, ALLT], at=r_base + 18 * KB)
        relu = place("relu", [P, 2, 2, ALLT], at=r_base + 16 * KB)
        relu2 = place("relu2", [P, 2, ALLT], at=r_base + 24 * KB)
        aq = place("aq", [P, 4, SEQ], at=r_base)
        ak = place("ak", [P, 4, SEQ], at=r_base + 4 * KB)
        av = place("av", [P, 2, 512], at=r_base + 8 * KB)
        bq = place("bq", [P, 2, SEQ], at=r_base + 12 * KB)
        bk = place("bk", [P, 2, SEQ], at=r_base + 14 * KB)
        bv = place("bv", [P, 2, 512], at=r_base + 16 * KB)
        bog = place("bog", [P, 4, SEQ], at=r_base + 20 * KB)
        bcum = place("bcum", [P, 2, SEQ], at=r_base + 24 * KB)
        wgk = place("wgk", [P, KT, 16], at=r_base + 26 * KB)
        wgk2 = place("wgk2", [16, SEQ], at=r_base + 26 * KB + 512)
        gkT = place("gkT", [16, SEQ], at=r_base + 26 * KB + 1536)
        rot_tmp = place("rot_tmp", [P, 2, SEQ], at=r_base + 30 * KB)
        conv_y = place("conv_y", [P, 2, 2, SEQ], at=r_base)
        gelu_g = place("gelu_g", [P, 2, SEQ], at=r_base + 4 * KB)
        ffn_p = place("ffn_p", [P, 2, SEQ], at=r_base + 6 * KB)
        conv_w = place("conv_w", [P, 64], at=r_base + 8 * KB)
        gate = place("gate", [P, KT, SEQ], at=r_base)
        xr = place("xr", [P, KT, SEQ], at=r_base + 8 * KB)
        rg_r = place("rg_r", [P, KT, SEQ], at=r_base + 16 * KB)
        rg_i = place("rg_i", [P, KT, SEQ], at=r_base + 24 * KB)
        prob = place("prob", [P, 2, 2, 512], at=g_base)
        wgt = place("wgt", [P, 2, 512], at=g_base + 8 * KB)
        wgtT = place("wgtT", [P, 2, 512], at=g_base + 12 * KB)
        o_sq = place("o_sq", [P, 512], at=g_base + 16 * KB)
        o_n = place("o_n", [P, 512], at=g_base + 18 * KB)
        rope_tmp = place("rope_tmp", [P, 2, SEQ], at=g_base + 20 * KB)
        pool_y = place("pool_y", [P, 2, SEQ], at=g_base + 22 * KB)
        pmat = place("pmat", [P, 2, 4, SEQ], at=g_base + 24 * KB)
        y_out = place("y_out", [P, KT, SEQ], at=g_base)
        a_p = place("a_p", [P, 8, SEQ], at=g_base)
        a_pT = place("a_pT", [P, 2, 8, P], at=g_base + 8 * KB)
        a_o = place("a_o", [P, 512], at=g_base + 16 * KB)
        a_raw = place("a_raw", [P, 4, P], at=g_base + 18 * KB)
        attn = place("attn", [P, 4, 2, 2, P], at=g_base)
        attnX = place("attnX", [P, 4, 2, P], at=g_base + 8 * KB)
        dec = place("dec", [P, 2, 2, SEQ], at=g_base + 16 * KB)
        gq = place("gq", [P, 2, 2, SEQ], at=g_base + 24 * KB)
        gk = place("gk", [P, 2, 2, SEQ], at=g_base + 28 * KB)
        b_o = place("b_o", [P, 512], at=g_base + 20 * KB)
        b_sq = place("b_sq", [P, 512], at=g_base + 22 * KB)
        b_raw = place("b_raw", [P, 4, P], at=g_base + 12 * KB)
        gl_e = place("gl_e", [P, 2, SEQ], at=g_base + 12 * KB)
        gl_z = place("gl_z", [P, 2, SEQ], at=g_base + 14 * KB)
        gmask = place("gmask", [P, 8, P], I32, at=a_base)
        xr_hi = place("xr_hi", [P, KT, SEQ], F32R, at=g_base)
        xr_lo = place("xr_lo", [P, KT, SEQ], F32R, at=g_base + 8 * KB)
        rg_a = place("rg_a", [P, KT, SEQ], at=g_base + 16 * KB)
        rg_t = place("rg_t", [P, KT, SEQ], at=g_base + 24 * KB)

        ps = ctx.enter_context(nc.psum_tensor("ps", [P, 8, 512], F32))

        def sem(name):
            return ctx.enter_context(nc.semaphore(name))

        raw_in = [sem(f"raw_in{i}") for i in range(4)]
        hi_ready, lo_ready, gemm_done, psum_free = sem("hi_ready"), sem("lo_ready"), sem("gemm_done"), sem("psum_free")
        half_hi, half_lo, half_used = sem("half_hi"), sem("half_lo"), sem("half_used")
        c_ready, rows_zero, col_done, ada_ready = sem("c_ready"), sem("rows_zero"), sem("col_done"), sem("ada_ready")
        vec_in_s, cst_in_s, x_in_s = sem("vec_in"), sem("cst_in"), sem("x_in")
        pool_in, glam_in, gk_in = sem("pool_in"), sem("glam_in"), sem("gk_in")
        silu_done = sem("silu_done")
        lam_prod, lam_sum, lam_exp, lam_done = sem("lam_prod"), sem("lam_sum"), sem("lam_exp"), sem("lam_done")
        h_ready, g_ready = sem("h_ready"), sem("g_ready")
        sq_done, sq_used, sq_ready, ss_done, std_ready, diag_ready, rbc_ready = (
            sem("sq_done"), sem("sq_used"), sem("sq_ready"), sem("ss_done"), sem("std_ready"), sem("diag_ready"), sem("rbc_ready"))
        norm_raw, norm_hi, x_final = sem("norm_raw"), sem("norm_hi"), sem("x_final")
        relu_ready, ghi_ready = sem("relu_ready"), sem("ghi_ready")
        py_done, py_copied, po_done, po_hi, po_lo = (
            sem("py_done"), sem("py_copied"), sem("po_done"), sem("po_hi"), sem("po_lo"))
        scores, nmax, exps, wgt_ready, wgtT_done, wgtT_copied, pv_done = (
            sem("scores"), sem("nmax"), sem("exps"), sem("wgt_ready"), sem("wgtT_done"), sem("wgtT_copied"),
            sem("pv_done"))
        osq_ready, oss_ready, ostd_ready, on_ready, oT_done, ohi_ready, olo_ready = (
            sem("osq_ready"), sem("oss_ready"), sem("ostd_ready"), sem("on_ready"), sem("oT_done"),
            sem("ohi_ready"), sem("olo_ready"))
        m_scores, m_max, m_exp, m_T, m_Tc, m_pv, m_o, m_oT, m_raw, m_hi, m_lo = (
            sem("m_scores"), sem("m_max"), sem("m_exp"), sem("m_T"), sem("m_Tc"), sem("m_pv"), sem("m_o"),
            sem("m_oT"), sem("m_raw"), sem("m_hi"), sem("m_lo"))
        gk_done, gk_copied, z_done, z_ready, e_ready, l_ready, b_ready = (
            sem("gk_done"), sem("gk_copied"), sem("z_done"), sem("z_ready"), sem("e_ready"), sem("l_ready"),
            sem("b_ready"))
        l_diff, l_dec, l_qk, l_scores, l_merged, bog_act = (
            sem("l_diff"), sem("l_dec"), sem("l_qk"), sem("l_scores"), sem("l_merged"), sem("bog_act"))
        b_pv, b_sqr, b_ssr, b_stdr, b_on, b_oT, b_rawr, b_hi, b_lo = (
            sem("b_pv"), sem("b_sqr"), sem("b_ssr"), sem("b_stdr"), sem("b_on"), sem("b_oT"), sem("b_rawr"),
            sem("b_hi"), sem("b_lo"))
        conv_w_ready, conv0, gelu_ready, prod_ready, prod_hi = (
            sem("conv_w_ready"), sem("conv0"), sem("gelu_ready"), sem("prod_ready"),
            sem("prod_hi"))
        xc0, xc_hi, gate_act = (
            sem("xc0"), sem("xc_hi"), sem("gate_act"))
        lam_e, lam_c, sig_r, sig_i, rg_exp, rg_s, rg_sqrt, rg_y, rg_yhi, rg_ylo = (
            sem("lam_e"), sem("lam_c"), sem("sig_r"), sem("sig_i"), sem("rg_exp"), sem("rg_s"), sem("rg_sqrt"),
            sem("rg_y"), sem("rg_yhi"), sem("rg_ylo"))
        out_ready, stored = sem("out_ready"), sem("stored")
        eps_set = sem("eps_set")
        act_step, dve_step = sem("act_step"), sem("dve_step")

        def V(name, i=0, n=1):
            return vec[:, VEC[name] + i:VEC[name] + i + n]

        def C(name, n=256):
            return cst[:, CST[name]:CST[name] + n]

        ones, ident, causal = C("ones", P), C("ident", P), C("causal", P)

        def bc(ap, n):
            return ap.rearrange("p (o m) -> p o m", o=1).broadcast_to([ap.shape[0], n, ap.shape[1]])

        def bcl(ap, n):
            return ap.rearrange("p (m o) -> p m o", o=1).broadcast_to([ap.shape[0], ap.shape[1], n])

        S_EPS, S_STD, S_RS, S_MAX, S_Z, S_R, S_NLAM, S_GS = 0, 1, 5, 9, 25, 33, 41, 43
        S_LP, S_LE, S_LAMP, S_OSS, S_OSTD, S_ORS = 45, 49, 53, 61, 69, 77

        def sm(c, n=1):
            return small[:, c:c + n]

        S2 = place("small2", [P, 64])
        assert top[0] <= nc.sbuf_usable_end, top[0]

        NORMS = [("mod", 0, 0, ALLT), ("mod", 0, 1, ALLT), ("mod", 1, 0, ALLT), ("mod", 1, 1, SEQ),
                 ("x", "g_final", None, SEQ), ("gain", "mix_g0", None, SEQ), ("gain", "ffn_g0", None, SEQ),
                 ("gain", "mix_g1", None, SEQ), ("gain", "ffn_g1", None, SEQ), ("out", "final_g", None, SEQ)]
        H_NORM = [0, 1, 2, 3, None, 4, 5, 6, 7, None]
        H0 = {"win0": 0, "mlp0": 8, "win1": 16, "mlp1": 24, "ev": 32, "ffn0": 40, "od": 48, "ffn1": 56}
        G0 = {"mlp0": 0, "mlp1": 32, "ffn0": 64, "od": 88, "ffn1": 96}
        X_AT = [0, 36, 84, 104, 136, 136, 152, 188, 202, 238]

        block = ctx.enter_context(nc.Block())

        @block.sync
        def _(sp):
            sp.dma_start(vec[:, :], vec_in).then_inc(vec_in_s, 16)
            sp.dma_start(x[:, :, :], x_in).then_inc(x_in_s, 16)
            for r in range(4):
                sp.dma_start(w_raw[:, r, :], w_stream[r]).then_inc(raw_in[r], 16)
            with sp.Fori(1, N_CHUNKS // 4) as it:
                for r in range(4):
                    sp.wait_ge(lo_ready, it * 4 + (r - 3))
                    sp.dma_start(w_raw[:, r, :], w_stream[bass.ds(it * 4 + r, 1)].rearrange("a p n -> p (a n)"))\
                        .then_inc(raw_in[r], 16)
            for n in range(N_CHUNKS // 4 * 4, N_CHUNKS):
                sp.wait_ge(lo_ready, n - 3)
                sp.dma_start(w_raw[:, n % 4, :], w_stream[n]).then_inc(raw_in[n % 4], 16)
            sp.wait_ge(out_ready, KT)
            sp.dma_start(out, y_out[:, :, :]).then_inc(stored, 16)
            sp.wait_ge(stored, 16)

        @block.gpsimd
        def _(pool):
            pool.memset(sm(S_EPS), EPS).then_inc(eps_set, 1)
            pool.memset(rows[:, :, :], 0.0).then_inc(rows_zero, 1)
            pool.dma_start(cst[:, :], cst_in).then_inc(cst_in_s, 16)
            pool.dma_start(wp[:, :, :, :], w_pool).then_inc(pool_in, 16)
            pool.dma_start(pmat[:, :, :, :], pool_mats).then_inc(pool_in, 16)
            pool.wait_ge(psum_free, N_WIN[1])
            pool.dma_start(pmat[:, :, :, :], pool_mats).then_inc(pool_in, 16)
            pool.wait_ge(rbc_ready, 6)
            pool.dma_start(gmask[:, :, :], gla_masks).then_inc(glam_in, 16)
            pool.wait_ge(psum_free, N_EV)
            pool.dma_start(wgk[:, :, :], w_gk).then_inc(gk_in, 16)
            pool.dma_start(wgk2[:, :], w_gk2).then_inc(gk_in, 16)

        @block.tensor
        def _(pe):
            mm = nc.tensor.matmul

            def same(n):
                return n

            def start_chunk(n, at):
                pe.wait_ge(half_lo, at(n + 1))
                if n >= 2:
                    pe.wait_ge(psum_free, at(n - 1))

            def gemm_f(n, hi, lo, cols, ready, at=same):
                start_chunk(n, at)
                s = n % 2
                for k in range(KT):
                    if k == KT // 2:
                        pe.wait_ge(lo_ready, at(n + 1))
                    if ready is not None:
                        pe.wait_ge(ready[0], at_of(ready, at)(k + 1))
                    for m in range(2):
                        o = ps[:, 2 * s + m, 0:cols.stop - cols.start]
                        wh, wl = w_hi[:, s, k, m * P:(m + 1) * P], w_lo[:, s, k, m * P:(m + 1) * P]
                        mm(o, wh, hi[:, k, cols], start=(k == 0), stop=False)
                        mm(o, wh, lo[:, k, cols], start=False, stop=False)
                        last = mm(o, wl, hi[:, k, cols], start=False, stop=(k == KT - 1))
                    if k == KT // 2 - 1:
                        last.then_inc(half_used, 1)
                last.then_inc(gemm_done, 1)

            def at_of(ready, at):
                if len(ready) == 2:
                    return lambda k: ready[1] + k
                return lambda k: ready[3] * ready[2] + (ready[1] + k)

            def gemm_t(n, tiles, ready=None):
                start_chunk(n, same)
                if ready is not None:
                    pe.wait_ge(ready[0], ready[1] + KT)
                s = n % 2
                for i in range(tiles):
                    o = ps[:, 2 * s + i // 2, (i % 2) * CH:(i % 2 + 1) * CH]
                    t = slice(i * P, (i + 1) * P)
                    for k in range(KT):
                        if i == 0 and k == KT // 2:
                            pe.wait_ge(lo_ready, n + 1)
                        mm(o, h_hi[:, k, t], w_hi[:, s, k, :], start=(k == 0), stop=False)
                        mm(o, h_lo[:, k, t], w_hi[:, s, k, :], start=False, stop=False)
                        last = mm(o, h_hi[:, k, t], w_lo[:, s, k, :], start=False, stop=(k == KT - 1))
                        if i == tiles - 1 and k == KT // 2 - 1:
                            last.then_inc(half_used, 1)
                last.then_inc(gemm_done, 1)

            def ada_chunk(n, at=same):
                start_chunk(n, at)
                s = n % 2
                for k in range(KT):
                    if k == KT // 2:
                        pe.wait_ge(lo_ready, at(n + 1))
                    for w in (w_hi, w_lo):
                        last = mm(ps[0:4, 2 * s, 0:CH], c_st[:, k, :], w[:, s, k, :], start=(k == 0 and w is w_hi),
                                  stop=(k == KT - 1 and w is w_lo))
                    if k == KT // 2 - 1:
                        last.then_inc(half_used, 1)
                last.then_inc(gemm_done, 1)

            def ada_columns(n, buf=0, at=same):
                pe.wait_ge(psum_free, at(n + 1))
                for half in range(2):
                    last = mm(ps[:, 6, half * 8:half * 8 + 8], rows[:, buf, half * P:(half + 1) * P], cst[:, CST["sel"]:CST["sel"] + 8],
                              start=True, stop=True)
                last.then_inc(col_done, 1)

            def norm(k):
                nt = NORMS[k][3] // P
                pe.wait_ge(sq_ready, k + 1)
                for j in range(nt):
                    last = mm(ps[:, 4, j:j + 1], acc2[:, 0, j * P:(j + 1) * P], ones[:, 0:1], start=True, stop=True)
                last.then_inc(ss_done, 1)
                pe.wait_ge(diag_ready, k + 1)
                mm(ps[:, 5, 0:nt * P], ones, diag[:, 0:nt, :], start=True, stop=True).then_inc(rbc_ready, 1)

            def pooling(streams, m0):
                def mix_out(m, g):
                    pe.wait_ge(py_copied, m + 1)
                    if m - m0 >= 2:
                        pe.wait_ge(po_lo, m - 1)
                    mm(ps[:, 2 + m % 2, 0:SEQ], wp[:, m0 // 8, g, :], pool_y[:, m % 2, :], start=True, stop=True)\
                        .then_inc(po_done, 1)
                todo = [(g, s) for g in range(4) for s in range(streams)]
                for i, (g, s) in enumerate(todo):
                    m = m0 + i
                    if i >= 2:
                        pe.wait_ge(py_copied, m - 1)
                    for t in range(2):
                        last = mm(ps[:, m % 2, 0:SEQ], u_tok[:, 2 * s + t, g * P:(g + 1) * P], pmat[:, t, g, :],
                                  start=(t == 0), stop=(t == 1))
                    last.then_inc(py_done, 1)
                    if i:
                        mix_out(m - 1, todo[i - 1][0])
                mix_out(m0 + len(todo) - 1, todo[-1][0])

            def attention(units, u0, q0):
                def score(i):
                    qt, hd, k0 = units[i]
                    u = u0 + i
                    if i >= 3:
                        pe.wait_ge(exps, u - 2)
                    for a in range(2):
                        r = slice(64 * a, 64 * a + 64)
                        last = mm(ps[:, 2 + 2 * (u % 3) + a, 0:ALLT - k0], qT[r, hd, qt * P:(qt + 1) * P],
                                  kT[r, hd, k0:ALLT], start=True, stop=True)
                    last.then_inc(scores, 1)

                def transposes(i):
                    u, kb = u0 + i, (ALLT - units[i][2]) // P
                    pe.wait_ge(wgt_ready, u + 1)
                    if i:
                        pe.wait_ge(wgtT_copied, u)
                    if i >= 4 and i % 4 == 1:
                        pe.wait_ge(olo_ready, q0 + i // 4)
                    for b in range(kb):
                        last = nc.tensor.transpose(ps[:, 0, b * P:(b + 1) * P], wgt[:, u % 2, b * P:(b + 1) * P], ident)
                    last.then_inc(wgtT_done, 1)

                def values(i):
                    qt, hd, k0 = units[i]
                    u, kb = u0 + i, (ALLT - k0) // P
                    pe.wait_ge(wgtT_copied, u + 1)
                    if hd == 0 and i >= 4:
                        pe.wait_ge(on_ready, q0 + i // 4)
                    for b in range(kb):
                        last = mm(ps[:, 1, hd * P:(hd + 1) * P], wgtT[:, u % 2, b * P:(b + 1) * P],
                                  v_tok[:, k0 // P + b, hd * P:(hd + 1) * P], start=(b == 0), stop=(b == kb - 1))
                    last.then_inc(pv_done, 1)

                def outputs(q):
                    pe.wait_ge(on_ready, q + 1)
                    pe.wait_ge(wgtT_copied, u0 + min(4 * (q - q0 + 1) + 1, len(units)))
                    for hd in range(4):
                        last = nc.tensor.transpose(ps[:, 0, hd * P:(hd + 1) * P], o_n[:, hd * P:(hd + 1) * P], ident)
                    last.then_inc(oT_done, 1)

                for i in range(3):
                    score(i)
                for i in range(len(units)):
                    transposes(i)
                    if i + 3 < len(units):
                        score(i + 3)
                    values(i)
                    if i >= 4 and i % 4 == 0:
                        outputs(q0 + i // 4 - 1)
                outputs(q0 + len(units) // 4 - 1)

            pe.wait_ge(cst_in_s, 16)
            pe.wait_ge(lam_prod, 1)
            mm(ps[:, 6, 0:4], ones, small[:, S_LAMP:S_LAMP + 4], start=True, stop=True).then_inc(lam_sum, 1)
            norm(0)
            pe.wait_ge(c_ready, 1)
            for n in range(8):
                ada_chunk(n)
                if n == 4:
                    ada_columns(3, 0)
            ada_columns(7, 1)

            for l in range(2):
                n0 = N_WIN[l]
                hr = (h_ready, H0[f"win{l}"])
                for c in range(8):
                    n = n0 + 2 * c
                    if c < 4:
                        width = ALLT if l == 0 or c >= 2 else SEQ
                        gemm_f(n, h_hi, h_lo, slice(0, width), hr if c == 0 else None)
                    else:
                        gemm_t(n, 4 if l == 0 or c < 6 else 2)
                    if c == 4:
                        ada_columns(n - 1)
                    ada_chunk(n + 1)
                ada_columns(n0 + 15)
                pe.wait_ge(psum_free, n0 + 16)
                pe.wait_ge(ada_ready, 4 + 8 * l)
                pe.wait_ge(pool_in, 32 + 16 * l)
                pooling(2 - l, 8 * l)
                pe.wait_ge(po_lo, 8 + 4 * l)
                if l == 0:
                    attention([(qt, hd, 0 if qt < 2 else SEQ) for qt in range(4) for hd in range(4)], 0, 0)
                else:
                    attention([(qt, hd, 0) for qt in range(2) for hd in range(4)], 16, 4)
                pe.wait_ge(olo_ready, 4 + 2 * l)
                for c in range(4):
                    n = N_WOUT[l] + (3 - 2 * l) * c
                    gemm_f(n, h_hi, h_lo, slice(0, ALLT if l == 0 else SEQ), None)
                    if l == 0:
                        if c == 2:
                            ada_columns(n - 1)
                        ada_chunk(n + 1)
                        ada_chunk(n + 2)
                if l == 0:
                    ada_columns(N_WOUT[0] + 11)
                norm(2 * l + 1)
                width = slice(0, ALLT if l == 0 else SEQ)
                per = (12, 8)[l]
                with pe.Fori(0, 4) as it:
                    def at(n):
                        return it * per + n
                    for c in range(8):
                        n = N_MLP[l] + (c if l else min(2 * c, c + 4))
                        if c < 4:
                            gemm_f(n, h_hi, h_lo, width, (h_ready, H0[f"mlp{l}"]) if c == 0 else None, at)
                            if l == 0:
                                ada_chunk(n + 1, at)
                        else:
                            gemm_f(n, g_hi, g_lo, width, (g_ready, G0[f"mlp{l}"], 8, it) if c == 4 else None, at)
                            if c == 4 and l == 0:
                                ada_columns(n - 1, 0, at)
                norm(2 * l + 2)
            norm(5)

            for c in range(12):
                n = N_EV + c
                if c in (4, 5, 8, 9):
                    gemm_t(n, 2)
                else:
                    gemm_f(n, h_hi, h_lo, slice(0, SEQ), (h_ready, H0["ev"]) if c == 0 else None)
            pe.wait_ge(gk_in, 32)
            for k in range(KT):
                for part in (h_hi, h_lo):
                    last = mm(ps[0:16, 4, 0:SEQ], wgk[:, k, :], part[:, k, 0:SEQ].bitcast(F32),
                              start=(k == 0 and part is h_hi), stop=(k == KT - 1 and part is h_lo))
            last.then_inc(gk_done, 1)
            pe.wait_ge(gk_copied, 1)
            for g in range(2):
                last = mm(ps[:, 5, g * SEQ:(g + 1) * SEQ], wgk2[:, g * P:(g + 1) * P], gkT[:, :], start=True, stop=True)
            last.then_inc(z_done, 1)
            pe.wait_ge(z_ready, 1)
            pe.wait_ge(psum_free, N_EV + 12)

            for qt in range(2):
                if qt:
                    pe.wait_ge(m_Tc, 1)
                for hd in range(8):
                    r = slice(64 * (hd % 2), 64 * (hd % 2) + 64)
                    c = (hd // 2 % 2) * SEQ
                    last = mm(ps[:, 4 + 2 * (hd // 4) + hd % 2, c:c + (qt + 1) * P], aq[r, hd // 2, qt * P:(qt + 1) * P],
                              ak[r, hd // 2, 0:(qt + 1) * P], start=True, stop=True)
                last.then_inc(m_scores, 1)
                pe.wait_ge(m_exp, qt + 1)
                for kb in range(qt + 1):
                    for hd in range(8):
                        last = nc.tensor.transpose(ps[:, 4 + 2 * kb + hd // 4, hd % 4 * P:(hd % 4 + 1) * P],
                                                   a_p[:, hd, kb * P:(kb + 1) * P], ident)
                last.then_inc(m_T, 1)
                pe.wait_ge(m_Tc, qt + 1)
                for hd in range(8):
                    for kb in range(qt + 1):
                        last = mm(ps[:, qt, hd * 64:(hd + 1) * 64], a_pT[:, kb, hd, :], av[:, kb, hd * 64:(hd + 1) * 64],
                                  start=(kb == 0), stop=(kb == qt))
                last.then_inc(m_pv, 1)
                pe.wait_ge(m_o, qt + 1)
                for i in range(4):
                    last = nc.tensor.transpose(ps[:, 2 + qt, i * P:(i + 1) * P], a_o[:, i * P:(i + 1) * P], ident)
                last.then_inc(m_oT, 1)

            pe.wait_ge(m_lo, 2)
            for lv in range(9):
                kk, qq = (bk, bq) if lv == 0 else (gk[:, lv % 2, :, :], gq[:, lv % 2, :, :])
                if lv:
                    pe.wait_ge(l_qk, lv)
                b0 = 4 * (lv % 2)
                if lv >= 2:
                    pe.wait_ge(l_merged, lv - 1)
                for hd in range(8):
                    r = slice(32 * (hd % 4), 32 * (hd % 4) + 32)
                    g = hd // 4
                    for t in range(2 if lv < 8 else 1):
                        c = (g * 2 + t) * P if lv < 8 else g * P
                        tq = t if lv < 8 else 1
                        last = mm(ps[:, b0 + hd % 4, c:c + P], kk[r, g, t * P:(t + 1) * P],
                                  qq[r, g, tq * P:(tq + 1) * P], start=True, stop=True, tile_position=(32 * (hd % 4), 0))
                last.then_inc(l_scores, 1)
            pe.wait_ge(l_merged, 9)
            for t in range(2):
                for hd in range(8):
                    o = ps[:, 4 + t, hd * 64:(hd + 1) * 64]
                    if t:
                        mm(o, attnX[:, hd % 4, hd // 4, :], bv[:, 0, hd * 64:(hd + 1) * 64], start=True, stop=False)
                    last = mm(o, attn[:, hd % 4, hd // 4, t, :], bv[:, t, hd * 64:(hd + 1) * 64], start=(t == 0), stop=True)
                last.then_inc(b_pv, 1)
            for t in range(2):
                pe.wait_ge(b_on, t + 1)
                for i in range(4):
                    last = nc.tensor.transpose(ps[:, 6 + t, i * P:(i + 1) * P], b_o[:, i * P:(i + 1) * P], ident)
                last.then_inc(b_oT, 1)

            pe.wait_ge(b_lo, 2)
            for c in range(4):
                gemm_f(N_EVOUT + c, h_hi, h_lo, slice(0, SEQ), None)
            norm(6)

            def ffn(l):
                with pe.Fori(0, 3) as it:
                    def at(n):
                        return it * 12 + n
                    for c in range(12):
                        n = N_FFN[l] + c
                        if c < 8:
                            gemm_f(n, h_hi, h_lo, slice(0, SEQ), (h_ready, H0[f"ffn{l}"]) if c == 0 else None, at)
                        else:
                            gemm_f(n, g_hi, g_lo, slice(0, SEQ), (g_ready, G0[f"ffn{l}"], 8, it) if c == 8 else None, at)

            ffn(0)
            norm(7)
            for c in range(8):
                gemm_f(N_OD + c, h_hi, h_lo, slice(0, SEQ), (h_ready, H0["od"]) if c == 0 else None)
            for w in range(2):
                n = N_RG + w
                pe.wait_ge(lo_ready, n + 1)
                if w == 0:
                    pe.wait_ge(g_ready, G0["od"] + KT)
                else:
                    pe.wait_ge(psum_free, N_RG)
                s = n % 2
                for b in range(4):
                    for m in range(2):
                        o = ps[:, 4 * (1 - w) + b, m * SEQ:(m + 1) * SEQ]
                        for kk in range(2):
                            k = 2 * b + kk
                            wh, wl = w_hi[:, s, k, m * P:(m + 1) * P], w_lo[:, s, k, m * P:(m + 1) * P]
                            mm(o, wh, xr_hi[:, k, :], start=(kk == 0), stop=False)
                            mm(o, wh, xr_lo[:, k, :], start=False, stop=False)
                            last = mm(o, wl, xr_hi[:, k, :], start=False, stop=(kk == 1))
                    if b == 1:
                        last.then_inc(half_used, 1)
                last.then_inc(gemm_done, 1)
            pe.wait_ge(rg_ylo, 2)
            for c in range(4):
                gemm_f(N_ODOUT + c, h_hi, h_lo, slice(0, SEQ), None)
            norm(8)
            ffn(1)
            norm(9)

        @block.scalar
        def _(act):
            A = nc.scalar.activation
            own = Steps(act, act_step)

            def same(n):
                return n

            def split_hi(n, at=same, it=None, per=0, parts=(0, 1)):
                if n >= N_CHUNKS:
                    return
                w = 16 * (n // 4 + 1)
                for part in parts:
                    if part == 0:
                        act.wait_ge(raw_in[n % 4], w if it is None else it * (per * 4) + w)
                    if n >= 2:
                        act.wait_ge((half_used, gemm_done)[part], at(n - 1))
                    k = slice(part * KT // 2, (part + 1) * KT // 2)
                    A(w_hi[:, n % 2, k, :].rearrange("p k n -> p (k n)"), w_raw[:, n % 4, k.start * CH:k.stop * CH], ACT.Copy)\
                        .then_inc((half_hi, hi_ready)[part], 1)

            def squares(k, j, n=None):
                w = NORMS[k][3]
                if n is not None:
                    act.wait_ge(psum_free, n + 1)
                if j > 1:
                    act.wait_ge(sq_used, 3 * k + j - 2)
                dst = acc2[:, :, 0:w] if j == 0 else sq[:, j % 2, :, 0:w]
                A(dst, x[:, 2 * j:2 * j + 2, 0:w], ACT.Square).then_inc(sq_done, 1)

            def norm(k):
                w = NORMS[k][3]
                act.wait_ge(ss_done, k + 1)
                A(small[:, S_STD:S_STD + w // P], ps[:, 4, 0:w // P], ACT.Sqrt, bias=sm(S_EPS), scale=1.0 / D)\
                    .then_inc(std_ready, 1)
                if H_NORM[k] is not None:
                    for t in range(KT):
                        n = KT * H_NORM[k] + t
                        act.wait_ge(norm_raw, n + 1)
                        A(h_hi[:, t, 0:w], h_raw[:, t % 2, 0:w], ACT.Copy).then_inc(norm_hi, 1)

            def pooling(streams, m0, l):
                todo = [(g, s) for g in range(4) for s in range(streams)]

                def scaled(m, g, s):
                    act.wait_ge(po_done, m + 1)
                    A(h_hi[:, g, s * SEQ:(s + 1) * SEQ], ps[:, 2 + m % 2, 0:SEQ], ACT.Copy, scale=V(f"s_pool{l}", g))\
                        .then_inc(po_hi, 1)
                for i, (g, s) in enumerate(todo):
                    m = m0 + i
                    act.wait_ge(py_done, m + 1)
                    A(pool_y[:, m % 2, :], ps[:, m % 2, 0:SEQ], ACT.Copy).then_inc(py_copied, 1)
                    if i:
                        scaled(m - 1, *todo[i - 1])
                scaled(m0 + len(todo) - 1, *todo[-1])

            def attention(units, u0, q0, l):
                def exponentials(i):
                    u, w = u0 + i, ALLT - units[i][2]
                    act.wait_ge(nmax, u + 1)
                    if i >= 2:
                        act.wait_ge(wgt_ready, u - 1)
                    for a in range(2):
                        last = A(prob[:, u % 2, a, 0:w], ps[:, 2 + 2 * (u % 3) + a, 0:w], ACT.Exp,
                                 bias=sm(S_MAX + 2 * (u % 4) + a), scale=0.125, accum_out=sm(S_Z + 2 * (u % 2) + a))
                    last.then_inc(exps, 1)

                def copyT(i):
                    u, w = u0 + i, ALLT - units[i][2]
                    act.wait_ge(wgtT_done, u + 1)
                    A(wgtT[:, u % 2, 0:w], ps[:, 0, 0:w], ACT.Copy).then_inc(wgtT_copied, 1)

                def head_norm(q):
                    act.wait_ge(pv_done, u0 + 4 * (q - q0 + 1))
                    A(o_sq[:, :], ps[:, 1, :], ACT.Square).then_inc(osq_ready, 1)
                    act.wait_ge(oss_ready, q + 1)
                    A(small[:, S_OSTD:S_OSTD + 4], small[:, S_OSS:S_OSS + 4], ACT.Sqrt, bias=sm(S_EPS), scale=1.0 / P)\
                        .then_inc(ostd_ready, 1)

                def out_hi(q):
                    act.wait_ge(oT_done, q + 1)
                    qt = units[4 * (q - q0)][0]
                    A(h_hi[:, 4:8, qt * P:(qt + 1) * P], ps[:, 0, :].rearrange("p (h t) -> p h t", h=4), ACT.Copy,
                      scale=small[:, S_GS + l:S_GS + l + 1]).then_inc(ohi_ready, 1)

                exponentials(0)
                for i in range(len(units)):
                    if i + 1 < len(units):
                        exponentials(i + 1)
                    copyT(i)
                    if i >= 3 and i % 4 == 3:
                        head_norm(q0 + i // 4)
                    if i >= 4 and i % 4 == 0:
                        out_hi(q0 + i // 4 - 1)
                out_hi(q0 + len(units) // 4 - 1)

            act.wait_ge(vec_in_s, 16)
            act.wait_ge(eps_set, 1)
            A(c_act[:, :, :].rearrange("p k s -> p (k s)"), V("c", 0, 16), ACT.Silu).then_inc(silu_done, 1)
            act.wait_ge(lam_sum, 1)
            A(sm(S_LE, 4), ps[:, 6, 0:4], ACT.Exp).then_inc(lam_exp, 1)
            act.wait_ge(silu_done, 1)
            A(c_st[:, :, 0:2], c_act[:, :, :], ACT.Copy).then_inc(silu_done, 1)
            act.wait_ge(x_in_s, 16)
            for j in range(4):
                squares(0, j)
            split_hi(0)
            split_hi(1)
            act.wait_ge(ss_done, 1)
            A(small[:, S_STD:S_STD + 4], ps[:, 4, 0:4], ACT.Sqrt, bias=sm(S_EPS), scale=1.0 / D).then_inc(std_ready, 1)
            for n in range(8):
                split_hi(n + 2)
            for t in range(KT):
                act.wait_ge(norm_raw, t + 1)
                A(h_hi[:, t, :], h_raw[:, t % 2, :], ACT.Copy).then_inc(norm_hi, 1)
            for l in range(2):
                for n in range(N_WIN[l], N_WIN[l] + 16):
                    split_hi(n + 2)
                pooling(2 - l, 8 * l, l)
                if l == 0:
                    attention([(qt, hd, 0 if qt < 2 else SEQ) for qt in range(4) for hd in range(4)], 0, 0, l)
                else:
                    attention([(qt, hd, 0) for qt in range(2) for hd in range(4)], 16, 4, l)
                each = 3 - 2 * l
                for c in range(4):
                    n = N_WOUT[l] + each * c
                    split_hi(n + 2, parts=(0,))
                    squares(2 * l + 1, c, n)
                    split_hi(n + 2, parts=(1,))
                    for m in range(1, each):
                        split_hi(n + m + 2)
                norm(2 * l + 1)
                w = ALLT if l == 0 else SEQ
                per = (12, 8)[l]

                def quarter(it, q):
                    def at(n):
                        return n + per * q if it is None else it * per + n

                    for c in range(8):
                        n = N_MLP[l] + (c if l else min(2 * c, c + 4))

                        def split(m, parts):
                            if it is None:
                                split_hi(n + m + 2 + per * q, parts=parts)
                            else:
                                split_hi(n + m + 2, at, it, per, parts)

                        split(0, (0,))
                        if c < 4:
                            up = 16 * l + 4 * q + c + 1 if it is None else it * 4 + (16 * l + c + 1)
                            act.wait_ge(gemm_done, at(n + 1))
                            A(relu[:, c % 2, :, 0:w], ps[:, 2 * (n % 2):2 * (n % 2) + 2, 0:w], ACT.Relu)\
                                .then_inc(relu_ready, 1)
                            act.wait_ge(relu_ready, up)
                            A(g_hi[:, 2 * c:2 * c + 2, 0:w], relu[:, c % 2, :, 0:w], ACT.Square).then_inc(ghi_ready, 1)
                        elif it is None:
                            squares(2 * l + 2, c - 4, n + per * q)
                        split(0, (1,))
                        if c < 4 and l == 0:
                            split(1, (0, 1))

                with act.Fori(0, 3) as it:
                    quarter(it, 0)
                quarter(None, 3)
                norm(2 * l + 2)
            for j in range(4):
                if j == 0:
                    act.wait_ge(x_final, KT)
                squares(5, j)
            norm(5)

            for c in range(12):
                split_hi(N_EV + c + 2, parts=(0,))
                if c >= 10:
                    act.wait_ge(psum_free, N_EV + c + 1)
                    b = bog[:, 2 * (c - 10):2 * (c - 10) + 2, :]
                    A(b, b, ACT.Silu).then_inc(bog_act, 1)
                split_hi(N_EV + c + 2, parts=(1,))
            act.wait_ge(gk_done, 1)
            A(gkT[:, :], ps[0:16, 4, 0:SEQ], ACT.Copy).then_inc(gk_copied, 1)
            act.wait_ge(z_ready, 1)
            A(gl_e[:, :, :], gl_z[:, :, :], ACT.Abs).then_inc(e_ready, 1)
            act.wait_ge(e_ready, 1)
            A(gl_e[:, :, :], gl_e[:, :, :], ACT.Exp, scale=-1.0).then_inc(e_ready, 1)
            act.wait_ge(e_ready, 2)
            A(gl_e[:, :, :], gl_e[:, :, :], ACT.Ln, bias=1.0).then_inc(l_ready, 1)

            for qt in range(2):
                act.wait_ge(m_max, qt + 1)
                for hd in range(8):
                    s_i = (2 * (hd // 4) + hd % 2) * 2 + hd // 2 % 2
                    c = (hd // 2 % 2) * SEQ
                    last = A(a_p[:, hd, 0:(qt + 1) * P], ps[:, 4 + 2 * (hd // 4) + hd % 2, c:c + (qt + 1) * P], ACT.Exp,
                             bias=sm(S_MAX + s_i), scale=0.125, accum_out=sm(S_Z + hd))
                last.then_inc(m_exp, 1)
                act.wait_ge(m_T, qt + 1)
                A(a_pT[:, 0:qt + 1, :, :].rearrange("p k h t -> p (k h t)"),
                  ps[:, 4:4 + 2 * (qt + 1), :].rearrange("p b c -> p (b c)"), ACT.Copy).then_inc(m_Tc, 1)
                act.wait_ge(m_oT, qt + 1)
                A(h_hi[:, 0:4, qt * P:(qt + 1) * P], ps[:, 2 + qt, :].rearrange("p (h t) -> p h t", h=4), ACT.Copy)\
                    .then_inc(m_hi, 1)

            for lv in range(1, 9):
                act.wait_ge(l_diff, lv)
                d = dec[:, lv % 2, :, :]
                own.step(A(d, d, ACT.Abs))
                own.join()
                A(d, d, ACT.Exp, scale=-1.0 / 32).then_inc(l_dec, 1)
            for t in range(2):
                act.wait_ge(b_pv, t + 1)
                if t:
                    act.wait_ge(b_ssr, 1)
                A(b_sq[:, :], ps[:, 4 + t, :], ACT.Square).then_inc(b_sqr, 1)
                act.wait_ge(b_ssr, t + 1)
                A(small[:, S_OSTD:S_OSTD + 8], small[:, S_OSS:S_OSS + 8], ACT.Sqrt, bias=sm(S_EPS), scale=1.0 / 64)\
                    .then_inc(b_stdr, 1)
            for t in range(2):
                act.wait_ge(b_rawr, t + 1)
                A(h_hi[:, 4:8, t * P:(t + 1) * P], b_raw[:, :, :], ACT.Copy).then_inc(b_hi, 1)
            for c in range(4):
                split_hi(N_EVOUT + c + 2, parts=(0,))
                squares(6, c, N_EVOUT + c)
                split_hi(N_EVOUT + c + 2, parts=(1,))
            norm(6)

            def ffn(l):
                def body(it, third):
                    def at(n):
                        return n + 12 * third if it is None else it * 12 + n

                    def pairs(j):
                        return 12 * l + 4 * third + j if it is None else it * 4 + (12 * l + j)

                    act.wait_ge(conv_w_ready, 3 * l + third + 1 if it is None else it + (3 * l + 1))
                    for c in range(12):
                        n = N_FFN[l] + c

                        def split(parts):
                            if it is None:
                                split_hi(n + 2 + 12 * third, parts=parts)
                            else:
                                split_hi(n + 2, at, it, 12, parts)

                        split((0,))
                        if c < 8:
                            p = c % 2
                            act.wait_ge(gemm_done, at(n + 1))
                            for m in range(2):
                                o = 32 * p + 2 * (c // 2) + m
                                last = A(conv_y[:, p, m, :], ps[:, 2 * (n % 2) + m, 0:SEQ], ACT.Identity,
                                         scale=conv_w[:, o + 16:o + 17], bias=conv_w[:, o + 24:o + 25])
                            last.then_inc(conv0, 1)
                        elif it is None:
                            squares(7 + 2 * l, c - 8, n + 12 * third)
                        split((1,))
                        if c < 8 and c % 2:
                            act.wait_ge(psum_free, at(n + 1))
                            A(gelu_g[:, :, :], conv_y[:, 1, :, :], ACT.Gelu_apprx_tanh).then_inc(gelu_ready, 1)
                            act.wait_ge(prod_ready, pairs(c // 2 + 1))
                            A(g_hi[:, c - 1:c + 1, 0:SEQ], ffn_p[:, :, :], ACT.Copy).then_inc(prod_hi, 1)
                with act.Fori(0, 2) as it:
                    body(it, 0)
                body(None, 2)

            ffn(0)
            norm(7)
            A(S2[:, 0:8], V("lam_od", 0, 8), ACT.Abs).then_inc(lam_e, 1)
            act.wait_ge(lam_e, 1)
            A(S2[:, 0:8], S2[:, 0:8], ACT.Exp, scale=-1.0).then_inc(lam_e, 1)
            for c in range(8):
                n = N_OD + c
                b = 2 * (n % 2)
                split_hi(n + 2, parts=(0,))
                if c < 4:
                    act.wait_ge(gemm_done, n + 1)
                    for m in range(2):
                        t = 2 * c + m
                        last = A(xr[:, t, :], ps[:, b + m, 0:SEQ], ACT.Identity, scale=V("od_w", 24 + t), bias=V("od_b", t))
                    last.then_inc(xc0, 1)
                split_hi(n + 2, parts=(1,))
                if c < 4:
                    act.wait_ge(psum_free, n + 1)
                    A(xr_hi[:, 2 * c:2 * c + 2, :], xr[:, 2 * c:2 * c + 2, :], ACT.Copy).then_inc(xc_hi, 1)
                else:
                    act.wait_ge(psum_free, n + 1)
                    g = gate[:, 2 * (c - 4):2 * (c - 4) + 2, :]
                    A(g, g, ACT.Gelu_apprx_tanh).then_inc(gate_act, 1)
            for w, (dst, name, done) in enumerate(((rg_r, "b_a", sig_r), (rg_i, "b_x", sig_i))):
                act.wait_ge(gemm_done, N_RG + w + 1)
                for t in range(KT):
                    last = A(dst[:, t, :], ps[:, 4 * (1 - w) + t // 2, (t % 2) * SEQ:(t % 2 + 1) * SEQ], ACT.Sigmoid,
                             bias=V(name, t))
                last.then_inc(done, 1)
                split_hi(N_RG + w + 2)
            act.wait_ge(lam_c, 1)
            act.wait_ge(sig_r, 1)
            for half in range(2):
                for t in range(4 * half, 4 * half + 4):
                    A(rg_a[:, t, :], rg_r[:, t, :], ACT.Exp, scale=S2[:, 16 + t:17 + t])
                    last = A(rg_t[:, t, :], rg_r[:, t, :], ACT.Tanh, scale=S2[:, 8 + t:9 + t])
                last.then_inc(rg_exp, 1)
            for half in range(2):
                act.wait_ge(rg_s, half + 1)
                a = rg_t[:, 4 * half:4 * half + 4, :]
                A(a, a, ACT.Sqrt).then_inc(rg_sqrt, 1)
            for half in range(2):
                act.wait_ge(rg_y, half + 1)
                A(h_hi[:, 4 * half:4 * half + 4, 0:SEQ], rg_r[:, 4 * half:4 * half + 4, :], ACT.Copy).then_inc(rg_yhi, 1)
            for c in range(4):
                split_hi(N_ODOUT + c + 2, parts=(0,))
                squares(8, c, N_ODOUT + c)
                split_hi(N_ODOUT + c + 2, parts=(1,))
            norm(8)
            ffn(1)
            norm(9)

        @block.vector
        def _(dve):
            TT, TS, STT, CP = nc.vector.tensor_tensor, nc.vector.tensor_scalar, nc.vector.scalar_tensor_tensor, nc.vector.tensor_copy
            own = Steps(dve, dve_step)

            def same(n):
                return n

            def split_lo(n, at=same, parts=(0, 1)):
                if n >= N_CHUNKS:
                    return
                for part in parts:
                    dve.wait_ge((half_hi, hi_ready)[part], at(n + 1))
                    k = slice(part * KT // 2, (part + 1) * KT // 2)
                    TT(w_lo[:, n % 2, k, :].rearrange("p k n -> p (k n)"), w_raw[:, n % 4, k.start * CH:k.stop * CH],
                       w_hi[:, n % 2, k, :].rearrange("p k n -> p (k n)").bitcast(F32), ALU.subtract)\
                        .then_inc((half_lo, lo_ready)[part], 1)

            def add_squares(k, j):
                w = NORMS[k][3]
                dve.wait_ge(sq_done, 4 * k + j + 1)
                if j > 1:
                    dve.wait_ge(sq_used, 3 * k + j - 1)
                TT(acc2[:, :, 0:w], acc2[:, :, 0:w], sq[:, j % 2, :, 0:w], ALU.add).then_inc(sq_used, 1)
                if j == 3:
                    dve.wait_ge(sq_used, 3 * k + 3)
                    TT(acc2[:, 0, 0:w], acc2[:, 0, 0:w], acc2[:, 1, 0:w], ALU.add).then_inc(sq_ready, 1)

            def norm(k, before=None):
                mode, p1, p2, w = NORMS[k]
                nt = w // P
                dve.wait_ge(std_ready, k + 1)
                own.step(nc.vector.reciprocal(small[:, S_RS:S_RS + nt], small[:, S_STD:S_STD + nt]))
                own.join()
                TT(diag[:, 0:nt, :], bc(ident, nt), bcl(small[:, S_RS:S_RS + nt], P), ALU.mult).then_inc(diag_ready, 1)
                if before is not None:
                    before()
                dve.wait_ge(rbc_ready, k + 1)
                if mode in ("x", "out"):
                    dst, done = (x, x_final) if mode == "x" else (y_out, out_ready)
                    for t in range(KT):
                        STT(dst[:, t, 0:w], x[:, t, 0:w], V(p1, t), ps[:, 5, 0:w], ALU.mult, ALU.mult).then_inc(done, 1)
                    return
                h0 = KT * H_NORM[k]

                def lo(t):
                    dve.wait_ge(norm_hi, h0 + t + 1)
                    TT(h_lo[:, t, 0:w], h_raw[:, t % 2, 0:w], h_hi[:, t, 0:w].bitcast(F32), ALU.subtract)\
                        .then_inc(h_ready, 1)

                for t in range(KT):
                    if t >= 2:
                        dve.wait_ge(h_ready, h0 + t - 1)
                    if mode == "gain":
                        STT(h_raw[:, t % 2, 0:w], x[:, t, 0:w], V(p1, t), ps[:, 5, 0:w], ALU.mult, ALU.mult)\
                            .then_inc(norm_raw, 1)
                    else:
                        for s in range(w // SEQ):
                            c = slice(s * SEQ, (s + 1) * SEQ)
                            own.step(STT(h_raw[:, t % 2, c], x[:, t, c], mod[:, p1, p2, t, s:s + 1], ps[:, 5, c],
                                         ALU.mult, ALU.mult))
                        own.join()
                        for s in range(w // SEQ):
                            c = slice(s * SEQ, (s + 1) * SEQ)
                            last = TS(h_raw[:, t % 2, c], h_raw[:, t % 2, c], ada[:, p1, 24 * p2 + t, s:s + 1], None, ALU.add)
                        last.then_inc(norm_raw, 1)
                    if t:
                        lo(t - 1)
                lo(KT - 1)

            def ada_rows(n, i, buf=0, at=same):
                dve.wait_ge(gemm_done, at(n + 1))
                CP(rows[32 * i:32 * i + 4, buf, :], ps[0:4, 2 * (n % 2), 0:CH]).then_inc(psum_free, 1)

            def ada_columns(l, v, count, at=None):
                dve.wait_ge(col_done, count)
                dst = ada[:, l, 8 * v:8 * v + 8, :] if at is None else \
                    ada[:, l, bass.ds(at, 8), :]
                b0 = VEC[f"b_ada{l}"]
                bias = vec[:, b0 + 8 * v:b0 + 8 * v + 8] if at is None else vec[:, bass.ds(at + b0, 8)]
                src = ps[:, 6, 0:16].rearrange("p (h i s) -> p h i s", h=2, i=4)
                for half in range(2):
                    d = dst.rearrange("p (i h) s -> p h i s", h=2)[:, half, :, :]
                    b = bias.rearrange("p (i h) -> p h i", h=2)[:, half, :]
                    last = TT(d, src[:, half, :, :], bcl(b, 2), ALU.add)
                last.then_inc(ada_ready, 1)

            def ada_mod(l, which):
                own.step(TS(mod[:, l, which, :, :], ada[:, l, 8 + 24 * which:16 + 24 * which, :], 1.0, None, ALU.add))
                own.join()
                return TT(mod[:, l, which, :, :], mod[:, l, which, :, :], bcl(V(("g_mix", "g_mlp")[which] + str(l), 0, 8), 2),
                          ALU.mult)

            def rope(dst, c, b, cos, sin, tmp, width):
                src = ps[:, b:b + 2, 0:SEQ]
                own.join()
                TT(dst[:, 2 * c:2 * c + 2, 0:SEQ], src, bc(cos, 2), ALU.mult)
                for q in range(4):
                    f, t = slice(32 * q, 32 * q + 32), slice(32 * (q ^ 1), 32 * (q ^ 1) + 32)
                    last = TT(tmp[t, :, :], ps[f, b:b + 2, 0:SEQ], bc(sin[f, :], 2), ALU.mult)
                if width > SEQ:
                    last = CP(dst[:, 2 * c:2 * c + 2, SEQ:width], ps[:, b:b + 2, SEQ:width])
                return last

            def rope_add(dst, c, tmp, n):
                dve.wait_ge(psum_free, n + 1)
                d = dst[:, 2 * c:2 * c + 2, 0:SEQ]
                own.step(TT(d, d, tmp[:, :, :], ALU.add))

            def pooling(streams, m0, l):
                todo = [(g, s) for g in range(4) for s in range(streams)]
                for i, (g, s) in enumerate(todo):
                    m = m0 + i
                    dve.wait_ge(po_hi, m + 1)
                    c = slice(s * SEQ, (s + 1) * SEQ)
                    STT(h_lo[:, g, c], ps[:, 2 + m % 2, 0:SEQ], V(f"s_pool{l}", g), h_hi[:, g, c].bitcast(F32),
                        ALU.mult, ALU.subtract).then_inc(po_lo, 1)

            def attention(units, u0, q0, l):
                def maxima(i):
                    u, k0 = u0 + i, units[i][2]
                    dve.wait_ge(scores, u + 1)
                    b, c = 2 + 2 * (u % 3), S_MAX + 2 * (u % 4)
                    own.step(nc.vector.tensor_reduce(small[:, c:c + 2], ps[:, b:b + 2, 0:ALLT - k0], AX_X, ALU.max))
                    own.join()
                    TS(small[:, c:c + 2], small[:, c:c + 2], -0.125, None, ALU.mult).then_inc(nmax, 1)

                def weights(i):
                    u, w = u0 + i, ALLT - units[i][2]
                    dve.wait_ge(exps, u + 1)
                    if u:
                        dve.wait_ge(wgt_ready, u)
                    own.step(nc.vector.reciprocal(small[:, S_R:S_R + 2], small[:, S_Z + 2 * (u % 2):S_Z + 2 * (u % 2) + 2]))
                    own.join()
                    own.step(TT(sm(S_R + 1), sm(S_R + 1), sm(S_NLAM + l), ALU.mult))
                    if i >= 2:
                        dve.wait_ge(wgtT_done, u - 1)
                    own.step(TS(wgt[:, u % 2, 0:w], prob[:, u % 2, 0, 0:w], sm(S_R), None, ALU.mult))
                    own.join()
                    STT(wgt[:, u % 2, 0:w], prob[:, u % 2, 1, 0:w], sm(S_R + 1), wgt[:, u % 2, 0:w], ALU.mult, ALU.add)\
                        .then_inc(wgt_ready, 1)

                def head_norm(q):
                    dve.wait_ge(osq_ready, q + 1)
                    nc.vector.tensor_reduce(small[:, S_OSS:S_OSS + 4], o_sq[:, :].rearrange("p (h d) -> p h d", h=4), AX_X,
                                            ALU.add).then_inc(oss_ready, 1)
                    dve.wait_ge(ostd_ready, q + 1)
                    own.step(nc.vector.reciprocal(small[:, S_ORS:S_ORS + 4], small[:, S_OSTD:S_OSTD + 4]))
                    own.join()
                    if q > q0:
                        dve.wait_ge(oT_done, q)
                    TT(o_n[:, :].rearrange("p (h d) -> p h d", h=4), ps[:, 1, :].rearrange("p (h d) -> p h d", h=4),
                       bcl(small[:, S_ORS:S_ORS + 4], P), ALU.mult).then_inc(on_ready, 1)

                def out_lo(q):
                    dve.wait_ge(ohi_ready, q + 1)
                    qt = units[4 * (q - q0)][0]
                    t = slice(qt * P, (qt + 1) * P)
                    STT(h_lo[:, 4:8, t], ps[:, 0, :].rearrange("p (h t) -> p h t", h=4), sm(S_GS + l),
                        h_hi[:, 4:8, t].bitcast(F32), ALU.mult, ALU.subtract).then_inc(olo_ready, 1)

                maxima(0)
                maxima(1)
                for i in range(len(units)):
                    weights(i)
                    if i + 2 < len(units):
                        maxima(i + 2)
                    if i >= 4 and i % 4 == 0:
                        head_norm(q0 + i // 4 - 1)
                        out_lo(q0 + i // 4 - 1)
                head_norm(q0 + len(units) // 4 - 1)
                out_lo(q0 + len(units) // 4 - 1)

            def gated(n, tile0, l, part, at=same):
                dve.wait_ge(gemm_done, at(n + 1))
                for m in range(2):
                    for s in range(2 - l):
                        c = slice(s * SEQ, (s + 1) * SEQ)
                        t = tile0 + m
                        last = STT(x[:, t, c], ps[:, 2 * (n % 2) + m, c], ada[:, l, part + t, s:s + 1], x[:, t, c],
                                   ALU.mult, ALU.add)
                last.then_inc(psum_free, 1)

            def added(n, tile0, at=same):
                dve.wait_ge(gemm_done, at(n + 1))
                t = slice(tile0, tile0 + 2)
                TT(x[:, t, 0:SEQ], ps[:, 2 * (n % 2):2 * (n % 2) + 2, 0:SEQ], x[:, t, 0:SEQ], ALU.add).then_inc(psum_free, 1)

            dve.wait_ge(vec_in_s, 16)
            dve.wait_ge(cst_in_s, 16)
            for l in range(2):
                last = TT(small[:, S_LAMP + 2 * l:S_LAMP + 2 * l + 2], V(f"lam{l}", 0, 2), V(f"lam{l}", 2, 2), ALU.mult)
            last.then_inc(lam_prod, 1)
            dve.wait_ge(lam_exp, 1)
            for l in range(2):
                own.step(TT(sm(S_NLAM + l), sm(S_LE + 2 * l + 1), sm(S_LE + 2 * l), ALU.subtract))
                own.step(TS(sm(S_GS + l), V(f"g_sub{l}"), 1.0 - LAM_INIT[l], None, ALU.mult))
                own.join()
                own.step(TS(sm(S_NLAM + l), sm(S_NLAM + l), -LAM_INIT[l], None, ALU.add))

            dve.wait_ge(silu_done, 2)
            TT(c_st[:, :, 2:4], c_act[:, :, :], c_st[:, :, 0:2].bitcast(F32), ALU.subtract).then_inc(c_ready, 1)
            for j in range(1, 4):
                add_squares(0, j)

            def first_parameters():
                split_lo(0)
                split_lo(1)
                for n in range(8):
                    ada_rows(n, n % 4, n // 4)
                    split_lo(n + 2)
                    if n == 4:
                        ada_columns(0, 0, 1)
                ada_columns(0, 1, 2)
                dve.wait_ge(ada_ready, 2)
                own.step(ada_mod(0, 0))
                own.join()

            dve.wait_ge(rows_zero, 1)
            norm(0, first_parameters)

            for l in range(2):
                cos, sin = C("cos"), C("sin")
                for c in range(8):
                    n = N_WIN[l] + 2 * c
                    b = 2 * (n % 2)
                    split_lo(n + 2, parts=(0,))
                    dve.wait_ge(gemm_done, n + 1)
                    if c < 4:
                        dst = (qT, kT)[c // 2]
                        rope(dst, c % 2, b, cos, sin, rope_tmp, ALLT if l == 0 or c >= 2 else SEQ).then_inc(psum_free, 1)
                        rope_add(dst, c % 2, rope_tmp, n)
                    else:
                        dst = (v_tok, u_tok)[c // 2 - 2]
                        nt = 4 if l == 0 or c < 6 else 2
                        CP(dst[:, 0:nt, (c % 2) * CH:(c % 2 + 1) * CH],
                           ps[:, b:b + nt // 2, :].rearrange("p b (t n) -> p (b t) n", t=2)).then_inc(psum_free, 1)
                    split_lo(n + 2, parts=(1,))
                    if c == 4:
                        ada_columns(l, 2 + 2 * l, 3 + 8 * l)
                    ada_rows(n + 1, c % 4)
                    split_lo(n + 3)
                ada_columns(l, 3 + 2 * l, 4 + 8 * l)
                pooling(2 - l, 8 * l, l)
                if l == 0:
                    attention([(qt, hd, 0 if qt < 2 else SEQ) for qt in range(4) for hd in range(4)], 0, 0, l)
                else:
                    attention([(qt, hd, 0) for qt in range(2) for hd in range(4)], 16, 4, l)
                each = 3 - 2 * l
                for c in range(4):
                    n = N_WOUT[l] + each * c
                    split_lo(n + 2, parts=(0,))
                    gated(n, 2 * c, l, 16)
                    split_lo(n + 2, parts=(1,))
                    if l == 0:
                        if c == 2:
                            ada_columns(0, 4, 5)
                        for m in (1, 2):
                            ada_rows(n + m, (2 * c + m - 1) % 4)
                            split_lo(n + m + 2)
                    if c:
                        add_squares(2 * l + 1, c)
                if l == 0:
                    ada_columns(0, 5, 6)
                dve.wait_ge(ada_ready, 6 + 6 * l)

                def mlp_gain():
                    own.step(ada_mod(l, 1))
                    own.join()

                norm(2 * l + 1, mlp_gain)
                w = ALLT if l == 0 else SEQ
                per = (12, 8)[l]

                def quarter(it, q):
                    def at(n):
                        return n + per * q if it is None else it * per + n

                    for c in range(8):
                        n = N_MLP[l] + (c if l else min(2 * c, c + 4))
                        m = n + 2 if it is not None else n + 2 + per * q
                        split_lo(m, at if it is not None else same, (0,))
                        if c < 4:
                            up = 16 * l + 4 * q + c + 1 if it is None else it * 4 + (16 * l + c + 1)
                            dve.wait_ge(relu_ready, up)
                            if c:
                                g0 = G0[f"mlp{l}"] + 2 * c
                                dve.wait_ge(g_ready, g0 + 8 * q if it is None else it * 8 + g0)
                            TT(relu2[:, :, 0:w], relu[:, c % 2, :, 0:w], relu[:, c % 2, :, 0:w], ALU.mult)\
                                .then_inc(psum_free, 1)
                            dve.wait_ge(psum_free, at(n + 1))
                            dve.wait_ge(ghi_ready, up)
                            TT(g_lo[:, 2 * c:2 * c + 2, 0:w], relu2[:, :, 0:w], g_hi[:, 2 * c:2 * c + 2, 0:w].bitcast(F32),
                               ALU.subtract).then_inc(g_ready, 2)
                        else:
                            gated(n, 2 * (c - 4), l, 40, at)
                        split_lo(m, at if it is not None else same, (1,))
                        if c < 4 and l == 0:
                            ada_rows(n + 1, c, 0, at)
                            split_lo(m + 1, at if it is not None else same)
                        if c == 4 and l == 0:
                            if it is None:
                                ada_columns(1, q, 7 + q)
                            else:
                                ada_columns(1, 0, it + 7, it * 8)
                        if it is None and c > 4:
                            add_squares(2 * l + 2, c - 4)

                with dve.Fori(0, 3) as it:
                    quarter(it, 0)
                quarter(None, 3)

                def mixer_gain():
                    dve.wait_ge(ada_ready, 10)
                    own.step(ada_mod(1, 0))
                    own.join()

                norm(2 * l + 2, mixer_gain if l == 0 else None)
            for j in range(1, 4):
                add_squares(5, j)
            norm(5)

            cos, sin = C("cos2"), C("sin2")
            for c in range(12):
                n = N_EV + c
                b = 2 * (n % 2)
                split_lo(n + 2, parts=(0,))
                dve.wait_ge(gemm_done, n + 1)
                two = ps[:, b:b + 2, 0:SEQ]
                if c < 4:
                    dst = (aq, ak)[c // 2]
                    rope(dst, c % 2, b, cos, sin, rot_tmp, SEQ).then_inc(psum_free, 1)
                    rope_add(dst, c % 2, rot_tmp, n)
                elif c in (4, 5, 8, 9):
                    dst = av if c < 6 else bv
                    CP(dst[:, :, (c % 2) * CH:(c % 2 + 1) * CH], ps[:, b, :].rearrange("p (t n) -> p t n", t=2))\
                        .then_inc(psum_free, 1)
                elif c == 6:
                    TS(bq[:, :, :], two, 32 ** -0.5, None, ALU.mult).then_inc(psum_free, 1)
                elif c == 7:
                    CP(bk[:, :, :], two).then_inc(psum_free, 1)
                else:
                    CP(bog[:, 2 * (c - 10):2 * (c - 10) + 2, :], two).then_inc(psum_free, 1)
                split_lo(n + 2, parts=(1,))

            dve.wait_ge(z_done, 1)
            for g in range(2):
                last = TS(gl_z[:, g, :], ps[:, 5, g * SEQ:(g + 1) * SEQ], V("b_gk", g), None, ALU.add)
            last.then_inc(z_ready, 1)
            dve.wait_ge(l_ready, 1)
            own.step(STT(gl_z[:, :, :], gl_z[:, :, :], 0.0, gl_e[:, :, :], ALU.min, ALU.subtract))
            own.join()
            for g in range(2):
                own.step(nc.vector.tensor_tensor_scan(bcum[:, g, :], gl_z[:, g, :], gl_z[:, g, :], 0.0, ALU.add, ALU.add))
            dve.wait_ge(bog_act, 2)
            for t in range(4):
                own.step(TS(bog[:, t, :], bog[:, t, :], V("g_gla", t), None, ALU.mult))
            own.join()

            for qt in range(2):
                dve.wait_ge(m_scores, qt + 1)
                s4 = ps[:, 4:8, :].rearrange("p b (c x) -> p b c x", c=2)
                dg = s4[:, :, :, qt * P:(qt + 1) * P]
                for b in range(4):
                    d = ps[:, 4 + b, :].rearrange("p (c x) -> p c x", c=2)[:, :, qt * P:(qt + 1) * P]
                    own.step(TT(d, d, bc(causal, 2), ALU.add))
                own.join()
                own.step(nc.vector.tensor_reduce(small[:, S_MAX:S_MAX + 8].rearrange("p (b c) -> p b c", c=2),
                                                 s4[:, :, :, 0:(qt + 1) * P], AX_X, ALU.max))
                own.join()
                TS(small[:, S_MAX:S_MAX + 8], small[:, S_MAX:S_MAX + 8], -0.125, None, ALU.mult).then_inc(m_max, 1)
                dve.wait_ge(m_exp, qt + 1)
                own.step(nc.vector.reciprocal(small[:, S_R:S_R + 8], small[:, S_Z:S_Z + 8]))
                dve.wait_ge(m_pv, qt + 1)
                own.join()
                TT(a_o[:, :].rearrange("p (h d) -> p h d", h=8), ps[:, qt, :].rearrange("p (h d) -> p h d", h=8),
                   bcl(small[:, S_R:S_R + 8], 64), ALU.mult).then_inc(m_o, 1)
                dve.wait_ge(m_hi, qt + 1)
                t = slice(qt * P, (qt + 1) * P)
                TT(h_lo[:, 0:4, t], ps[:, 2 + qt, :].rearrange("p (h t) -> p h t", h=4), h_hi[:, 0:4, t].bitcast(F32),
                   ALU.subtract).then_inc(m_lo, 1)

            dve.wait_ge(glam_in, 16)
            own.step(nc.vector.memset(attn[:, :, :, :, :].rearrange("p a b c t -> p (a b c t)"), 0.0))

            def difference(lv):
                half = 1 << (lv - 1)
                for g in range(2):
                    bb = bcum[:, g, :].rearrange("p (b x) -> p b x", x=2 * half)
                    mid = bb[:, :, half - 1:half].broadcast_to([P, SEQ // (2 * half), 2 * half])
                    last = TT(dec[:, lv % 2, g, :].rearrange("p (b x) -> p b x", x=2 * half), bb, mid, ALU.subtract)
                last.then_inc(l_diff, 1)

            def merge(lv):
                dve.wait_ge(l_scores, lv + 1)
                b0 = 4 * (lv % 2)
                if lv == 8:
                    CP(attnX[:, :, :, :].rearrange("p a g t -> p a (g t)"), ps[:, b0:b0 + 4, 0:2 * P]).then_inc(l_merged, 1)
                    return
                if lv:
                    dve.wait_ge(l_merged, lv)
                nc.vector.copy_predicated(attn[:, :, :, :, :].rearrange("p a b c t -> p (a b c) t"), bc(gmask[:, lv, :], 16),
                                          ps[:, b0:b0 + 4, :].rearrange("p a (b t) -> p (a b) t", t=P)).then_inc(l_merged, 1)

            difference(1)
            own.join()
            for lv in range(1, 9):
                if lv < 8:
                    if lv > 1:
                        dve.wait_ge(l_qk, lv - 1)
                    difference(lv + 1)
                dve.wait_ge(l_dec, lv)
                if lv >= 3:
                    dve.wait_ge(l_scores, lv - 1)
                TT(gq[:, lv % 2, :, :], bq[:, :, :], dec[:, lv % 2, :, :], ALU.mult)
                TT(gk[:, lv % 2, :, :], bk[:, :, :], dec[:, lv % 2, :, :], ALU.mult).then_inc(l_qk, 1)
                merge(lv - 1)
            merge(8)
            for t in range(2):
                dve.wait_ge(b_sqr, t + 1)
                nc.vector.tensor_reduce(small[:, S_OSS:S_OSS + 8], b_sq[:, :].rearrange("p (h d) -> p h d", h=8), AX_X,
                                        ALU.add).then_inc(b_ssr, 1)
                dve.wait_ge(b_stdr, t + 1)
                own.step(nc.vector.reciprocal(small[:, S_ORS:S_ORS + 8], small[:, S_OSTD:S_OSTD + 8]))
                own.join()
                if t:
                    dve.wait_ge(b_oT, t)
                TT(b_o[:, :].rearrange("p (h d) -> p h d", h=8), ps[:, 4 + t, :].rearrange("p (h d) -> p h d", h=8),
                   bcl(small[:, S_ORS:S_ORS + 8], 64), ALU.mult).then_inc(b_on, 1)
            for t in range(2):
                dve.wait_ge(b_oT, t + 1)
                if t:
                    dve.wait_ge(b_lo, t)
                c = slice(t * P, (t + 1) * P)
                TT(b_raw[:, :, :], ps[:, 6 + t, :].rearrange("p (h t) -> p h t", h=4), bog[:, :, c], ALU.mult)\
                    .then_inc(b_rawr, 1)
                dve.wait_ge(b_hi, t + 1)
                TT(h_lo[:, 4:8, c], b_raw[:, :, :], h_hi[:, 4:8, c].bitcast(F32), ALU.subtract).then_inc(b_lo, 1)
            for c in range(4):
                split_lo(N_EVOUT + c + 2, parts=(0,))
                added(N_EVOUT + c, 2 * c)
                split_lo(N_EVOUT + c + 2, parts=(1,))
                if c:
                    add_squares(6, c)
            norm(6)

            def ffn(l):
                def body(it, third):
                    def at(n):
                        return n + 12 * third if it is None else it * 12 + n

                    def pairs(j):
                        return 12 * l + 4 * third + j if it is None else it * 4 + (12 * l + j)

                    def convs(j):
                        return 24 * l + 8 * third + j if it is None else it * 8 + (24 * l + j)

                    v0 = VEC[f"ffn{l}"]
                    cw = vec[:, v0 + 64 * third:v0 + 64 * third + 64] if it is None else vec[:, bass.ds(it * 64 + v0, 64)]
                    CP(conv_w[:, :], cw).then_inc(conv_w_ready, 1)
                    for c in range(12):
                        n = N_FFN[l] + c
                        m = n + 2 if it is not None else n + 2 + 12 * third
                        split_lo(m, at if it is not None else same, (0,))
                        if c < 8:
                            p = c % 2
                            dve.wait_ge(conv0, convs(c + 1))
                            for back in (1, 2):
                                for t in range(2):
                                    o = 32 * p + 8 * (2 - back) + 2 * (c // 2) + t
                                    y = conv_y[:, p, t, back:SEQ]
                                    last = STT(y, ps[:, 2 * (n % 2) + t, 0:SEQ - back], conv_w[:, o:o + 1], y, ALU.mult, ALU.add)
                                    if back == 1:
                                        own.step(last)
                                if back == 1:
                                    own.join()
                            last.then_inc(psum_free, 1)
                        else:
                            added(n, 2 * (c - 8), at)
                        split_lo(m, at if it is not None else same, (1,))
                        if it is None and c > 8:
                            add_squares(7 + 2 * l, c - 8)
                        if c < 8 and c % 2:
                            dve.wait_ge(gelu_ready, pairs(c // 2 + 1))
                            TT(ffn_p[:, :, :], conv_y[:, 0, :, :], gelu_g[:, :, :], ALU.mult).then_inc(prod_ready, 1)
                            dve.wait_ge(prod_hi, pairs(c // 2 + 1))
                            TT(g_lo[:, c - 1:c + 1, 0:SEQ], ffn_p[:, :, :], g_hi[:, c - 1:c + 1, 0:SEQ].bitcast(F32),
                               ALU.subtract).then_inc(g_ready, 2)
                with dve.Fori(0, 2) as it:
                    own.enter(it, 16)
                    body(it, 0)
                own.leave(2)
                body(None, 2)

            ffn(0)
            norm(7)

            dve.wait_ge(lam_e, 2)
            e_, s_, q_, p_ = S2[:, 0:8], S2[:, 24:32], S2[:, 32:40], S2[:, 40:48]

            def then(ins):
                own.step(ins)
                own.join()

            then(TS(s_, e_, 2.0, None, ALU.add))
            then(nc.vector.reciprocal(s_, s_))
            then(TT(s_, s_, e_, ALU.mult))
            then(TT(q_, s_, s_, ALU.mult))
            then(TS(p_, q_, 1.0 / 17, 1.0 / 15, ALU.mult, ALU.add))
            for k in (13, 11, 9, 7, 5, 3, 1):
                then(TT(p_, p_, q_, ALU.mult))
                then(TS(p_, p_, 1.0 / k, None, ALU.add))
            then(STT(p_, p_, 2.0, s_, ALU.mult, ALU.mult))
            then(TS(q_, V("lam_od", 0, 8), -1.0, 0.0, ALU.mult, ALU.max))
            then(TT(p_, p_, q_, ALU.add))
            then(TS(S2[:, 8:16], p_, 8.0, None, ALU.mult))
            TS(S2[:, 16:24], p_, -8.0, None, ALU.mult).then_inc(lam_c, 1)

            for c in range(8):
                n = N_OD + c
                b = 2 * (n % 2)
                split_lo(n + 2, parts=(0,))
                if c < 4:
                    dve.wait_ge(xc0, c + 1)
                    for back in (1, 2, 3):
                        for m in range(2):
                            t = 2 * c + m
                            y = xr[:, t, back:SEQ]
                            last = STT(y, ps[:, b + m, 0:SEQ - back], V("od_w", 8 * (3 - back) + t), y, ALU.mult, ALU.add)
                            if back < 3:
                                own.step(last)
                        if back < 3:
                            own.join()
                    last.then_inc(psum_free, 1)
                else:
                    dve.wait_ge(gemm_done, n + 1)
                    CP(gate[:, 2 * (c - 4):2 * (c - 4) + 2, :], ps[:, b:b + 2, 0:SEQ]).then_inc(psum_free, 1)
                split_lo(n + 2, parts=(1,))
                if c < 4:
                    dve.wait_ge(xc_hi, c + 1)
                    t = slice(2 * c, 2 * c + 2)
                    TT(xr_lo[:, t, :], xr[:, t, :], xr_hi[:, t, :].bitcast(F32), ALU.subtract).then_inc(g_ready, 2)
            for w in range(2):
                split_lo(N_RG + w + 2)
            dve.wait_ge(sig_i, 1)
            TT(rg_i[:, :, :], rg_i[:, :, :], xr[:, :, :], ALU.mult).then_inc(psum_free, 2)
            for half in range(2):
                t = slice(4 * half, 4 * half + 4)
                dve.wait_ge(rg_exp, half + 1)
                own.step(TT(rg_r[:, t, :], rg_a[:, t, :], rg_a[:, t, :], ALU.mult))
                own.join()
                STT(rg_t[:, t, :], rg_r[:, t, :], 1.0, rg_t[:, t, :], ALU.add, ALU.mult).then_inc(rg_s, 1)
            dve.wait_ge(gate_act, 4)
            for half in range(2):
                t = slice(4 * half, 4 * half + 4)
                dve.wait_ge(rg_sqrt, half + 1)
                own.step(TT(rg_i[:, t, :], rg_i[:, t, :], rg_t[:, t, :], ALU.mult))
                own.join()
                for k in range(4 * half, 4 * half + 4):
                    own.step(nc.vector.tensor_tensor_scan(rg_t[:, k, :], rg_a[:, k, :], rg_i[:, k, :], 0.0, ALU.mult, ALU.add))
                own.join()
                TT(rg_r[:, t, :], rg_t[:, t, :], gate[:, t, :], ALU.mult).then_inc(rg_y, 1)
            for half in range(2):
                t = slice(4 * half, 4 * half + 4)
                dve.wait_ge(rg_yhi, half + 1)
                TT(h_lo[:, t, 0:SEQ], rg_r[:, t, :], h_hi[:, t, 0:SEQ].bitcast(F32), ALU.subtract).then_inc(rg_ylo, 1)
            for c in range(4):
                split_lo(N_ODOUT + c + 2, parts=(0,))
                added(N_ODOUT + c, 2 * c)
                split_lo(N_ODOUT + c + 2, parts=(1,))
                if c:
                    add_squares(8, c)
            norm(8)
            ffn(1)
            norm(9)


def chunks(w):
    k, c = w.shape
    w = w.reshape(k // D, KT, P, c // CH, CH)
    return w.transpose(3, 0, 2, 1, 4).reshape(-1, P, KT * CH)


def tiles(v):
    return v.reshape(-1, P).T


def constants():
    c = np.zeros((P, C_COLS), np.float32)
    t = np.arange(SEQ)
    inv = (10000.0 ** (-np.arange(0, 32, 2, dtype=np.float32) / np.float32(32))).astype(np.float32)
    ang = np.concatenate([(t // 64).astype(np.float32)[:, None] * inv, (t % 64).astype(np.float32)[:, None] * inv], -1)
    inv2 = (10000.0 ** (-np.arange(32, dtype=np.float32) / np.float32(32))).astype(np.float32)
    ang2 = t.astype(np.float32)[:, None] * inv2
    p = np.arange(P)
    sign = np.where(p // 32 % 2 == 0, 1, -1)[:, None]
    for name, a in (("", ang), ("2", ang2)):
        a = a.astype(np.float64).T[p % 32]
        c[:, CST["cos" + name]:CST["cos" + name] + SEQ] = np.cos(a)
        c[:, CST["sin" + name]:CST["sin" + name] + SEQ] = np.sin(a) * sign
    c[:, CST["ident"]:CST["ident"] + P] = np.eye(P)
    c[:, CST["ones"]:CST["ones"] + P] = 1
    c[:, CST["causal"]:CST["causal"] + P] = np.where(p[None, :] <= p[:, None], 0, -1e30)
    for i in range(4):
        for r in range(4):
            c[32 * i + r, CST["sel"] + 2 * i + r % 2] = 1
    pm = np.zeros((4, SEQ, SEQ))
    for g, w in enumerate((2, 4, 8, 16)):
        for i in range(SEQ):
            lo, hi = max(i - w // 2, 0), min(i + w - w // 2, SEQ)
            pm[g, lo:hi, i] = 1.0 / (hi - lo)
            pm[g, i, i] -= 1.0
    pm = pm.reshape(4, 2, P, SEQ).transpose(2, 1, 0, 3).astype(np.float32)
    gm = np.zeros((P, 8, P), np.int32)
    gm[:, 0] = np.eye(P)
    s_, t_ = p[:, None], p[None, :]
    for lv in range(1, 8):
        h = 1 << (lv - 1)
        gm[:, lv] = (s_ // (2 * h) == t_ // (2 * h)) & (s_ // h % 2 == 0) & (t_ // h % 2 == 1)
    return c, np.ascontiguousarray(pm), gm


def layout(i):
    a = {k: np.asarray(v) for k, v in i.items()}
    two = {k[:-2]: v for k, v in a.items() if k.endswith("_2")}
    def woven(w, ada, each):
        return np.concatenate([w[:, None], ada.reshape(-1, each, P, KT * CH)], 1).reshape(-1, P, KT * CH)

    ada = [chunks(a["w_ada"][l]) for l in range(2)]
    parts = [ada[0][:8]]
    for l in range(2):
        w = a["w_in"][l]
        w = chunks(np.concatenate([w[:, 512:], w[:, :512]], 1))
        parts.append(woven(w, ada[l][(8, 16)[l]:(16, 24)[l]], 1))
        w = chunks(a["w_out"][l])
        parts.append(w if l else woven(w, ada[0][16:], 2))
        up = chunks(a["w_mlp1"][l])
        down = chunks(a["w_mlp2"][l]).reshape(4, 4, P, KT * CH)
        for q in range(4):
            u = up[4 * q:4 * q + 4]
            parts += [u if l else woven(u, ada[1][4 * q:4 * q + 4], 1), down[:, q]]

    def ffn(l):
        up = chunks(two["ffn_w_up"][l])
        down = chunks(two["ffn_w_down"][l]).reshape(4, 3, P, KT * CH)
        for q in range(3):
            for j in range(4):
                parts.append(up[[4 * q + j, 12 + 4 * q + j]])
            parts.append(down[:, q])

    w = two["ev_w_in"][0]
    parts.append(chunks(np.concatenate([w[:, :2560], w[:, 2576:]], 1)))
    parts.append(chunks(two["ev_w_out"][0]))
    ffn(0)
    w = two["od_w_in"][0]
    parts.append(chunks(np.concatenate([w[:, D:], w[:, :D]], 1)))
    for k in ("od_w_a", "od_w_x"):
        parts.append(chunks(two[k][0].reshape(D, CH)))
    parts.append(chunks(two["od_w_out"][0]))
    ffn(1)
    stream = np.concatenate(parts, 0)
    assert stream.shape == (N_CHUNKS, P, KT * CH), stream.shape

    def both(u, v):
        return np.stack([tiles(u), tiles(v)], 2).reshape(P, 16)

    def short(v):
        return np.concatenate([v, np.zeros(P - v.shape[0], v.dtype)])[:, None]

    cols = [both(a["c"][0], a["c_ctx"])]
    for l in range(2):
        cols += [tiles(a["g_mix"][l]), tiles(a["g_mlp"][l]), tiles(a["s_pool"][l]), tiles(a["g_subln"][l]),
                 tiles(a["b_ada"][l])] + [short(a[k][l]) for k in ("lam_q1", "lam_q2", "lam_k1", "lam_k2")]
    cols += [tiles(a["g_final"]), tiles(two["mix_norm_g"][0]), tiles(two["mix_norm_g"][1]),
             tiles(two["ffn_norm_g"][0]), tiles(two["ffn_norm_g"][1]), tiles(two["final_norm_g"]),
             tiles(two["ev_b_gk2"][0]), tiles(two["ev_gla_norm_g"][0].reshape(-1)), tiles(two["od_conv_w"][0].reshape(-1)),
             tiles(two["od_conv_b"][0]), tiles(two["od_b_a"][0]), tiles(two["od_b_x"][0]), tiles(two["od_lambda"][0])]
    for l in range(2):
        cw = np.concatenate([two["ffn_conv_w"][l], two["ffn_conv_b"][l][None]], 0)
        cw = cw.reshape(4, 2, 3, 8, P).transpose(4, 2, 1, 0, 3)
        cols.append(cw.reshape(P, 192))
    vec = np.concatenate(cols, 1)
    assert vec.shape == (P, V_COLS), vec.shape
    xs = np.concatenate([a["x"][0], a["ctx"][0]], 0)
    cst, pm, gm = constants()
    return {
        "w_stream": stream, "x_in": xs.reshape(ALLT, KT, P).transpose(2, 1, 0),
        "vec_in": vec, "cst_in": cst, "pool_mats": pm, "gla_masks": gm,
        "w_pool": a["w_pool"].transpose(2, 0, 1, 3),
        "w_gk": two["ev_w_in"][0][:, 2560:2576].reshape(KT, P, 16).transpose(1, 0, 2),
        "w_gk2": two["ev_w_gk2"][0],
    }


def kernel(**inputs):
    import concourse.bacc as bacc
    from concourse.bass_utils import run_bass_kernel_spmd

    nc = bacc.Bacc("TRN2", target_bir_lowering=False, num_devices=1)
    arrays, args = {}, []
    for name, a in layout(inputs).items():
        a = np.ascontiguousarray(a)
        arrays[f"in_{name}"] = a
        args.append(nc.dram_tensor(f"in_{name}", a.shape, mybir.dt.from_np(a.dtype), kind="ExternalInput").ap())
    out = nc.dram_tensor("out", (P, KT, SEQ), F32, kind="ExternalOutput").ap()
    build_program(nc, *args, out)
    r = run_bass_kernel_spmd(nc, [arrays], core_ids=[0])
    y = r.results[0]["out"]
    return np.ascontiguousarray(np.asarray(y).transpose(2, 1, 0).reshape(1, SEQ, D))
```

```python
import concourse.bass as bass
from concourse import mybir
from contextlib import ExitStack
import math
import numpy as np

F32 = mybir.dt.float32
F32R = mybir.dt.float32r
I32 = mybir.dt.int32
ALU = mybir.AluOpType
ACT = mybir.ActivationFunctionType
AX_X = mybir.AxisListType.X

P = 128
D = 1024
KT = D // P
SEQ = 256
ALLT = 2 * SEQ
EPS = 1e-6
CH = 256
LAM_INIT = [0.8 - 0.6 * math.exp(-0.3 * l) for l in range(2)]

N_WIN = [8, 84]
N_WOUT = [24, 100]
N_MLP = [36, 104]
N_EV, N_EVOUT = 136, 148
N_FFN = [152, 202]
N_OD, N_RG, N_ODOUT = 188, 193, 198
N_GATE = [192, 195, 196, 197]
N_CHUNKS = 238

VEC = {}
V_COLS = 0
for _name, _n in (
    [("c", 16)]
    + [(f"{k}{l}", n) for l in range(2) for k, n in
       (("g_mix", 8), ("g_mlp", 8), ("s_pool", 4), ("g_sub", 1), ("b_ada", 48), ("lam", 4))]
    + [("g_final", 8), ("mix_g0", 8), ("mix_g1", 8), ("ffn_g0", 8), ("ffn_g1", 8), ("final_g", 8),
       ("b_gk", 2), ("g_gla", 4), ("od_w", 32), ("od_b", 8), ("b_a", 8), ("b_x", 8), ("lam_od", 8),
       ("ffn0", 192), ("ffn1", 192)]
):
    VEC[_name] = V_COLS
    V_COLS += _n

CST = {"cos": 0, "sin": 256, "cos2": 512, "sin2": 768, "ident": 1024, "ones": 1152, "causal": 1280, "sel": 1408}
C_COLS = 1416


class Steps:

    def __init__(self, eng, sem):
        self.eng, self.sem, self.n, self.loop = eng, sem, 0, None

    def step(self, ins):
        ins.then_inc(self.sem, 1)
        self.n += 1
        return ins

    def join(self):
        self.eng.wait_ge(self.sem, self.n if self.loop is None else self.loop[0] * self.loop[1] + self.n)

    def enter(self, i, per):
        self.loop, self.start = (i, per), self.n

    def leave(self, iters):
        per = self.n - self.start
        assert per == self.loop[1], (per, self.loop[1])
        self.n += per * (iters - 1)
        self.loop = None


def build_program(nc, w_stream, x_in, vec_in, cst_in, pool_mats, gla_masks, w_pool, w_gk, w_gk2,
                  out):
    ctx = ExitStack()
    with ctx:
        base = (nc.sbuf_base + 31) // 32 * 32
        top = [base]

        def place(name, shape, dt=F32, at=None):
            size = 4
            for d in shape[1:]:
                size *= d
            if at is None:
                at = top[0]
                top[0] += size
            return nc.alloc_sbuf_tensor_at(name, shape, dt, offset=at)

        x = place("x", [P, KT, ALLT])
        h_hi = place("h_hi", [P, KT, ALLT], F32R)
        h_lo = place("h_lo", [P, KT, ALLT], F32R)
        g_base = top[0]
        g_hi = place("g_hi", [P, KT, ALLT], F32R)
        g_lo = place("g_lo", [P, KT, ALLT], F32R)
        w_raw = place("w_raw", [P, 4, KT * CH])
        w_hi = place("w_hi", [P, 2, KT, CH], F32R)
        w_lo = place("w_lo", [P, 2, KT, CH], F32R)
        r_base = top[0]
        top[0] += 32768
        acc2 = place("acc2", [P, 2, ALLT])
        a_base = top[0]
        sq = place("sq", [P, 2, 2, ALLT])
        diag = place("diag", [P, 4, P])
        rows = place("rows", [P, 2, CH])
        vec = place("vec", [P, V_COLS])
        cst = place("cst", [P, C_COLS])
        wp = place("wp", [P, 2, 4, P])
        c_act = place("c_act", [P, KT, 2])
        c_st = place("c_st", [P, KT, 4], F32R)
        ada = place("ada", [P, 2, 48, 2])
        mod = place("mod", [P, 2, 2, KT, 2])
        small = place("small", [P, 112])
        assert top[0] <= nc.sbuf_usable_end, top[0]

        KB = 1024
        qT = place("qT", [P, 4, ALLT], at=r_base)
        kT = place("kT", [P, 4, ALLT], at=r_base + 8 * KB)
        v_tok = place("v_tok", [P, 4, 512], at=r_base + 16 * KB)
        u_tok = place("u_tok", [P, 4, 512], at=r_base + 24 * KB)
        h_raw = place("h_raw", [P, 2, ALLT], at=r_base + 18 * KB)
        relu = place("relu", [P, 2, 2, ALLT], at=r_base + 16 * KB)
        relu2 = place("relu2", [P, 2, ALLT], at=r_base + 24 * KB)
        aq = place("aq", [P, 4, SEQ], at=r_base)
        ak = place("ak", [P, 4, SEQ], at=r_base + 4 * KB)
        av = place("av", [P, 2, 512], at=r_base + 8 * KB)
        bq = place("bq", [P, 2, SEQ], at=r_base + 12 * KB)
        bk = place("bk", [P, 2, SEQ], at=r_base + 14 * KB)
        bv = place("bv", [P, 2, 512], at=r_base + 16 * KB)
        bog = place("bog", [P, 4, SEQ], at=r_base + 20 * KB)
        bcum = place("bcum", [P, 2, SEQ], at=r_base + 24 * KB)
        wgk = place("wgk", [P, KT, 16], at=r_base + 26 * KB)
        wgk2 = place("wgk2", [16, SEQ], at=r_base + 26 * KB + 512)
        wgk_hi = place("wgk_hi", [P, KT, 16], F32R, at=r_base + 28 * KB + 512)
        wgk_lo = place("wgk_lo", [P, KT, 16], F32R, at=r_base + 29 * KB)
        gkT = place("gkT", [16, SEQ], at=r_base + 26 * KB + 1536)
        rot_tmp = place("rot_tmp", [P, 2, SEQ], at=r_base + 30 * KB)
        conv_y = place("conv_y", [P, 2, 2, SEQ], at=r_base)
        gelu_g = place("gelu_g", [P, 2, SEQ], at=r_base + 4 * KB)
        ffn_p = place("ffn_p", [P, 2, SEQ], at=r_base + 6 * KB)
        conv_w = place("conv_w", [P, 64], at=r_base + 8 * KB)
        gate = place("gate", [P, KT, SEQ], at=r_base)
        xr = place("xr", [P, KT, SEQ], at=r_base + 8 * KB)
        rg_r = place("rg_r", [P, KT, SEQ], at=r_base + 16 * KB)
        rg_i = place("rg_i", [P, KT, SEQ], at=r_base + 24 * KB)
        prob = place("prob", [P, 2, 2, 512], at=g_base)
        wgt = place("wgt", [P, 2, 512], at=g_base + 8 * KB)
        wgtT = place("wgtT", [P, 2, 512], at=g_base + 12 * KB)
        o_sq = place("o_sq", [P, 512], at=g_base + 16 * KB)
        o_n = place("o_n", [P, 2, 512], at=g_base + 18 * KB)
        o_raw = place("o_raw", [P, 4, 512], at=g_base + 24 * KB)
        rope_tmp = place("rope_tmp", [P, 2, SEQ], at=g_base + 20 * KB)
        pool_y = place("pool_y", [P, 2, SEQ], at=g_base + 22 * KB)
        pmat = place("pmat", [P, 2, 4, SEQ], at=g_base + 24 * KB)
        y_out = place("y_out", [P, KT, SEQ], at=g_base)
        a_p = place("a_p", [P, 2, 4, SEQ], at=g_base)
        a_pT = place("a_pT", [P, 2, 4, P], at=g_base + 8 * KB)
        a_o = place("a_o", [P, 2, SEQ], at=g_base + 12 * KB)
        attn = place("attn", [P, 4, 2, 2, P], at=g_base)
        attnX = place("attnX", [P, 4, 2, P], at=g_base + 8 * KB)
        dec = place("dec", [P, 2, 2, SEQ], at=g_base + 16 * KB)
        gq = place("gq", [P, 2, 2, SEQ], at=g_base + 24 * KB)
        gk = place("gk", [P, 2, 2, SEQ], at=g_base + 28 * KB)
        b_o = place("b_o", [P, 512], at=g_base + 20 * KB)
        b_sq = place("b_sq", [P, 512], at=g_base + 22 * KB)
        b_raw = place("b_raw", [P, 4, P], at=g_base + 12 * KB)
        gl_e = place("gl_e", [P, 2, SEQ], at=g_base + 12 * KB)
        gl_z = place("gl_z", [P, 2, SEQ], at=g_base + 14 * KB)
        gmask = place("gmask", [P, 8, P], I32, at=a_base)
        xr_hi = place("xr_hi", [P, KT, SEQ], F32R, at=g_base)
        xr_lo = place("xr_lo", [P, KT, SEQ], F32R, at=g_base + 8 * KB)
        rg_a = place("rg_a", [P, KT, SEQ], at=g_base + 16 * KB)
        rg_t = place("rg_t", [P, KT, SEQ], at=g_base + 24 * KB)

        ps = ctx.enter_context(nc.psum_tensor("ps", [P, 8, 512], F32))

        def sem(name):
            return ctx.enter_context(nc.semaphore(name))

        raw_in = [sem(f"raw_in{i}") for i in range(4)]
        hi_ready, lo_ready, gemm_done, psum_free = sem("hi_ready"), sem("lo_ready"), sem("gemm_done"), sem("psum_free")
        half_hi, half_lo, half_used = sem("half_hi"), sem("half_lo"), sem("half_used")
        c_ready, rows_zero, col_done, ada_ready = sem("c_ready"), sem("rows_zero"), sem("col_done"), sem("ada_ready")
        vec_in_s, cst_in_s, x_in_s = sem("vec_in"), sem("cst_in"), sem("x_in")
        pool_in, glam_in, gk_in = sem("pool_in"), sem("glam_in"), sem("gk_in")
        silu_done = sem("silu_done")
        lam_prod, lam_sum, lam_exp = sem("lam_prod"), sem("lam_sum"), sem("lam_exp")
        h_ready, g_ready = sem("h_ready"), sem("g_ready")
        sq_done, sq_used, ss_done, std_ready, diag_ready, rbc_ready = (
            sem("sq_done"), sem("sq_used"), sem("ss_done"), sem("std_ready"), sem("diag_ready"), sem("rbc_ready"))
        norm_raw, norm_hi, x_final = sem("norm_raw"), sem("norm_hi"), sem("x_final")
        relu_ready, ghi_ready = sem("relu_ready"), sem("ghi_ready")
        py_done, py_copied, po_done, po_hi, po_lo = (
            sem("py_done"), sem("py_copied"), sem("po_done"), sem("po_hi"), sem("po_lo"))
        scores, nmax, exps, wgt_ready, wgtT_done, wgtT_copied, pv_done = (
            sem("scores"), sem("nmax"), sem("exps"), sem("wgt_ready"), sem("wgtT_done"), sem("wgtT_copied"),
            sem("pv_done"))
        o_copied = sem("o_copied")
        osq_ready, oss_ready, ostd_ready, on_ready, oT_done, ohi_ready, olo_ready = (
            sem("osq_ready"), sem("oss_ready"), sem("ostd_ready"), sem("on_ready"), sem("oT_done"),
            sem("ohi_ready"), sem("olo_ready"))
        m_scores, m_max, m_exp, m_T, m_Tc, m_pv, m_o, m_oT, m_hi, m_lo = (
            sem("m_scores"), sem("m_max"), sem("m_exp"), sem("m_T"), sem("m_Tc"), sem("m_pv"), sem("m_o"),
            sem("m_oT"), sem("m_hi"), sem("m_lo"))
        wgk_hi_ready, wgk_lo_ready = sem("wgk_hi_ready"), sem("wgk_lo_ready")
        gk_done, gk_copied, z_done, z_ready, e_ready, l_ready = (
            sem("gk_done"), sem("gk_copied"), sem("z_done"), sem("z_ready"), sem("e_ready"), sem("l_ready"))
        l_diff, l_dec, l_qk, l_scores, l_merged, bog_act = (
            sem("l_diff"), sem("l_dec"), sem("l_qk"), sem("l_scores"), sem("l_merged"), sem("bog_act"))
        b_pv, b_sqr, b_ssr, b_stdr, b_on, b_oT, b_rawr, b_hi, b_lo = (
            sem("b_pv"), sem("b_sqr"), sem("b_ssr"), sem("b_stdr"), sem("b_on"), sem("b_oT"), sem("b_rawr"),
            sem("b_hi"), sem("b_lo"))
        conv_w_ready, conv0, gelu_ready, prod_ready, prod_hi = (
            sem("conv_w_ready"), sem("conv0"), sem("gelu_ready"), sem("prod_ready"),
            sem("prod_hi"))
        xc0, xc_hi, gate_act = (
            sem("xc0"), sem("xc_hi"), sem("gate_act"))
        lam_e, lam_c, sig_r, sig_i, rg_exp, rg_s, rg_sqrt, rg_y, rg_yhi, rg_ylo = (
            sem("lam_e"), sem("lam_c"), sem("sig_r"), sem("sig_i"), sem("rg_exp"), sem("rg_s"), sem("rg_sqrt"),
            sem("rg_y"), sem("rg_yhi"), sem("rg_ylo"))
        out_ready, stored = sem("out_ready"), sem("stored")
        eps_set = sem("eps_set")
        act_step, dve_step = sem("act_step"), sem("dve_step")

        def V(name, i=0, n=1):
            return vec[:, VEC[name] + i:VEC[name] + i + n]

        def C(name, n=256):
            return cst[:, CST[name]:CST[name] + n]

        ones, ident, causal = C("ones", P), C("ident", P), C("causal", P)

        def bc(ap, n):
            return ap.rearrange("p (o m) -> p o m", o=1).broadcast_to([ap.shape[0], n, ap.shape[1]])

        def bcl(ap, n):
            return ap.rearrange("p (m o) -> p m o", o=1).broadcast_to([ap.shape[0], ap.shape[1], n])

        S_EPS, S_STD, S_RS, S_MAX, S_Z, S_R, S_NLAM, S_GS = 0, 1, 5, 9, 25, 33, 41, 43
        S_SQRT, S_LE, S_LAMP, S_OSS, S_OSTD, S_ORS = 45, 49, 53, 64, 80, 96

        def sm(c, n=1):
            return small[:, c:c + n]

        S2 = place("small2", [P, 64])
        assert top[0] <= nc.sbuf_usable_end, top[0]

        NORMS = [("mod", 0, 0, ALLT), ("mod", 0, 1, ALLT), ("mod", 1, 0, ALLT), ("mod", 1, 1, SEQ),
                 ("x", "g_final", None, SEQ), ("gain", "mix_g0", None, SEQ), ("gain", "ffn_g0", None, SEQ),
                 ("gain", "mix_g1", None, SEQ), ("gain", "ffn_g1", None, SEQ), ("out", "final_g", None, SEQ)]
        H_NORM = [0, 1, 2, 3, None, 4, 5, 6, 7, None]
        H0 = {"win0": 0, "mlp0": 8, "win1": 16, "mlp1": 24, "ev": 32, "ffn0": 40, "od": 48, "ffn1": 56}
        G0 = {"mlp0": 0, "mlp1": 32, "ffn0": 64, "od": 88, "ffn1": 96}
        X_AT = [0, 36, 84, 104, 136, 136, 152, 188, 202, 238]

        MOBA = {("S", 0): 0, ("S", 1): 3, ("S", 2): 6, ("S", 3): 9}
        for _u in range(4):
            MOBA["T", _u], MOBA["V", _u], MOBA["O", _u] = (MOBA["S", _u] + _d for _d in (2, 3, 4))

        def moba_steps(c, end):
            slot = 2 * (c - 6) + 2 + end if c >= 6 else c - 4 if end else None
            return sorted((step for step, at in MOBA.items() if at == slot), key=lambda step: step[1])

        RG_TILES = [slice(0, 4), slice(4, 6), slice(6, 8)]

        block = ctx.enter_context(nc.Block())

        @block.sync
        def _(sp):
            sp.dma_start(vec[:, :], vec_in).then_inc(vec_in_s, 16)
            for r in range(4):
                sp.dma_start(w_raw[:, r, :], w_stream[r]).then_inc(raw_in[r], 16)
            for n in range(4, 8):
                if n == 6:
                    sp.dma_start(x[:, :, :], x_in).then_inc(x_in_s, 16)
                sp.wait_ge(lo_ready, n - 3)
                sp.dma_start(w_raw[:, n % 4, :], w_stream[n]).then_inc(raw_in[n % 4], 16)
            with sp.Fori(2, N_CHUNKS // 4) as it:
                for r in range(4):
                    sp.wait_ge(lo_ready, it * 4 + (r - 3))
                    sp.dma_start(w_raw[:, r, :], w_stream[bass.ds(it * 4 + r, 1)].rearrange("a p n -> p (a n)"))\
                        .then_inc(raw_in[r], 16)
            for n in range(N_CHUNKS // 4 * 4, N_CHUNKS):
                sp.wait_ge(lo_ready, n - 3)
                sp.dma_start(w_raw[:, n % 4, :], w_stream[n]).then_inc(raw_in[n % 4], 16)
            sp.wait_ge(out_ready, KT)
            sp.dma_start(out, y_out[:, :, :]).then_inc(stored, 16)
            sp.wait_ge(stored, 16)

        @block.gpsimd
        def _(pool):
            pool.memset(sm(S_EPS), EPS).then_inc(eps_set, 1)
            pool.memset(rows[:, :, :], 0.0).then_inc(rows_zero, 1)
            pool.dma_start(cst[:, :], cst_in).then_inc(cst_in_s, 16)
            pool.wait_ge(half_hi, 9)
            pool.dma_start(wp[:, :, :, :], w_pool).then_inc(pool_in, 16)
            pool.dma_start(pmat[:, :, :, :], pool_mats).then_inc(pool_in, 16)
            pool.wait_ge(psum_free, N_WIN[1])
            pool.dma_start(pmat[:, :, :, :], pool_mats).then_inc(pool_in, 16)
            pool.wait_ge(rbc_ready, 6)
            pool.dma_start(gmask[:, :, :], gla_masks).then_inc(glam_in, 16)
            pool.wait_ge(psum_free, N_EV)
            pool.dma_start(wgk[:, :, :], w_gk).then_inc(gk_in, 16)
            pool.dma_start(wgk2[:, :], w_gk2).then_inc(gk_in, 16)

        @block.tensor
        def _(pe):
            mm = nc.tensor.matmul

            def same(n):
                return n

            def start_chunk(n, at, free=None):
                pe.wait_ge(half_lo, at(n + 1))
                if n >= 2:
                    pe.wait_ge(psum_free, at(n - 1 if free is None else free))

            def gemm_f(n, hi, lo, cols, ready, at=same, bank=None, free=None, middle=None):
                start_chunk(n, at, free)
                s = n % 2
                bank = 2 * s if bank is None else bank
                for k in range(KT):
                    if k == KT // 2:
                        pe.wait_ge(lo_ready, at(n + 1))
                        if middle is not None:
                            middle()
                    if ready is not None:
                        pe.wait_ge(ready[0], at_of(ready, at)(k + 1))
                    for m in range(2):
                        o = ps[:, bank + m, 0:cols.stop - cols.start]
                        wh, wl = w_hi[:, s, k, m * P:(m + 1) * P], w_lo[:, s, k, m * P:(m + 1) * P]
                        mm(o, wh, hi[:, k, cols], start=(k == 0), stop=False)
                        mm(o, wh, lo[:, k, cols], start=False, stop=False)
                        last = mm(o, wl, hi[:, k, cols], start=False, stop=(k == KT - 1))
                    if k == KT // 2 - 1:
                        last.then_inc(half_used, 1)
                last.then_inc(gemm_done, 1)

            def gemm_f_pair(n, hi, lo, cols, ready, at=same, free=(None, None), early=KT - 2,
                            middle=None):
                def part(n, ks):
                    s = n % 2
                    for k in ks:
                        if k == KT // 2:
                            pe.wait_ge(lo_ready, at(n + 1))
                        if ready is not None:
                            pe.wait_ge(ready[0], at_of(ready, at)(k + 1))
                        for m in range(2):
                            o = ps[:, 2 * s + m, 0:cols.stop - cols.start]
                            wh, wl = w_hi[:, s, k, m * P:(m + 1) * P], w_lo[:, s, k, m * P:(m + 1) * P]
                            mm(o, wh, hi[:, k, cols], start=(k == 0), stop=False)
                            mm(o, wh, lo[:, k, cols], start=False, stop=False)
                            last = mm(o, wl, hi[:, k, cols], start=False, stop=(k == KT - 1))
                        if k == KT // 2 - 1:
                            last.then_inc(half_used, 1)
                    return last
                for c in range(2):
                    start_chunk(n + c, at, free[c])
                    part(n + c, range(early))
                if middle is not None:
                    middle()
                for c in range(2):
                    part(n + c, range(early, KT)).then_inc(gemm_done, 1)

            def gemm_1(n, middle):
                start_chunk(n, same)
                pe.wait_ge(lo_ready, n + 1)
                s = n % 2
                for m in range(2):
                    for k in range(KT):
                        o = ps[:, s, m * SEQ:(m + 1) * SEQ]
                        wh, wl = w_hi[:, s, k, m * P:(m + 1) * P], w_lo[:, s, k, m * P:(m + 1) * P]
                        mm(o, wh, h_hi[:, k, 0:SEQ], start=(k == 0), stop=False)
                        mm(o, wh, h_lo[:, k, 0:SEQ], start=False, stop=False)
                        last = mm(o, wl, h_hi[:, k, 0:SEQ], start=False, stop=(k == KT - 1))
                        if m and k == KT // 2 - 1:
                            last.then_inc(half_used, 1)
                    if m == 0:
                        middle()
                last.then_inc(gemm_done, 1)

            def at_of(ready, at):
                if len(ready) == 2:
                    return lambda k: ready[1] + k
                return lambda k: ready[3] * ready[2] + (ready[1] + k)

            def gemm_t(n, tiles, ready=None, bank=None, free=None, middle=None):
                start_chunk(n, same, free)
                if ready is not None:
                    pe.wait_ge(ready[0], ready[1] + KT)
                s = n % 2
                bank = 2 * s if bank is None else bank
                for i in range(tiles):
                    o = ps[:, bank + i // 2, (i % 2) * CH:(i % 2 + 1) * CH]
                    t = slice(i * P, (i + 1) * P)
                    for k in range(KT):
                        if i == 0 and k == KT // 2:
                            pe.wait_ge(lo_ready, n + 1)
                        mm(o, h_hi[:, k, t], w_hi[:, s, k, :], start=(k == 0), stop=False)
                        mm(o, h_lo[:, k, t], w_hi[:, s, k, :], start=False, stop=False)
                        last = mm(o, h_hi[:, k, t], w_lo[:, s, k, :], start=False, stop=(k == KT - 1))
                        if i == tiles - 1 and k == KT // 2 - 1:
                            last.then_inc(half_used, 1)
                    if i == 0 and middle is not None:
                        middle()
                last.then_inc(gemm_done, 1)

            def ada_chunk(n, at=same, bank=7, free=None):
                start_chunk(n, at, free)
                s = n % 2
                for k in range(KT):
                    if k == KT // 2:
                        pe.wait_ge(lo_ready, at(n + 1))
                    for w in (w_hi, w_lo):
                        last = mm(ps[0:4, bank, 0:CH], c_st[:, k, :], w[:, s, k, :], start=(k == 0 and w is w_hi),
                                  stop=(k == KT - 1 and w is w_lo))
                    if k == KT // 2 - 1:
                        last.then_inc(half_used, 1)
                last.then_inc(gemm_done, 1)

            def ada_columns(n, buf=0, at=same):
                pe.wait_ge(psum_free, at(n + 1))
                for half in range(2):
                    last = mm(ps[:, 6, half * 8:half * 8 + 8], rows[:, buf, half * P:(half + 1) * P], cst[:, CST["sel"]:CST["sel"] + 8],
                              start=True, stop=True)
                last.then_inc(col_done, 1)

            def norm_sums(k):
                nt = NORMS[k][3] // P
                pe.wait_ge(sq_used, 3 * k + 3)
                pe.wait_ge(sq_done, 4 * k + 4)
                for j in range(nt):
                    for i, part in enumerate((acc2[:, 0], sq[:, 1, 0], sq[:, 1, 1])):
                        last = mm(ps[:, 4, j:j + 1], part[:, j * P:(j + 1) * P], ones[:, 0:1], start=(i == 0), stop=(i == 2))
                last.then_inc(ss_done, 1)

            def norm_broadcast(k):
                nt = NORMS[k][3] // P
                pe.wait_ge(diag_ready, k + 1)
                mm(ps[:, 5, 0:nt * P], ones, diag[:, 0:nt, :], start=True, stop=True).then_inc(rbc_ready, 1)

            def norm(k):
                norm_sums(k)
                norm_broadcast(k)

            def pooling(streams, m0, bank):
                def mix_out(m, g):
                    pe.wait_ge(py_copied, m + 1)
                    if m - m0 >= 2:
                        pe.wait_ge(po_lo, m - 1)
                    mm(ps[:, bank + m % 2, 0:SEQ], wp[:, m0 // 8, g, :], pool_y[:, m % 2, :], start=True, stop=True)\
                        .then_inc(po_done, 1)
                todo = [(g, s) for g in range(4) for s in range(streams)]
                for i, (g, s) in enumerate(todo):
                    m = m0 + i
                    if i >= 2:
                        pe.wait_ge(py_copied, m - 1)
                    for t in range(2):
                        last = mm(ps[:, m % 2, 0:SEQ], u_tok[:, 2 * s + t, g * P:(g + 1) * P], pmat[:, t, g, :],
                                  start=(t == 0), stop=(t == 1))
                    last.then_inc(py_done, 1)
                    if i:
                        mix_out(m - 1, todo[i - 1][0])
                mix_out(m0 + len(todo) - 1, todo[-1][0])

            def attention(units, u0, q0, pool):
                def score(i):
                    qt, hd, k0 = units[i]
                    u = u0 + i
                    if i >= 3:
                        pe.wait_ge(exps, u - 2)
                    for a in range(2):
                        r = slice(64 * a, 64 * a + 64)
                        last = mm(ps[:, 2 + 2 * (u % 3) + a, 0:ALLT - k0], qT[r, hd, qt * P:(qt + 1) * P],
                                  kT[r, hd, k0:ALLT], start=True, stop=True)
                    last.then_inc(scores, 1)

                def transposes(i):
                    u, kb = u0 + i, (ALLT - units[i][2]) // P
                    pe.wait_ge(wgt_ready, u + 1)
                    if i:
                        pe.wait_ge(wgtT_copied, u)
                    for b in range(kb):
                        last = nc.tensor.transpose(ps[:, 0, b * P:(b + 1) * P], wgt[:, u % 2, b * P:(b + 1) * P], ident)
                    last.then_inc(wgtT_done, 1)

                def values(i):
                    qt, hd, k0 = units[i]
                    u, kb = u0 + i, (ALLT - k0) // P
                    pe.wait_ge(wgtT_copied, u + 1)
                    if hd == 0 and i >= 4:
                        pe.wait_ge(o_copied, q0 + i // 4)
                    for b in range(kb):
                        last = mm(ps[:, 1, hd * P:(hd + 1) * P], wgtT[:, u % 2, b * P:(b + 1) * P],
                                  v_tok[:, k0 // P + b, hd * P:(hd + 1) * P], start=(b == 0), stop=(b == kb - 1))
                    last.then_inc(pv_done, 1)

                def outputs(q):
                    pe.wait_ge(on_ready, q + 1)
                    for hd in range(4):
                        last = nc.tensor.transpose(ps[:, 2 + q - q0, hd * P:(hd + 1) * P], o_n[:, q % 2, hd * P:(hd + 1) * P], ident)
                    last.then_inc(oT_done, 1)

                score(0)
                score(1)
                pool()
                score(2)
                for i in range(len(units)):
                    transposes(i)
                    if i + 3 < len(units):
                        score(i + 3)
                    values(i)

                def finish():
                    for q in range(len(units) // 4):
                        outputs(q0 + q)
                    pe.wait_ge(olo_ready, q0 + len(units) // 4)
                pe.wait_ge(o_copied, q0 + len(units) // 4)
                return finish

            pe.wait_ge(c_ready, 1)
            for n in range(8):
                ada_chunk(n, bank=2 * (n % 2))
                if n == 1:
                    pe.wait_ge(cst_in_s, 16)
                    pe.wait_ge(lam_prod, 1)
                    mm(ps[:, 6, 0:4], ones, small[:, S_LAMP:S_LAMP + 4], start=True, stop=True).then_inc(lam_sum, 1)
                if n == 4:
                    pe.wait_ge(lam_exp, 1)
                    ada_columns(3, 0)
                if n == 5:
                    norm_sums(0)
            norm_broadcast(0)
            ada_columns(7, 1)

            for l in range(2):
                n0 = N_WIN[l]
                hr = (h_ready, H0[f"win{l}"])
                for c in range(8):
                    n = n0 + 2 * c
                    free = (n - 1, n - 2, n - 3)[min(c, 2)]
                    if c < 4:
                        width = ALLT if l == 0 or c >= 2 else SEQ
                        gemm_f(n, h_hi, h_lo, slice(0, width), hr if c == 0 else None, bank=2 * (c % 2), free=free)
                    else:
                        gemm_t(n, 4 if l == 0 or c < 6 else 2, bank=2 * (c % 2), free=free)
                    if c == 4:
                        ada_columns(n - 1)
                    ada_chunk(n + 1)
                ada_columns(n0 + 15)
                pe.wait_ge(psum_free, n0 + 16)
                pe.wait_ge(ada_ready, 4 + 8 * l)

                def pool():
                    pe.wait_ge(pool_in, 32 + 16 * l)
                    pooling(2 - l, 8 * l, (6, 2)[l])
                    pe.wait_ge(po_lo, 8 + 4 * l)

                if l == 0:
                    finish = attention([(qt, hd, 0 if qt < 2 else SEQ) for qt in range(4) for hd in range(4)], 0, 0, pool)
                else:
                    finish = attention([(qt, hd, 0) for qt in range(2) for hd in range(4)], 16, 4, pool)
                for c in range(4):
                    n = N_WOUT[l] + (3 - 2 * l) * c
                    free = (n - 1, n - 3, n - 5)[min(c, 2)] if l == 0 else None
                    gemm_f(n, h_hi, h_lo, slice(0, ALLT if l == 0 else SEQ), None, bank=2 * (c % 2), free=free,
                           middle=finish if c == 0 else None)
                    if l == 0:
                        if c == 2:
                            ada_columns(n - 1)
                        ada_chunk(n + 1, free=n - 1)
                        ada_chunk(n + 2, bank=5, free=n)
                if l == 0:
                    ada_columns(N_WOUT[0] + 11)
                norm(2 * l + 1)
                width = slice(0, ALLT if l == 0 else SEQ)
                per = (12, 8)[l]
                with pe.Fori(0, 4) as it:
                    def at(n):
                        return it * per + n
                    for c in range(8):
                        n = N_MLP[l] + (c if l else min(2 * c, c + 4))
                        free = n - (1, 2, 3, 3, 3, 2, 1, 1)[c] if l == 0 else None
                        if c < 4:
                            gemm_f(n, h_hi, h_lo, width, (h_ready, H0[f"mlp{l}"]) if c == 0 else None, at,
                                   2 * (c % 2), free)
                            if l == 0:
                                ada_chunk(n + 1, at)
                        elif c == 4:
                            gemm_f_pair(n, g_hi, g_lo, width, (g_ready, G0[f"mlp{l}"], 8, it), at,
                                        (free, None if l else n - 1))
                            if l == 0:
                                ada_columns(n - 1, 0, at)
                        elif c > 5:
                            gemm_f(n, g_hi, g_lo, width, None, at)
                norm(2 * l + 2)
            norm(5)

            def moba(step, u):
                qt, hh, B = u // 2, u % 2, 2 + 3 * (u % 2)
                if step == "S":
                    if u >= 2:
                        pe.wait_ge(m_lo, u - 1)
                    else:
                        pe.wait_ge(psum_free, N_EV + 4)
                        pe.wait_ge(z_ready, 1)
                    for j in range(4):
                        r = slice(64 * (j % 2), 64 * (j % 2) + 64)
                        last = mm(ps[:, B + j % 2, j // 2 * SEQ:j // 2 * SEQ + (qt + 1) * P],
                                  aq[r, 2 * hh + j // 2, qt * P:(qt + 1) * P], ak[r, 2 * hh + j // 2, 0:(qt + 1) * P],
                                  start=True, stop=True)
                    last.then_inc(m_scores, 1)
                elif step == "T":
                    pe.wait_ge(m_exp, u + 1)
                    for kb in range(qt + 1):
                        for j in range(4):
                            last = nc.tensor.transpose(ps[:, B + kb, j * P:(j + 1) * P], a_p[:, u % 2, j, kb * P:(kb + 1) * P],
                                                       ident)
                    last.then_inc(m_T, 1)
                elif step == "V":
                    pe.wait_ge(m_Tc, u + 1)
                    for j in range(4):
                        hd = 4 * hh + j
                        for kb in range(qt + 1):
                            last = mm(ps[:, B + 2, j * 64:(j + 1) * 64], a_pT[:, kb, j, :], av[:, kb, hd * 64:(hd + 1) * 64],
                                      start=(kb == 0), stop=(kb == qt))
                    last.then_inc(m_pv, 1)
                else:
                    pe.wait_ge(m_o, u + 1)
                    for i in range(2):
                        last = nc.tensor.transpose(ps[:, B + 2, SEQ + i * P:SEQ + (i + 1) * P], a_o[:, u % 2, i * P:(i + 1) * P],
                                                   ident)
                    last.then_inc(m_oT, 1)

            def moba_at(c, end):
                for step in moba_steps(c, end):
                    moba(*step)

            for c in range(12):
                n = N_EV + c
                if c == 0:
                    gemm_f(n, h_hi, h_lo, slice(0, SEQ), (h_ready, H0["ev"]), bank=2)
                    pe.wait_ge(wgk_lo_ready, 1)
                    for k in range(KT):
                        mm(ps[0:16, 6, 0:SEQ], wgk_hi[:, k, :], h_hi[:, k, 0:SEQ], start=(k == 0), stop=False)
                        mm(ps[0:16, 6, 0:SEQ], wgk_hi[:, k, :], h_lo[:, k, 0:SEQ], start=False, stop=False)
                        last = mm(ps[0:16, 6, 0:SEQ], wgk_lo[:, k, :], h_hi[:, k, 0:SEQ], start=False, stop=(k == KT - 1))
                    last.then_inc(gk_done, 1)
                elif c in (4, 5, 8, 9):
                    gemm_t(n, 2, bank=n % 2, middle=lambda: moba_at(c, 0))
                else:
                    gemm_1(n, lambda: moba_at(c, 0))
                if c == 1:
                    pe.wait_ge(gk_copied, 1)
                    for g in range(2):
                        last = mm(ps[:, 7, g * SEQ:(g + 1) * SEQ], wgk2[:, g * P:(g + 1) * P], gkT[:, :], start=True, stop=True)
                    last.then_inc(z_done, 1)
                moba_at(c, 1)
            pe.wait_ge(psum_free, N_EV + 12)

            for lv in range(9):
                kk, qq = (bk, bq) if lv == 0 else (gk[:, lv % 2, :, :], gq[:, lv % 2, :, :])
                if lv:
                    pe.wait_ge(l_qk, lv)
                b0 = 4 * (lv % 2)
                if lv < 2:
                    pe.wait_ge(m_lo, 3 + lv)
                else:
                    pe.wait_ge(l_merged, lv - 1)
                for hd in range(8):
                    r = slice(32 * (hd % 4), 32 * (hd % 4) + 32)
                    g = hd // 4
                    for t in range(2 if lv < 8 else 1):
                        c = (g * 2 + t) * P if lv < 8 else g * P
                        tq = t if lv < 8 else 1
                        last = mm(ps[:, b0 + hd % 4, c:c + P], kk[r, g, t * P:(t + 1) * P],
                                  qq[r, g, tq * P:(tq + 1) * P], start=True, stop=True, tile_position=(32 * (hd % 4), 0))
                last.then_inc(l_scores, 1)
            pe.wait_ge(l_merged, 9)
            for t in range(2):
                for hd in range(8):
                    o = ps[:, 4 + t, hd * 64:(hd + 1) * 64]
                    if t:
                        mm(o, attnX[:, hd % 4, hd // 4, :], bv[:, 0, hd * 64:(hd + 1) * 64], start=True, stop=False)
                    last = mm(o, attn[:, hd % 4, hd // 4, t, :], bv[:, t, hd * 64:(hd + 1) * 64], start=(t == 0), stop=True)
                last.then_inc(b_pv, 1)

            def gla_outputs():
                for t in range(2):
                    pe.wait_ge(b_on, t + 1)
                    for i in range(4):
                        last = nc.tensor.transpose(ps[:, 6 + t, i * P:(i + 1) * P], b_o[:, i * P:(i + 1) * P], ident)
                    last.then_inc(b_oT, 1)
                pe.wait_ge(b_lo, 2)

            gemm_f_pair(N_EVOUT, h_hi, h_lo, slice(SEQ, ALLT), None, early=KT // 2, middle=gla_outputs)
            for c in (2, 3):
                gemm_f(N_EVOUT + c, h_hi, h_lo, slice(SEQ, ALLT), None)
            norm(6)

            def ffn(l):
                with pe.Fori(0, 3) as it:
                    def at(n):
                        return it * 12 + n
                    for c in range(12):
                        n = N_FFN[l] + c
                        if c < 8:
                            gemm_f(n, h_hi, h_lo, slice(0, SEQ), (h_ready, H0[f"ffn{l}"]) if c == 0 else None, at)
                        elif c == 8:
                            gemm_f_pair(n, g_hi, g_lo, slice(0, SEQ), (g_ready, G0[f"ffn{l}"], 8, it), at)
                        elif c > 9:
                            gemm_f(n, g_hi, g_lo, slice(0, SEQ), None, at)

            ffn(0)
            norm(7)
            for n in range(N_OD, N_RG):
                gemm_f(n, h_hi, h_lo, slice(0, SEQ), (h_ready, H0["od"]) if n == N_OD else None)
            for w in range(2):
                n = N_RG + w
                pe.wait_ge(lo_ready, n + 1)
                if w == 0:
                    pe.wait_ge(g_ready, G0["od"] + KT)
                else:
                    pe.wait_ge(psum_free, N_RG)
                s = n % 2
                for b in range(4):
                    for m in range(2):
                        o = ps[:, 4 * (1 - w) + b, m * SEQ:(m + 1) * SEQ]
                        for kk in range(2):
                            k = 2 * b + kk
                            wh, wl = w_hi[:, s, k, m * P:(m + 1) * P], w_lo[:, s, k, m * P:(m + 1) * P]
                            mm(o, wh, xr_hi[:, k, :], start=(kk == 0), stop=False)
                            mm(o, wh, xr_lo[:, k, :], start=False, stop=False)
                            last = mm(o, wl, xr_hi[:, k, :], start=False, stop=(kk == 1))
                    if b == 1:
                        last.then_inc(half_used, 1)
                last.then_inc(gemm_done, 1)
            for n in N_GATE[1:]:
                if n == N_GATE[2]:
                    pe.wait_ge(sig_i, 2)
                gemm_f(n, h_hi, h_lo, slice(0, SEQ), None)
            gemm_f_pair(N_ODOUT, xr_hi, xr_lo, slice(0, SEQ), (rg_ylo, 0), early=KT // 2)
            for c in (2, 3):
                gemm_f(N_ODOUT + c, xr_hi, xr_lo, slice(0, SEQ), None)
            norm(8)
            ffn(1)
            norm(9)

        @block.scalar
        def _(act):
            A = nc.scalar.activation
            own = Steps(act, act_step)

            def same(n):
                return n

            def split_hi(n, at=same, it=None, per=0, parts=(0, 1)):
                if n >= N_CHUNKS:
                    return
                w = 16 * (n // 4 + 1)
                for part in parts:
                    if part == 0:
                        act.wait_ge(raw_in[n % 4], w if it is None else it * (per * 4) + w)
                    if n >= 2:
                        act.wait_ge((half_used, gemm_done)[part], at(n - 1))
                    k = slice(part * KT // 2, (part + 1) * KT // 2)
                    A(w_hi[:, n % 2, k, :].rearrange("p k n -> p (k n)"), w_raw[:, n % 4, k.start * CH:k.stop * CH], ACT.Copy)\
                        .then_inc((half_hi, hi_ready)[part], 1)

            def squares(k, j, n=None):
                w = NORMS[k][3]
                if n is not None:
                    act.wait_ge(psum_free, n + 1)
                if j == 3:
                    act.wait_ge(sq_used, 3 * k + 1)
                dst = acc2[:, :, 0:w] if j == 0 else sq[:, j % 2, :, 0:w]
                A(dst, x[:, 2 * j:2 * j + 2, 0:w], ACT.Square).then_inc(sq_done, 1)

            def norm_root(k):
                w = NORMS[k][3]
                A(sm(S_SQRT), sm(S_EPS), ACT.Sqrt)
                act.wait_ge(ss_done, k + 1)
                A(small[:, S_STD:S_STD + w // P], ps[:, 4, 0:w // P], ACT.Sqrt, bias=sm(S_EPS), scale=1.0 / D)\
                    .then_inc(std_ready, 1)

            def norm(k, before=None):
                norm_root(k)
                if before is not None:
                    before()
                norm_split(k)

            def norm_split(k):
                mode, p1, p2, w = NORMS[k]
                if H_NORM[k] is not None:
                    for t in range(KT):
                        n = KT * H_NORM[k] + t
                        act.wait_ge(norm_raw, n + 1)
                        if mode == "gain":
                            last = A(h_hi[:, t, 0:w], h_raw[:, t % 2, 0:w], ACT.Copy)
                        else:
                            for s in range(w // SEQ):
                                c = slice(s * SEQ, (s + 1) * SEQ)
                                last = A(h_hi[:, t, c], h_raw[:, t % 2, c], ACT.Identity, bias=ada[:, p1, 24 * p2 + t, s:s + 1])
                        last.then_inc(norm_hi, 1)

            def pooling(streams, m0, l):
                todo = [(g, s) for g in range(4) for s in range(streams)]

                def scaled(m, g, s):
                    act.wait_ge(po_done, m + 1)
                    A(h_hi[:, g, s * SEQ:(s + 1) * SEQ], ps[:, (6, 2)[l] + m % 2, 0:SEQ], ACT.Copy, scale=V(f"s_pool{l}", g))\
                        .then_inc(po_hi, 1)
                for i, (g, s) in enumerate(todo):
                    m = m0 + i
                    act.wait_ge(py_done, m + 1)
                    A(pool_y[:, m % 2, :], ps[:, m % 2, 0:SEQ], ACT.Copy).then_inc(py_copied, 1)
                    if i:
                        scaled(m - 1, *todo[i - 1])
                scaled(m0 + len(todo) - 1, *todo[-1])

            def attention(units, u0, q0, l):
                def exponentials(i):
                    u, w = u0 + i, ALLT - units[i][2]
                    act.wait_ge(nmax, u + 1)
                    if i >= 2:
                        act.wait_ge(wgt_ready, u - 1)
                    for a in range(2):
                        last = A(prob[:, u % 2, a, 0:w], ps[:, 2 + 2 * (u % 3) + a, 0:w], ACT.Exp,
                                 bias=sm(S_MAX + 2 * (u % 4) + a), scale=0.125, accum_out=sm(S_Z + 2 * (u % 2) + a))
                    last.then_inc(exps, 1)

                def copyT(i):
                    u, w = u0 + i, ALLT - units[i][2]
                    act.wait_ge(wgtT_done, u + 1)
                    A(wgtT[:, u % 2, 0:w], ps[:, 0, 0:w], ACT.Copy).then_inc(wgtT_copied, 1)

                def copy_o(q):
                    act.wait_ge(pv_done, u0 + 4 * (q - q0 + 1))
                    A(o_raw[:, q - q0, :], ps[:, 1, :], ACT.Copy).then_inc(o_copied, 1)

                def o_squares(q):
                    act.wait_ge(o_copied, q + 1)
                    if q > q0:
                        act.wait_ge(oss_ready, q)
                    A(o_sq[:, :], o_raw[:, q - q0, :], ACT.Square).then_inc(osq_ready, 1)

                def out_hi(q):
                    act.wait_ge(oT_done, q + 1)
                    qt = units[4 * (q - q0)][0]
                    A(h_hi[:, 4:8, qt * P:(qt + 1) * P], ps[:, 2 + q - q0, :].rearrange("p (h t) -> p h t", h=4), ACT.Copy,
                      scale=small[:, S_GS + l:S_GS + l + 1]).then_inc(ohi_ready, 1)

                nq = len(units) // 4
                exponentials(0)
                pooling(2 - l, 8 * l, l)
                for i in range(len(units)):
                    if i + 1 < len(units):
                        exponentials(i + 1)
                    if i >= 4 and i % 4 == 0:
                        copy_o(q0 + i // 4 - 1)
                    copyT(i)
                    if i >= 4 and i % 4 == 0:
                        o_squares(q0 + i // 4 - 1)
                copy_o(q0 + nq - 1)
                o_squares(q0 + nq - 1)
                A(sm(S_SQRT), sm(S_EPS), ACT.Sqrt)
                act.wait_ge(oss_ready, q0 + nq)
                A(small[:, S_OSTD:S_OSTD + 4 * nq], small[:, S_OSS:S_OSS + 4 * nq], ACT.Sqrt, bias=sm(S_EPS), scale=1.0 / P)\
                    .then_inc(ostd_ready, 1)
                for q in range(nq):
                    out_hi(q0 + q)

            act.wait_ge(vec_in_s, 16)
            act.wait_ge(eps_set, 1)
            A(c_act[:, :, :].rearrange("p k s -> p (k s)"), V("c", 0, 16), ACT.Silu).then_inc(silu_done, 1)
            act.wait_ge(silu_done, 1)
            A(c_st[:, :, 0:2], c_act[:, :, :], ACT.Copy).then_inc(silu_done, 1)
            split_hi(0)
            split_hi(1)
            for n in range(8):
                split_hi(n + 2)
                if n == 1:
                    act.wait_ge(lam_sum, 1)
                    A(sm(S_LE, 4), ps[:, 6, 0:4], ACT.Exp).then_inc(lam_exp, 1)
                if n == 3:
                    act.wait_ge(x_in_s, 16)
                    for j in range(4):
                        squares(0, j)
                if n == 4:
                    norm_root(0)
            norm_split(0)
            for l in range(2):
                for n in range(N_WIN[l], N_WIN[l] + 16):
                    split_hi(n + 2)
                if l == 0:
                    attention([(qt, hd, 0 if qt < 2 else SEQ) for qt in range(4) for hd in range(4)], 0, 0, l)
                else:
                    attention([(qt, hd, 0) for qt in range(2) for hd in range(4)], 16, 4, l)
                each = 3 - 2 * l
                for c in range(4):
                    n = N_WOUT[l] + each * c
                    split_hi(n + 2, parts=(0,))
                    if l == 0 or c < 3:
                        split_hi(n + 2, parts=(1,))
                    if l == 0:
                        split_hi(n + 3)
                    squares(2 * l + 1, c, n)
                    if l == 0 and c < 3:
                        split_hi(n + 4)
                norm(2 * l + 1, lambda: split_hi(N_MLP[l] + 1, parts=(1,) if l else (0, 1)))
                w = ALLT if l == 0 else SEQ
                per = (12, 8)[l]

                def quarter(it, q):
                    def at(n):
                        return n + per * q if it is None else it * per + n

                    for c in range(8):
                        n = N_MLP[l] + (c if l else min(2 * c, c + 4))

                        def split(m, parts):
                            if it is None:
                                split_hi(n + m + 2 + per * q, parts=parts)
                            else:
                                split_hi(n + m + 2, at, it, per, parts)

                        split(0, (0,))
                        if c < 4:
                            up = 16 * l + 4 * q + c + 1 if it is None else it * 4 + (16 * l + c + 1)
                            act.wait_ge(gemm_done, at(n + 1))
                            A(relu[:, c % 2, :, 0:w], ps[:, 2 * (c % 2):2 * (c % 2) + 2, 0:w], ACT.Relu)\
                                .then_inc(relu_ready, 1)
                            act.wait_ge(relu_ready, up)
                            A(g_hi[:, 2 * c:2 * c + 2, 0:w], relu[:, c % 2, :, 0:w], ACT.Square).then_inc(ghi_ready, 1)
                        if it is not None or c < 7:
                            split(0, (1,))
                        if c < 4 and l == 0:
                            split(1, (0, 1))
                        if it is None and c >= 4:
                            squares(2 * l + 2, c - 4, n + per * q)

                with act.Fori(0, 3) as it:
                    quarter(it, 0)
                quarter(None, 3)
                norm(2 * l + 2, lambda: split_hi(X_AT[2 * l + 2] + 1, parts=(1,)))
            for j in range(4):
                act.wait_ge(x_final, 2 * j + 2)
                squares(5, j)
            norm(5)

            def moba(step, u):
                qt, hh, B = u // 2, u % 2, 2 + 3 * (u % 2)
                if step == "S":
                    act.wait_ge(m_max, u + 1)
                    for j in range(4):
                        last = A(a_p[:, u % 2, j, 0:(qt + 1) * P], ps[:, B + j % 2, j // 2 * SEQ:j // 2 * SEQ + (qt + 1) * P],
                                 ACT.Exp, bias=sm(S_MAX + 4 * (u % 2) + 2 * (j % 2) + j // 2), scale=0.125,
                                 accum_out=sm(S_Z + 4 * (u % 2) + j))
                    last.then_inc(m_exp, 1)
                elif step == "T":
                    act.wait_ge(m_T, u + 1)
                    if u:
                        act.wait_ge(m_pv, u)
                    A(a_pT[:, 0:qt + 1, :, :].rearrange("p k h t -> p k (h t)"), ps[:, B:B + qt + 1, :], ACT.Copy)\
                        .then_inc(m_Tc, 1)
                elif step == "O":
                    act.wait_ge(m_oT, u + 1)
                    t = slice(SEQ + qt * P, SEQ + (qt + 1) * P)
                    A(h_hi[:, 2 * hh:2 * hh + 2, t], ps[:, B + 2, SEQ:2 * SEQ].rearrange("p (i t) -> p i t", i=2), ACT.Copy)\
                        .then_inc(m_hi, 1)

            def decays(lv):
                act.wait_ge(l_diff, lv)
                d = dec[:, lv % 2, :, :]
                own.step(A(d, d, ACT.Abs))
                own.join()
                A(d, d, ACT.Exp, scale=-1.0 / 32).then_inc(l_dec, 1)

            act.wait_ge(gk_in, 32)
            A(wgk_hi[:, :, :], wgk[:, :, :], ACT.Copy).then_inc(wgk_hi_ready, 1)
            for c in range(12):
                for step in moba_steps(c, 0):
                    moba(*step)
                split_hi(N_EV + c + 2, parts=(0,))
                for step in moba_steps(c, 1):
                    moba(*step)
                if c == 0:
                    act.wait_ge(gk_done, 1)
                    A(gkT[:, :], ps[0:16, 6, 0:SEQ], ACT.Copy).then_inc(gk_copied, 1)
                if c == 2:
                    act.wait_ge(z_ready, 1)
                    A(gl_e[:, :, :], gl_z[:, :, :], ACT.Abs).then_inc(e_ready, 1)
                    act.wait_ge(e_ready, 1)
                    A(gl_e[:, :, :], gl_e[:, :, :], ACT.Exp, scale=-1.0).then_inc(e_ready, 1)
                    act.wait_ge(e_ready, 2)
                    A(gl_e[:, :, :], gl_e[:, :, :], ACT.Ln, bias=1.0).then_inc(l_ready, 1)
                if c == 9:
                    decays(1)
                split_hi(N_EV + c + 2, parts=(1,))
            for lv in range(2, 9):
                decays(lv)
            act.wait_ge(psum_free, N_EV + 12)
            A(bog[:, :, :], bog[:, :, :], ACT.Silu).then_inc(bog_act, 1)
            for t in range(2):
                act.wait_ge(b_pv, t + 1)
                if t:
                    act.wait_ge(b_ssr, 1)
                A(b_sq[:, :], ps[:, 4 + t, :], ACT.Square).then_inc(b_sqr, 1)
                act.wait_ge(b_ssr, t + 1)
                A(small[:, S_OSTD:S_OSTD + 8], small[:, S_OSS:S_OSS + 8], ACT.Sqrt, bias=sm(S_EPS), scale=1.0 / 64)\
                    .then_inc(b_stdr, 1)
            for t in range(2):
                act.wait_ge(b_rawr, t + 1)
                A(h_hi[:, 4:8, SEQ + t * P:SEQ + (t + 1) * P], b_raw[:, :, :], ACT.Copy).then_inc(b_hi, 1)
            for c in range(4):
                split_hi(N_EVOUT + c + 2, parts=(0,))
                if c < 3:
                    split_hi(N_EVOUT + c + 2, parts=(1,))
                squares(6, c, N_EVOUT + c)
            norm(6, lambda: split_hi(N_EVOUT + 5, parts=(1,)))

            def ffn(l):
                def body(it, third):
                    def at(n):
                        return n + 12 * third if it is None else it * 12 + n

                    def pairs(j):
                        return 12 * l + 4 * third + j if it is None else it * 4 + (12 * l + j)

                    act.wait_ge(conv_w_ready, 3 * l + third + 1 if it is None else it + (3 * l + 1))
                    for c in range(12):
                        n = N_FFN[l] + c

                        def split(parts):
                            if it is None:
                                split_hi(n + 2 + 12 * third, parts=parts)
                            else:
                                split_hi(n + 2, at, it, 12, parts)

                        split((0,))
                        if c < 8:
                            p = c % 2
                            act.wait_ge(gemm_done, at(n + 1))
                            for m in range(2):
                                o = 32 * p + 2 * (c // 2) + m
                                last = A(conv_y[:, p, m, :], ps[:, 2 * (n % 2) + m, 0:SEQ], ACT.Identity,
                                         scale=conv_w[:, o + 16:o + 17], bias=conv_w[:, o + 24:o + 25])
                            last.then_inc(conv0, 1)
                        if it is not None or c < 11:
                            split((1,))
                        if it is None and c >= 8:
                            squares(7 + 2 * l, c - 8, n + 12 * third)
                        if c < 8 and c % 2:
                            act.wait_ge(psum_free, at(n + 1))
                            A(gelu_g[:, :, :], conv_y[:, 1, :, :], ACT.Gelu_apprx_tanh).then_inc(gelu_ready, 1)
                            act.wait_ge(prod_ready, pairs(c // 2 + 1))
                            A(g_hi[:, c - 1:c + 1, 0:SEQ], ffn_p[:, :, :], ACT.Copy).then_inc(prod_hi, 1)
                with act.Fori(0, 2) as it:
                    body(it, 0)
                body(None, 2)

            ffn(0)
            norm(7, lambda: split_hi(X_AT[7] + 1, parts=(1,)))
            A(S2[:, 0:8], V("lam_od", 0, 8), ACT.Abs).then_inc(lam_e, 1)
            act.wait_ge(lam_e, 1)
            A(S2[:, 0:8], S2[:, 0:8], ACT.Exp, scale=-1.0).then_inc(lam_e, 1)
            for c in range(4):
                n = N_OD + c
                b = 2 * (n % 2)
                split_hi(n + 2, parts=(0,))
                act.wait_ge(gemm_done, n + 1)
                for m in range(2):
                    t = 2 * c + m
                    last = A(xr[:, t, :], ps[:, b + m, 0:SEQ], ACT.Identity, scale=V("od_w", 24 + t), bias=V("od_b", t))
                last.then_inc(xc0, 1)
                split_hi(n + 2, parts=(1,))
                act.wait_ge(psum_free, n + 1)
                A(xr_hi[:, 2 * c:2 * c + 2, :], xr[:, 2 * c:2 * c + 2, :], ACT.Copy).then_inc(xc_hi, 1)
            split_hi(N_GATE[0] + 2)
            for w, (dst, name, done) in enumerate(((rg_r, "b_a", sig_r), (rg_i, "b_x", sig_i))):
                split_hi(N_RG + w + 2, parts=(0,))
                act.wait_ge(gemm_done, N_RG + w + 1)
                for half in (1, 0):
                    for t in range(4 * half, 4 * half + 4):
                        last = A(dst[:, t, :], ps[:, 4 * (1 - w) + t // 2, (t % 2) * SEQ:(t % 2 + 1) * SEQ], ACT.Sigmoid,
                                 bias=V(name, t))
                    last.then_inc(done, 1)
                split_hi(N_RG + w + 2, parts=(1,))
            act.wait_ge(lam_c, 1)
            act.wait_ge(sig_r, 2)
            for half in range(2):
                for t in range(4 * half, 4 * half + 4):
                    A(rg_a[:, t, :], rg_r[:, t, :], ACT.Exp, scale=S2[:, 16 + t:17 + t])
                    last = A(rg_t[:, t, :], rg_r[:, t, :], ACT.Tanh, scale=S2[:, 8 + t:9 + t])
                last.then_inc(rg_exp, 1)
                if half == 0:
                    split_hi(N_GATE[1] + 2)
            for half in range(2):
                act.wait_ge(rg_s, half + 1)
                a = rg_t[:, 4 * half:4 * half + 4, :]
                A(a, a, ACT.Sqrt).then_inc(rg_sqrt, 1)

            def gelu(i, chunk):
                act.wait_ge(psum_free, chunk + 1)
                g = gate[:, RG_TILES[i], :]
                A(g, g, ACT.Gelu_apprx_tanh).then_inc(gate_act, 1)

            def y_hi(i):
                act.wait_ge(rg_y, i + 1)
                A(xr_hi[:, RG_TILES[i], :], rg_r[:, RG_TILES[i], :], ACT.Copy).then_inc(rg_yhi, 1)

            gelu(0, N_GATE[1])
            split_hi(N_GATE[2] + 2, parts=(0,))
            y_hi(0)
            split_hi(N_GATE[2] + 2, parts=(1,))
            gelu(1, N_GATE[2])
            split_hi(N_GATE[3] + 2, parts=(0,))
            gelu(2, N_GATE[3])
            y_hi(1)
            split_hi(N_GATE[3] + 2, parts=(1,))
            y_hi(2)
            for c in range(4):
                split_hi(N_ODOUT + c + 2, parts=(0,))
                if c < 3:
                    split_hi(N_ODOUT + c + 2, parts=(1,))
                squares(8, c, N_ODOUT + c)
            norm(8, lambda: split_hi(N_ODOUT + 5, parts=(1,)))
            ffn(1)
            norm(9, lambda: split_hi(X_AT[9] + 1, parts=(1,)))

        @block.vector
        def _(dve):
            TT, TS, STT, CP = nc.vector.tensor_tensor, nc.vector.tensor_scalar, nc.vector.scalar_tensor_tensor, nc.vector.tensor_copy
            own = Steps(dve, dve_step)

            def same(n):
                return n

            def split_lo(n, at=same, parts=(0, 1)):
                if n >= N_CHUNKS:
                    return
                for part in parts:
                    dve.wait_ge((half_hi, hi_ready)[part], at(n + 1))
                    k = slice(part * KT // 2, (part + 1) * KT // 2)
                    TT(w_lo[:, n % 2, k, :].rearrange("p k n -> p (k n)"), w_raw[:, n % 4, k.start * CH:k.stop * CH],
                       w_hi[:, n % 2, k, :].rearrange("p k n -> p (k n)").bitcast(F32), ALU.subtract)\
                        .then_inc((half_lo, lo_ready)[part], 1)

            def add_squares(k, j):
                if j == 3:
                    return
                w = NORMS[k][3]
                dve.wait_ge(sq_done, 4 * k + j + 1)
                if j == 2:
                    dve.wait_ge(sq_used, 3 * k + 1)
                TT(acc2[:, :, 0:w], acc2[:, :, 0:w], sq[:, j % 2, :, 0:w], ALU.add).then_inc(sq_used, 1)
                if j == 2:
                    dve.wait_ge(sq_used, 3 * k + 2)
                    TT(acc2[:, 0, 0:w], acc2[:, 0, 0:w], acc2[:, 1, 0:w], ALU.add).then_inc(sq_used, 1)

            def norm_diagonal(k):
                nt = NORMS[k][3] // P
                dve.wait_ge(std_ready, k + 1)
                own.step(nc.vector.reciprocal(small[:, S_RS:S_RS + nt], small[:, S_STD:S_STD + nt]))
                own.join()
                TT(diag[:, 0:nt, :], bc(ident, nt), bcl(small[:, S_RS:S_RS + nt], P), ALU.mult).then_inc(diag_ready, 1)

            def norm(k, before=None):
                norm_diagonal(k)
                if before is not None:
                    before()
                norm_apply(k)

            def norm_apply(k):
                mode, p1, p2, w = NORMS[k]
                dve.wait_ge(rbc_ready, k + 1)
                if mode in ("x", "out"):
                    dst, done = (x, x_final) if mode == "x" else (y_out, out_ready)
                    for t in range(KT):
                        STT(dst[:, t, 0:w], x[:, t, 0:w], V(p1, t), ps[:, 5, 0:w], ALU.mult, ALU.mult).then_inc(done, 1)
                    return
                h0 = KT * H_NORM[k]

                def lo(t):
                    dve.wait_ge(norm_hi, h0 + t + 1)
                    if mode == "gain":
                        last = TT(h_lo[:, t, 0:w], h_raw[:, t % 2, 0:w], h_hi[:, t, 0:w].bitcast(F32), ALU.subtract)
                    else:
                        for s in range(w // SEQ):
                            c = slice(s * SEQ, (s + 1) * SEQ)
                            last = STT(h_lo[:, t, c], h_raw[:, t % 2, c], ada[:, p1, 24 * p2 + t, s:s + 1],
                                       h_hi[:, t, c].bitcast(F32), ALU.add, ALU.subtract)
                    last.then_inc(h_ready, 1)

                for t in range(KT):
                    if t >= 2:
                        dve.wait_ge(h_ready, h0 + t - 1)
                    if mode == "gain":
                        STT(h_raw[:, t % 2, 0:w], x[:, t, 0:w], V(p1, t), ps[:, 5, 0:w], ALU.mult, ALU.mult)\
                            .then_inc(norm_raw, 1)
                    else:
                        for s in range(w // SEQ):
                            c = slice(s * SEQ, (s + 1) * SEQ)
                            last = STT(h_raw[:, t % 2, c], x[:, t, c], mod[:, p1, p2, t, s:s + 1], ps[:, 5, c], ALU.mult,
                                       ALU.mult)
                        last.then_inc(norm_raw, 1)
                    if t:
                        lo(t - 1)
                lo(KT - 1)

            def ada_rows(n, i, buf=0, at=same, bank=7):
                dve.wait_ge(gemm_done, at(n + 1))
                CP(rows[32 * i:32 * i + 4, buf, :], ps[0:4, bank, 0:CH]).then_inc(psum_free, 1)

            def ada_columns(l, v, count, at=None):
                dve.wait_ge(col_done, count)
                dst = ada[:, l, 8 * v:8 * v + 8, :] if at is None else \
                    ada[:, l, bass.ds(at, 8), :]
                b0 = VEC[f"b_ada{l}"]
                bias = vec[:, b0 + 8 * v:b0 + 8 * v + 8] if at is None else vec[:, bass.ds(at + b0, 8)]
                src = ps[:, 6, 0:16].rearrange("p (h i s) -> p h i s", h=2, i=4)
                for half in range(2):
                    d = dst.rearrange("p (i h) s -> p h i s", h=2)[:, half, :, :]
                    b = bias.rearrange("p (i h) -> p h i", h=2)[:, half, :]
                    last = TT(d, src[:, half, :, :], bcl(b, 2), ALU.add)
                last.then_inc(ada_ready, 1)

            def ada_mod(l, which):
                own.step(TS(mod[:, l, which, :, :], ada[:, l, 8 + 24 * which:16 + 24 * which, :], 1.0, None, ALU.add))
                own.join()
                return TT(mod[:, l, which, :, :], mod[:, l, which, :, :], bcl(V(("g_mix", "g_mlp")[which] + str(l), 0, 8), 2),
                          ALU.mult)

            def rope(dst, c, b, cos, sin, tmp, width, src=None):
                src = ps[:, b:b + 2, 0:SEQ] if src is None else src
                own.join()
                TT(dst[:, 2 * c:2 * c + 2, 0:SEQ], src, bc(cos, 2), ALU.mult)
                for q in range(4):
                    f, t = slice(32 * q, 32 * q + 32), slice(32 * (q ^ 1), 32 * (q ^ 1) + 32)
                    last = TT(tmp[t, :, :], src[f], bc(sin[f, :], 2), ALU.mult)
                if width > SEQ:
                    last = CP(dst[:, 2 * c:2 * c + 2, SEQ:width], ps[:, b:b + 2, SEQ:width])
                return last

            def rope_add(dst, c, tmp, n):
                dve.wait_ge(psum_free, n + 1)
                d = dst[:, 2 * c:2 * c + 2, 0:SEQ]
                own.step(TT(d, d, tmp[:, :, :], ALU.add))

            def pooling(streams, m0, l):
                todo = [(g, s) for g in range(4) for s in range(streams)]
                for i, (g, s) in enumerate(todo):
                    m = m0 + i
                    dve.wait_ge(po_hi, m + 1)
                    c = slice(s * SEQ, (s + 1) * SEQ)
                    STT(h_lo[:, g, c], ps[:, (6, 2)[l] + m % 2, 0:SEQ], V(f"s_pool{l}", g), h_hi[:, g, c].bitcast(F32),
                        ALU.mult, ALU.subtract).then_inc(po_lo, 1)

            def attention(units, u0, q0, l):
                def maxima(i):
                    u, k0 = u0 + i, units[i][2]
                    dve.wait_ge(scores, u + 1)
                    b, c = 2 + 2 * (u % 3), S_MAX + 2 * (u % 4)
                    own.step(nc.vector.tensor_reduce(small[:, c:c + 2], ps[:, b:b + 2, 0:ALLT - k0], AX_X, ALU.max))
                    own.join()
                    TS(small[:, c:c + 2], small[:, c:c + 2], -0.125, None, ALU.mult).then_inc(nmax, 1)

                def weights(i):
                    u, w = u0 + i, ALLT - units[i][2]
                    dve.wait_ge(exps, u + 1)
                    if u:
                        dve.wait_ge(wgt_ready, u)
                    own.step(nc.vector.reciprocal(small[:, S_R:S_R + 2], small[:, S_Z + 2 * (u % 2):S_Z + 2 * (u % 2) + 2]))
                    own.join()
                    own.step(TT(sm(S_R + 1), sm(S_R + 1), sm(S_NLAM + l), ALU.mult))
                    if i >= 2:
                        dve.wait_ge(wgtT_done, u - 1)
                    own.step(TS(wgt[:, u % 2, 0:w], prob[:, u % 2, 0, 0:w], sm(S_R), None, ALU.mult))
                    own.join()
                    STT(wgt[:, u % 2, 0:w], prob[:, u % 2, 1, 0:w], sm(S_R + 1), wgt[:, u % 2, 0:w], ALU.mult, ALU.add)\
                        .then_inc(wgt_ready, 1)

                def o_sums(q):
                    dve.wait_ge(osq_ready, q + 1)
                    c = S_OSS + 4 * (q - q0)
                    nc.vector.tensor_reduce(small[:, c:c + 4], o_sq[:, :].rearrange("p (h d) -> p h d", h=4), AX_X, ALU.add)\
                        .then_inc(oss_ready, 1)

                def normed(q):
                    if q - q0 >= 2:
                        dve.wait_ge(oT_done, q - 1)
                    c = S_ORS + 4 * (q - q0)
                    TT(o_n[:, q % 2, :].rearrange("p (h d) -> p h d", h=4), o_raw[:, q - q0, :].rearrange("p (h d) -> p h d", h=4),
                       bcl(small[:, c:c + 4], P), ALU.mult).then_inc(on_ready, 1)

                def out_lo(q):
                    dve.wait_ge(ohi_ready, q + 1)
                    qt = units[4 * (q - q0)][0]
                    t = slice(qt * P, (qt + 1) * P)
                    STT(h_lo[:, 4:8, t], ps[:, 2 + q - q0, :].rearrange("p (h t) -> p h t", h=4), sm(S_GS + l),
                        h_hi[:, 4:8, t].bitcast(F32), ALU.mult, ALU.subtract).then_inc(olo_ready, 1)

                nq = len(units) // 4
                maxima(0)
                maxima(1)
                pooling(2 - l, 8 * l, l)
                for i in range(len(units)):
                    weights(i)
                    if i + 2 < len(units):
                        maxima(i + 2)
                    if i >= 4 and i % 4 == 1:
                        o_sums(q0 + i // 4 - 1)
                o_sums(q0 + nq - 1)
                dve.wait_ge(ostd_ready, l + 1)
                own.step(nc.vector.reciprocal(small[:, S_ORS:S_ORS + 4 * nq], small[:, S_OSTD:S_OSTD + 4 * nq]))
                own.join()
                normed(q0)
                for q in range(nq):
                    if q + 1 < nq:
                        normed(q0 + q + 1)
                    out_lo(q0 + q)

            def gated(n, tile0, l, part, at=same):
                dve.wait_ge(gemm_done, at(n + 1))
                for m in range(2):
                    for s in range(2 - l):
                        c = slice(s * SEQ, (s + 1) * SEQ)
                        t = tile0 + m
                        last = STT(x[:, t, c], ps[:, tile0 % 4 + m, c], ada[:, l, part + t, s:s + 1], x[:, t, c],
                                   ALU.mult, ALU.add)
                last.then_inc(psum_free, 1)

            def added(n, tile0, at=same):
                dve.wait_ge(gemm_done, at(n + 1))
                t = slice(tile0, tile0 + 2)
                TT(x[:, t, 0:SEQ], ps[:, 2 * (n % 2):2 * (n % 2) + 2, 0:SEQ], x[:, t, 0:SEQ], ALU.add).then_inc(psum_free, 1)

            dve.wait_ge(vec_in_s, 16)
            for l in range(2):
                last = TT(small[:, S_LAMP + 2 * l:S_LAMP + 2 * l + 2], V(f"lam{l}", 0, 2), V(f"lam{l}", 2, 2), ALU.mult)
            last.then_inc(lam_prod, 1)
            dve.wait_ge(silu_done, 2)
            TT(c_st[:, :, 2:4], c_act[:, :, :], c_st[:, :, 0:2].bitcast(F32), ALU.subtract).then_inc(c_ready, 1)
            dve.wait_ge(rows_zero, 1)
            split_lo(0)
            split_lo(1)
            for n in range(8):
                ada_rows(n, n % 4, n // 4, bank=2 * (n % 2))
                split_lo(n + 2)
                if n == 2:
                    dve.wait_ge(lam_exp, 1)
                    for l in range(2):
                        own.step(TT(sm(S_NLAM + l), sm(S_LE + 2 * l + 1), sm(S_LE + 2 * l), ALU.subtract))
                        own.step(TS(sm(S_GS + l), V(f"g_sub{l}"), 1.0 - LAM_INIT[l], None, ALU.mult))
                        own.join()
                        own.step(TS(sm(S_NLAM + l), sm(S_NLAM + l), -LAM_INIT[l], None, ALU.add))
                if n == 3:
                    add_squares(0, 1)
                    add_squares(0, 2)
                if n == 4:
                    ada_columns(0, 0, 1)
                if n == 5:
                    dve.wait_ge(cst_in_s, 16)
                    norm_diagonal(0)
            ada_columns(0, 1, 2)
            dve.wait_ge(ada_ready, 2)
            own.step(ada_mod(0, 0))
            own.join()
            norm_apply(0)

            for l in range(2):
                cos, sin = C("cos"), C("sin")
                for c in range(8):
                    n = N_WIN[l] + 2 * c
                    b = 2 * (c % 2)
                    split_lo(n + 2, parts=(0,))
                    dve.wait_ge(gemm_done, n + 1)
                    if c < 4:
                        dst = (qT, kT)[c // 2]
                        rope(dst, c % 2, b, cos, sin, rope_tmp, ALLT if l == 0 or c >= 2 else SEQ).then_inc(psum_free, 1)
                        rope_add(dst, c % 2, rope_tmp, n)
                    else:
                        dst = (v_tok, u_tok)[c // 2 - 2]
                        nt = 4 if l == 0 or c < 6 else 2
                        CP(dst[:, 0:nt, (c % 2) * CH:(c % 2 + 1) * CH],
                           ps[:, b:b + nt // 2, :].rearrange("p b (t n) -> p (b t) n", t=2)).then_inc(psum_free, 1)
                    split_lo(n + 2, parts=(1,))
                    if c == 4:
                        ada_columns(l, 2 + 2 * l, 3 + 8 * l)
                    ada_rows(n + 1, c % 4)
                    split_lo(n + 3)
                ada_columns(l, 3 + 2 * l, 4 + 8 * l)
                if l == 0:
                    attention([(qt, hd, 0 if qt < 2 else SEQ) for qt in range(4) for hd in range(4)], 0, 0, l)
                else:
                    attention([(qt, hd, 0) for qt in range(2) for hd in range(4)], 16, 4, l)
                each = 3 - 2 * l
                for c in range(4):
                    n = N_WOUT[l] + each * c
                    split_lo(n + 2, parts=(0,))
                    if l == 0:
                        split_lo(n + 2, parts=(1,))
                        split_lo(n + 3, parts=(0,))
                    gated(n, 2 * c, l, 16)
                    if l == 0 or c < 3:
                        split_lo(n + 3 - l, parts=(1,))
                    if l == 0:
                        if c == 2:
                            ada_columns(0, 4, 5)
                        for m in (1, 2):
                            ada_rows(n + m, (2 * c + m - 1) % 4, bank=(7, 5)[m - 1])
                        if c < 3:
                            split_lo(n + 4)
                    if c:
                        add_squares(2 * l + 1, c)
                if l == 0:
                    ada_columns(0, 5, 6)
                dve.wait_ge(ada_ready, 6 + 6 * l)

                def mlp_gain():
                    own.step(ada_mod(l, 1))
                    split_lo(N_MLP[l] + 1, parts=(1,) if l else (0, 1))
                    own.join()

                norm(2 * l + 1, mlp_gain)
                w = ALLT if l == 0 else SEQ
                per = (12, 8)[l]

                def quarter(it, q):
                    def at(n):
                        return n + per * q if it is None else it * per + n

                    for c in range(8):
                        n = N_MLP[l] + (c if l else min(2 * c, c + 4))
                        m = n + 2 if it is not None else n + 2 + per * q
                        split_lo(m, at if it is not None else same, (0,))
                        if c < 4:
                            up = 16 * l + 4 * q + c + 1 if it is None else it * 4 + (16 * l + c + 1)
                            dve.wait_ge(relu_ready, up)
                            if c:
                                g0 = G0[f"mlp{l}"] + 2 * c
                                dve.wait_ge(g_ready, g0 + 8 * q if it is None else it * 8 + g0)
                            TT(relu2[:, :, 0:w], relu[:, c % 2, :, 0:w], relu[:, c % 2, :, 0:w], ALU.mult)\
                                .then_inc(psum_free, 1)
                            dve.wait_ge(psum_free, at(n + 1))
                            dve.wait_ge(ghi_ready, up)
                            TT(g_lo[:, 2 * c:2 * c + 2, 0:w], relu2[:, :, 0:w], g_hi[:, 2 * c:2 * c + 2, 0:w].bitcast(F32),
                               ALU.subtract).then_inc(g_ready, 2)
                        else:
                            gated(n, 2 * (c - 4), l, 40, at)
                        if it is not None or c < 7:
                            split_lo(m, at if it is not None else same, (1,))
                        if c < 4 and l == 0:
                            ada_rows(n + 1, c, 0, at)
                            split_lo(m + 1, at if it is not None else same)
                        if c == 4 and l == 0:
                            if it is None:
                                ada_columns(1, q, 7 + q)
                            else:
                                ada_columns(1, 0, it + 7, it * 8)
                        if it is None and c > 4:
                            add_squares(2 * l + 2, c - 4)

                with dve.Fori(0, 3) as it:
                    quarter(it, 0)
                quarter(None, 3)

                def mixer_gain():
                    if l == 0:
                        dve.wait_ge(ada_ready, 10)
                        own.step(ada_mod(1, 0))
                    split_lo(X_AT[2 * l + 2] + 1, parts=(1,))
                    own.join()

                norm(2 * l + 2, mixer_gain)
            for j in range(1, 3):
                add_squares(5, j)
            norm(5)

            cos, sin = C("cos2"), C("sin2")
            def moba(step, u):
                qt, hh, B, m4 = u // 2, u % 2, 2 + 3 * (u % 2), 4 * (u % 2)
                t = slice(SEQ + qt * P, SEQ + (qt + 1) * P)
                if step == "S":
                    dve.wait_ge(m_scores, u + 1)
                    s4 = ps[:, B:B + 2, :].rearrange("p b (c x) -> p b c x", c=2)
                    for b in range(2):
                        d = s4[:, b, :, qt * P:(qt + 1) * P]
                        own.step(TT(d, d, bc(causal, 2), ALU.add))
                    own.join()
                    own.step(nc.vector.tensor_reduce(small[:, S_MAX + m4:S_MAX + m4 + 4].rearrange("p (b c) -> p b c", c=2),
                                                     s4[:, :, :, 0:(qt + 1) * P], AX_X, ALU.max))
                    own.join()
                    TS(small[:, S_MAX + m4:S_MAX + m4 + 4], small[:, S_MAX + m4:S_MAX + m4 + 4], -0.125, None, ALU.mult)\
                        .then_inc(m_max, 1)
                elif step == "V":
                    dve.wait_ge(m_exp, u + 1)
                    own.step(nc.vector.reciprocal(small[:, S_R + m4:S_R + m4 + 4], small[:, S_Z + m4:S_Z + m4 + 4]))
                    dve.wait_ge(m_pv, u + 1)
                    own.join()
                    TT(a_o[:, u % 2, :].rearrange("p (h d) -> p h d", h=4), ps[:, B + 2, 0:SEQ].rearrange("p (h d) -> p h d", h=4),
                       bcl(small[:, S_R + m4:S_R + m4 + 4], 64), ALU.mult).then_inc(m_o, 1)
                elif step == "O":
                    dve.wait_ge(m_hi, u + 1)
                    TT(h_lo[:, 2 * hh:2 * hh + 2, t], ps[:, B + 2, SEQ:2 * SEQ].rearrange("p (i t) -> p i t", i=2),
                       h_hi[:, 2 * hh:2 * hh + 2, t].bitcast(F32), ALU.subtract).then_inc(m_lo, 1)

            def difference(lv):
                half = 1 << (lv - 1)
                for g in range(2):
                    bb = bcum[:, g, :].rearrange("p (b x) -> p b x", x=2 * half)
                    mid = bb[:, :, half - 1:half].broadcast_to([P, SEQ // (2 * half), 2 * half])
                    last = TT(dec[:, lv % 2, g, :].rearrange("p (b x) -> p b x", x=2 * half), bb, mid, ALU.subtract)
                last.then_inc(l_diff, 1)

            def decayed(lv):
                dve.wait_ge(l_dec, lv)
                if lv >= 3:
                    dve.wait_ge(l_scores, lv - 1)
                TT(gq[:, lv % 2, :, :], bq[:, :, :], dec[:, lv % 2, :, :], ALU.mult)
                TT(gk[:, lv % 2, :, :], bk[:, :, :], dec[:, lv % 2, :, :], ALU.mult).then_inc(l_qk, 1)

            dve.wait_ge(wgk_hi_ready, 1)
            TT(wgk_lo[:, :, :], wgk[:, :, :], wgk_hi[:, :, :].bitcast(F32), ALU.subtract).then_inc(wgk_lo_ready, 1)
            for c in range(12):
                n = N_EV + c
                for step in moba_steps(c, 0):
                    moba(*step)
                split_lo(n + 2, parts=(0,))
                dve.wait_ge(gemm_done, n + 1)
                two = ps[:, 2:4, 0:SEQ] if c == 0 else ps[:, n % 2, :].rearrange("p (m t) -> p m t", m=2)
                if c < 4:
                    dst = (aq, ak)[c // 2]
                    rope(dst, c % 2, None, cos, sin, rot_tmp, SEQ, two).then_inc(psum_free, 1)
                    rope_add(dst, c % 2, rot_tmp, n)
                elif c in (4, 5, 8, 9):
                    dst = av if c < 6 else bv
                    CP(dst[:, :, (c % 2) * CH:(c % 2 + 1) * CH], two).then_inc(psum_free, 1)
                elif c == 6:
                    TS(bq[:, :, :], two, 32 ** -0.5, None, ALU.mult).then_inc(psum_free, 1)
                elif c == 7:
                    CP(bk[:, :, :], two).then_inc(psum_free, 1)
                else:
                    CP(bog[:, 2 * (c - 10):2 * (c - 10) + 2, :], two).then_inc(psum_free, 1)
                for step in moba_steps(c, 1):
                    moba(*step)
                if c == 1:
                    dve.wait_ge(z_done, 1)
                    for g in range(2):
                        last = TS(gl_z[:, g, :], ps[:, 7, g * SEQ:(g + 1) * SEQ], V("b_gk", g), None, ALU.add)
                    last.then_inc(z_ready, 1)
                if c == 3:
                    dve.wait_ge(l_ready, 1)
                    own.step(STT(gl_z[:, :, :], gl_z[:, :, :], 0.0, gl_e[:, :, :], ALU.min, ALU.subtract))
                    own.join()
                    for g in range(2):
                        own.step(nc.vector.tensor_tensor_scan(bcum[:, g, :], gl_z[:, g, :], gl_z[:, g, :], 0.0, ALU.add, ALU.add))
                if c == 9:
                    own.join()
                    difference(1)
                split_lo(n + 2, parts=(1,))
                if c == 10:
                    decayed(1)
            dve.wait_ge(l_qk, 1)
            difference(2)

            dve.wait_ge(glam_in, 16)
            own.step(nc.vector.memset(attn[:, :, :, :, :].rearrange("p a b c t -> p (a b c t)"), 0.0))

            def merge(lv):
                dve.wait_ge(l_scores, lv + 1)
                b0 = 4 * (lv % 2)
                if lv == 8:
                    CP(attnX[:, :, :, :].rearrange("p a g t -> p a (g t)"), ps[:, b0:b0 + 4, 0:2 * P]).then_inc(l_merged, 1)
                    return
                if lv:
                    dve.wait_ge(l_merged, lv)
                nc.vector.copy_predicated(attn[:, :, :, :, :].rearrange("p a b c t -> p (a b c) t"), bc(gmask[:, lv, :], 16),
                                          ps[:, b0:b0 + 4, :].rearrange("p a (b t) -> p (a b) t", t=P)).then_inc(l_merged, 1)

            own.join()
            for lv in range(2, 9):
                decayed(lv)
                if lv < 8:
                    dve.wait_ge(l_qk, lv)
                    difference(lv + 1)
                merge(lv - 2)
            merge(7)
            dve.wait_ge(bog_act, 1)
            for t in range(4):
                own.step(TS(bog[:, t, :], bog[:, t, :], V("g_gla", t), None, ALU.mult))
            merge(8)
            for t in range(2):
                dve.wait_ge(b_sqr, t + 1)
                nc.vector.tensor_reduce(small[:, S_OSS:S_OSS + 8], b_sq[:, :].rearrange("p (h d) -> p h d", h=8), AX_X,
                                        ALU.add).then_inc(b_ssr, 1)
                dve.wait_ge(b_stdr, t + 1)
                own.step(nc.vector.reciprocal(small[:, S_ORS:S_ORS + 8], small[:, S_OSTD:S_OSTD + 8]))
                own.join()
                if t:
                    dve.wait_ge(b_oT, t)
                TT(b_o[:, :].rearrange("p (h d) -> p h d", h=8), ps[:, 4 + t, :].rearrange("p (h d) -> p h d", h=8),
                   bcl(small[:, S_ORS:S_ORS + 8], 64), ALU.mult).then_inc(b_on, 1)
            for t in range(2):
                dve.wait_ge(b_oT, t + 1)
                if t:
                    dve.wait_ge(b_lo, t)
                c = slice(t * P, (t + 1) * P)
                TT(b_raw[:, :, :], ps[:, 6 + t, :].rearrange("p (h t) -> p h t", h=4), bog[:, :, c], ALU.mult)\
                    .then_inc(b_rawr, 1)
                dve.wait_ge(b_hi, t + 1)
                c = slice(SEQ + t * P, SEQ + (t + 1) * P)
                TT(h_lo[:, 4:8, c], b_raw[:, :, :], h_hi[:, 4:8, c].bitcast(F32), ALU.subtract).then_inc(b_lo, 1)
            for c in range(4):
                split_lo(N_EVOUT + c + 2, parts=(0,))
                added(N_EVOUT + c, 2 * c)
                if c < 3:
                    split_lo(N_EVOUT + c + 2, parts=(1,))
                if c:
                    add_squares(6, c)
            norm(6, lambda: split_lo(X_AT[6] + 1, parts=(1,)))

            def ffn(l):
                def body(it, third):
                    def at(n):
                        return n + 12 * third if it is None else it * 12 + n

                    def pairs(j):
                        return 12 * l + 4 * third + j if it is None else it * 4 + (12 * l + j)

                    def convs(j):
                        return 24 * l + 8 * third + j if it is None else it * 8 + (24 * l + j)

                    v0 = VEC[f"ffn{l}"]
                    cw = vec[:, v0 + 64 * third:v0 + 64 * third + 64] if it is None else vec[:, bass.ds(it * 64 + v0, 64)]
                    CP(conv_w[:, :], cw).then_inc(conv_w_ready, 1)
                    for c in range(12):
                        n = N_FFN[l] + c
                        m = n + 2 if it is not None else n + 2 + 12 * third
                        split_lo(m, at if it is not None else same, (0,))
                        if c < 8:
                            p = c % 2
                            dve.wait_ge(conv0, convs(c + 1))
                            for back in (1, 2):
                                for t in range(2):
                                    o = 32 * p + 8 * (2 - back) + 2 * (c // 2) + t
                                    y = conv_y[:, p, t, back:SEQ]
                                    last = STT(y, ps[:, 2 * (n % 2) + t, 0:SEQ - back], conv_w[:, o:o + 1], y, ALU.mult, ALU.add)
                                    if back == 1:
                                        own.step(last)
                                if back == 1:
                                    own.join()
                            last.then_inc(psum_free, 1)
                        else:
                            added(n, 2 * (c - 8), at)
                        if it is not None or c < 11:
                            split_lo(m, at if it is not None else same, (1,))
                        if it is None and c > 8:
                            add_squares(7 + 2 * l, c - 8)
                        if c < 8 and c % 2:
                            dve.wait_ge(gelu_ready, pairs(c // 2 + 1))
                            TT(ffn_p[:, :, :], conv_y[:, 0, :, :], gelu_g[:, :, :], ALU.mult).then_inc(prod_ready, 1)
                            dve.wait_ge(prod_hi, pairs(c // 2 + 1))
                            TT(g_lo[:, c - 1:c + 1, 0:SEQ], ffn_p[:, :, :], g_hi[:, c - 1:c + 1, 0:SEQ].bitcast(F32),
                               ALU.subtract).then_inc(g_ready, 2)
                with dve.Fori(0, 2) as it:
                    own.enter(it, 16)
                    body(it, 0)
                own.leave(2)
                body(None, 2)

            ffn(0)
            norm(7, lambda: split_lo(X_AT[7] + 1, parts=(1,)))

            dve.wait_ge(lam_e, 2)
            e_, s_, q_, p_ = S2[:, 0:8], S2[:, 24:32], S2[:, 32:40], S2[:, 40:48]

            def then(ins):
                own.step(ins)
                own.join()

            then(TS(s_, e_, 2.0, None, ALU.add))
            then(nc.vector.reciprocal(s_, s_))
            then(TT(s_, s_, e_, ALU.mult))
            then(TT(q_, s_, s_, ALU.mult))
            then(TS(p_, q_, 1.0 / 17, 1.0 / 15, ALU.mult, ALU.add))
            for k in (13, 11, 9, 7, 5, 3, 1):
                then(TT(p_, p_, q_, ALU.mult))
                then(TS(p_, p_, 1.0 / k, None, ALU.add))
            then(STT(p_, p_, 2.0, s_, ALU.mult, ALU.mult))
            then(TS(q_, V("lam_od", 0, 8), -1.0, 0.0, ALU.mult, ALU.max))
            then(TT(p_, p_, q_, ALU.add))
            then(TS(S2[:, 8:16], p_, 8.0, None, ALU.mult))
            TS(S2[:, 16:24], p_, -8.0, None, ALU.mult).then_inc(lam_c, 1)

            for c in range(4):
                n = N_OD + c
                b = 2 * (n % 2)
                split_lo(n + 2, parts=(0,))
                dve.wait_ge(xc0, c + 1)
                for back in (1, 2, 3):
                    for m in range(2):
                        t = 2 * c + m
                        y = xr[:, t, back:SEQ]
                        last = STT(y, ps[:, b + m, 0:SEQ - back], V("od_w", 8 * (3 - back) + t), y, ALU.mult, ALU.add)
                        if back < 3:
                            own.step(last)
                    if back < 3:
                        own.join()
                last.then_inc(psum_free, 1)
                split_lo(n + 2, parts=(1,))
                dve.wait_ge(xc_hi, c + 1)
                t = slice(2 * c, 2 * c + 2)
                TT(xr_lo[:, t, :], xr[:, t, :], xr_hi[:, t, :].bitcast(F32), ALU.subtract).then_inc(g_ready, 2)

            def copy_gate(j):
                n = N_GATE[j]
                if j != 2:
                    split_lo(n + 2, parts=(0,))
                dve.wait_ge(gemm_done, n + 1)
                b = 2 * (n % 2)
                CP(gate[:, 2 * j:2 * j + 2, :], ps[:, b:b + 2, 0:SEQ]).then_inc(psum_free, 1)

            def decay(half):
                t = slice(4 * half, 4 * half + 4)
                dve.wait_ge(rg_exp, half + 1)
                own.step(TT(rg_r[:, t, :], rg_a[:, t, :], rg_a[:, t, :], ALU.mult))
                own.join()
                STT(rg_t[:, t, :], rg_r[:, t, :], 1.0, rg_t[:, t, :], ALU.add, ALU.mult).then_inc(rg_s, 1)

            def recurrence_input(half):
                t = slice(4 * half, 4 * half + 4)
                dve.wait_ge(rg_sqrt, half + 1)
                own.step(TT(rg_i[:, t, :], rg_i[:, t, :], rg_t[:, t, :], ALU.mult))

            def recurrence(half):
                own.join()
                for k in range(4 * half, 4 * half + 4):
                    own.step(nc.vector.tensor_tensor_scan(rg_t[:, k, :], rg_a[:, k, :], rg_i[:, k, :], 0.0, ALU.mult, ALU.add))

            def gated_y(i):
                own.join()
                dve.wait_ge(gate_act, i + 1)
                t = RG_TILES[i]
                TT(rg_r[:, t, :], rg_t[:, t, :], gate[:, t, :], ALU.mult).then_inc(rg_y, 1)

            def y_lo(i):
                dve.wait_ge(rg_yhi, i + 1)
                t = RG_TILES[i]
                TT(xr_lo[:, t, :], rg_r[:, t, :], xr_hi[:, t, :].bitcast(F32), ALU.subtract).then_inc(rg_ylo, t.stop - t.start)

            copy_gate(0)
            split_lo(N_GATE[0] + 2, parts=(1,))
            split_lo(N_RG + 2)
            split_lo(N_RG + 3, parts=(0,))
            dve.wait_ge(sig_i, 1)
            TT(rg_i[:, 4:6, :], rg_i[:, 4:6, :], xr[:, 4:6, :], ALU.mult).then_inc(psum_free, 2)
            dve.wait_ge(psum_free, N_RG + 2)
            own.step(TT(rg_i[:, 6:8, :], rg_i[:, 6:8, :], xr[:, 6:8, :], ALU.mult))
            dve.wait_ge(sig_i, 2)
            own.step(TT(rg_i[:, 0:4, :], rg_i[:, 0:4, :], xr[:, 0:4, :], ALU.mult))
            split_lo(N_RG + 3, parts=(1,))
            decay(0)
            copy_gate(1)
            split_lo(N_GATE[1] + 2, parts=(1,))
            decay(1)
            recurrence_input(0)
            recurrence(0)
            copy_gate(2)
            gated_y(0)
            recurrence_input(1)
            split_lo(N_GATE[2] + 2, parts=(0,))
            y_lo(0)
            recurrence(1)
            split_lo(N_GATE[2] + 2, parts=(1,))
            copy_gate(3)
            gated_y(1)
            gated_y(2)
            y_lo(1)
            split_lo(N_GATE[3] + 2, parts=(1,))
            y_lo(2)
            for c in range(4):
                split_lo(N_ODOUT + c + 2, parts=(0,))
                added(N_ODOUT + c, 2 * c)
                if c < 3:
                    split_lo(N_ODOUT + c + 2, parts=(1,))
                if c:
                    add_squares(8, c)
            norm(8, lambda: split_lo(X_AT[8] + 1, parts=(1,)))
            ffn(1)
            norm(9, lambda: split_lo(X_AT[9] + 1, parts=(1,)))


def chunks(w):
    k, c = w.shape
    w = w.reshape(k // D, KT, P, c // CH, CH)
    return w.transpose(3, 0, 2, 1, 4).reshape(-1, P, KT * CH)


def tiles(v):
    return v.reshape(-1, P).T


def constants():
    c = np.zeros((P, C_COLS), np.float32)
    t = np.arange(SEQ)
    inv = (10000.0 ** (-np.arange(0, 32, 2, dtype=np.float32) / np.float32(32))).astype(np.float32)
    ang = np.concatenate([(t // 64).astype(np.float32)[:, None] * inv, (t % 64).astype(np.float32)[:, None] * inv], -1)
    inv2 = (10000.0 ** (-np.arange(32, dtype=np.float32) / np.float32(32))).astype(np.float32)
    ang2 = t.astype(np.float32)[:, None] * inv2
    p = np.arange(P)
    sign = np.where(p // 32 % 2 == 0, 1, -1)[:, None]
    for name, a in (("", ang), ("2", ang2)):
        a = a.astype(np.float64).T[p % 32]
        c[:, CST["cos" + name]:CST["cos" + name] + SEQ] = np.cos(a)
        c[:, CST["sin" + name]:CST["sin" + name] + SEQ] = np.sin(a) * sign
    c[:, CST["ident"]:CST["ident"] + P] = np.eye(P)
    c[:, CST["ones"]:CST["ones"] + P] = 1
    c[:, CST["causal"]:CST["causal"] + P] = np.where(p[None, :] <= p[:, None], 0, -1e30)
    for i in range(4):
        for r in range(4):
            c[32 * i + r, CST["sel"] + 2 * i + r % 2] = 1
    pm = np.zeros((4, SEQ, SEQ))
    for g, w in enumerate((2, 4, 8, 16)):
        for i in range(SEQ):
            lo, hi = max(i - w // 2, 0), min(i + w - w // 2, SEQ)
            pm[g, lo:hi, i] = 1.0 / (hi - lo)
            pm[g, i, i] -= 1.0
    pm = pm.reshape(4, 2, P, SEQ).transpose(2, 1, 0, 3).astype(np.float32)
    gm = np.zeros((P, 8, P), np.int32)
    gm[:, 0] = np.eye(P)
    s_, t_ = p[:, None], p[None, :]
    for lv in range(1, 8):
        h = 1 << (lv - 1)
        gm[:, lv] = (s_ // (2 * h) == t_ // (2 * h)) & (s_ // h % 2 == 0) & (t_ // h % 2 == 1)
    return c, np.ascontiguousarray(pm), gm


def layout(i):
    a = {k: np.asarray(v) for k, v in i.items()}
    two = {k[:-2]: v for k, v in a.items() if k.endswith("_2")}
    def woven(w, ada, each):
        return np.concatenate([w[:, None], ada.reshape(-1, each, P, KT * CH)], 1).reshape(-1, P, KT * CH)

    ada = [chunks(a["w_ada"][l]) for l in range(2)]
    parts = [ada[0][:8]]
    for l in range(2):
        w = a["w_in"][l]
        w = chunks(np.concatenate([w[:, 512:], w[:, :512]], 1))
        parts.append(woven(w, ada[l][(8, 16)[l]:(16, 24)[l]], 1))
        w = chunks(a["w_out"][l])
        parts.append(w if l else woven(w, ada[0][16:], 2))
        up = chunks(a["w_mlp1"][l])
        down = chunks(a["w_mlp2"][l]).reshape(4, 4, P, KT * CH)
        for q in range(4):
            u = up[4 * q:4 * q + 4]
            parts += [u if l else woven(u, ada[1][4 * q:4 * q + 4], 1), down[:, q]]

    def ffn(l):
        up = chunks(two["ffn_w_up"][l])
        down = chunks(two["ffn_w_down"][l]).reshape(4, 3, P, KT * CH)
        for q in range(3):
            for j in range(4):
                parts.append(up[[4 * q + j, 12 + 4 * q + j]])
            parts.append(down[:, q])

    w = two["ev_w_in"][0]
    parts.append(chunks(np.concatenate([w[:, :2560], w[:, 2576:]], 1)))
    parts.append(chunks(two["ev_w_out"][0]))
    ffn(0)
    w = two["od_w_in"][0]
    w = chunks(np.concatenate([w[:, D:], w[:, :D]], 1))
    parts.append(w[:5])
    for k in ("od_w_a", "od_w_x"):
        parts.append(chunks(two[k][0].reshape(D, CH)))
    parts.append(w[5:])
    parts.append(chunks(two["od_w_out"][0]))
    ffn(1)
    stream = np.concatenate(parts, 0)
    assert stream.shape == (N_CHUNKS, P, KT * CH), stream.shape

    def both(u, v):
        return np.stack([tiles(u), tiles(v)], 2).reshape(P, 16)

    def short(v):
        return np.concatenate([v, np.zeros(P - v.shape[0], v.dtype)])[:, None]

    cols = [both(a["c"][0], a["c_ctx"])]
    for l in range(2):
        cols += [tiles(a["g_mix"][l]), tiles(a["g_mlp"][l]), tiles(a["s_pool"][l]), tiles(a["g_subln"][l]),
                 tiles(a["b_ada"][l])] + [short(a[k][l]) for k in ("lam_q1", "lam_q2", "lam_k1", "lam_k2")]
    cols += [tiles(a["g_final"]), tiles(two["mix_norm_g"][0]), tiles(two["mix_norm_g"][1]),
             tiles(two["ffn_norm_g"][0]), tiles(two["ffn_norm_g"][1]), tiles(two["final_norm_g"]),
             tiles(two["ev_b_gk2"][0]), tiles(two["ev_gla_norm_g"][0].reshape(-1)), tiles(two["od_conv_w"][0].reshape(-1)),
             tiles(two["od_conv_b"][0]), tiles(two["od_b_a"][0]), tiles(two["od_b_x"][0]), tiles(two["od_lambda"][0])]
    for l in range(2):
        cw = np.concatenate([two["ffn_conv_w"][l], two["ffn_conv_b"][l][None]], 0)
        cw = cw.reshape(4, 2, 3, 8, P).transpose(4, 2, 1, 0, 3)
        cols.append(cw.reshape(P, 192))
    vec = np.concatenate(cols, 1)
    assert vec.shape == (P, V_COLS), vec.shape
    xs = np.concatenate([a["x"][0], a["ctx"][0]], 0)
    cst, pm, gm = constants()
    return {
        "w_stream": stream, "x_in": xs.reshape(ALLT, KT, P).transpose(2, 1, 0),
        "vec_in": vec, "cst_in": cst, "pool_mats": pm, "gla_masks": gm,
        "w_pool": a["w_pool"].transpose(2, 0, 1, 3),
        "w_gk": two["ev_w_in"][0][:, 2560:2576].reshape(KT, P, 16).transpose(1, 0, 2),
        "w_gk2": two["ev_w_gk2"][0],
    }


def kernel(**inputs):
    import concourse.bacc as bacc
    from concourse.bass_utils import run_bass_kernel_spmd

    nc = bacc.Bacc("TRN2", target_bir_lowering=False, num_devices=1)
    arrays, args = {}, []
    for name, a in layout(inputs).items():
        a = np.ascontiguousarray(a)
        arrays[f"in_{name}"] = a
        args.append(nc.dram_tensor(f"in_{name}", a.shape, mybir.dt.from_np(a.dtype), kind="ExternalInput").ap())
    out = nc.dram_tensor("out", (P, KT, SEQ), F32, kind="ExternalOutput").ap()
    build_program(nc, *args, out)
    r = run_bass_kernel_spmd(nc, [arrays], core_ids=[0])
    y = r.results[0]["out"]
    return np.ascontiguousarray(np.asarray(y).transpose(2, 1, 0).reshape(1, SEQ, D))
```
